# Optimizing a Trainium2 kernel written in Bass

```python
import jax, jax.numpy as jnp
from jax import lax
import numpy as np

D_MODEL = 1024
BATCH = 1
SEQ = 256
DEPTH = 1

GRID_W = 64
CTX_LEN = 256
N_MOD = 6
EPS = 1e-6
MLA_HEADS = 4
MLA_Q_RANK = 256
MLA_KV_RANK = 128
MLA_NOPE = 128
MLA_ROPE = 64
MLA_V = 128
MLA_QK = MLA_NOPE + MLA_ROPE
ROPE_AXIS = MLA_ROPE // 2
ROPE_BASE = 10000.0
Q_BLOCK = 128
ML_HEADS = 4
ML_QK = 64
ML_V = 128
ML_CHUNK = 64
CONV_W = 3
FGATE_BIAS_LO = 3.0
FGATE_BIAS_HI = 6.0
MLA_COLS = MLA_Q_RANK + MLA_KV_RANK + MLA_ROPE
ML_COLS = 2 * ML_HEADS * ML_QK + 2 * ML_HEADS * ML_V + 4 * ML_HEADS
IN_COLS = MLA_COLS + ML_COLS
MIX_WIDTH = MLA_HEADS * MLA_V + ML_HEADS * ML_V
PEER_HEADS = 8
N_KEYS = 128
N_EXPERTS = N_KEYS * N_KEYS
PEER_DK = 256
PEER_DKH = PEER_DK // 2
PEER_TOPK = 16
PEER_BLOCK = 128


def rmsnorm(x, g):
    xf = x.astype(jnp.float32)
    y = xf * lax.rsqrt(jnp.mean(xf * xf, axis=-1, keepdims=True) + EPS)
    return (y * g.astype(jnp.float32)).astype(x.dtype)

def rope_tables(rows):
    row = jnp.repeat(jnp.arange(rows, dtype=jnp.float32), GRID_W)
    col = jnp.tile(jnp.arange(GRID_W, dtype=jnp.float32), rows)
    inv = ROPE_BASE ** (-jnp.arange(ROPE_AXIS // 2, dtype=jnp.float32) * (2.0 / ROPE_AXIS))
    ang_r = row[:, None] * inv
    ang_c = col[:, None] * inv
    return (jnp.cos(ang_r), jnp.sin(ang_r), jnp.cos(ang_c), jnp.sin(ang_c))

def rotate(t, cos, sin):
    half = t.shape[-1] // 2
    t1, t2 = t[..., :half], t[..., half:]
    cos = cos.astype(t.dtype)
    sin = sin.astype(t.dtype)
    return jnp.concatenate([t1 * cos - t2 * sin, t2 * cos + t1 * sin], axis=-1)

def apply_rope2d(t, rope):
    cos_r, sin_r, cos_c, sin_c = rope
    t_row = rotate(t[..., MLA_NOPE:MLA_NOPE + ROPE_AXIS], cos_r, sin_r)
    t_col = rotate(t[..., MLA_NOPE + ROPE_AXIS:], cos_c, sin_c)
    return jnp.concatenate([t[..., :MLA_NOPE], t_row, t_col], axis=-1)

def split_heads(t, n_heads):
    b, n, _ = t.shape
    return t.reshape(b, n, n_heads, -1).transpose(0, 2, 1, 3)

def merge_heads(t):
    b, h, n, d = t.shape
    return t.transpose(0, 2, 1, 3).reshape(b, n, h * d)

def mla_prep(cols, g_cq, w_uq, g_ckv, w_ukv, g_qn, g_kn, rope):
    b, n, _ = cols.shape
    c_q = cols[..., :MLA_Q_RANK]
    c_kv = cols[..., MLA_Q_RANK:MLA_Q_RANK + MLA_KV_RANK]
    k_rope = cols[..., MLA_Q_RANK + MLA_KV_RANK:]
    q = (rmsnorm(c_q, g_cq) @ w_uq).reshape(b, n, MLA_HEADS, MLA_QK)
    kv = (rmsnorm(c_kv, g_ckv) @ w_ukv).reshape(b, n, MLA_HEADS, MLA_NOPE + MLA_V)
    k = jnp.concatenate([kv[..., :MLA_NOPE],
                         jnp.broadcast_to(k_rope[:, :, None, :], (b, n, MLA_HEADS, MLA_ROPE))], axis=-1)
    v = kv[..., MLA_NOPE:].transpose(0, 2, 1, 3)
    q = rmsnorm(q, g_qn).transpose(0, 2, 1, 3)
    k = rmsnorm(k, g_kn).transpose(0, 2, 1, 3)
    if rope is not None:
        q = apply_rope2d(q, rope)
        k = apply_rope2d(k, rope)
    return q, k, v

def attend(q, k, v):
    s = jnp.einsum('bhqd,bhkd->bhqk', q, k).astype(jnp.float32) * (MLA_QK ** -0.5)
    p = jax.nn.softmax(s, axis=-1).astype(v.dtype)
    return jnp.einsum('bhqk,bhkd->bhqd', p, v)

def attend_blocked(q, k, v):
    b, h, n, dk = q.shape
    nb = n // Q_BLOCK
    qb = jnp.moveaxis(q.reshape(b, h, nb, Q_BLOCK, dk), 2, 0)
    ob = lax.map(lambda q_blk: attend(q_blk, k, v), qb)
    return jnp.moveaxis(ob, 0, 2).reshape(b, h, n, -1)

def mla_mixer(cols_lat, cols_ctx, g_cq, w_uq, g_ckv, w_ukv, g_qn, g_kn, rope, need_ctx_out):
    q_l, k_l, v_l = mla_prep(cols_lat, g_cq, w_uq, g_ckv, w_ukv, g_qn, g_kn, rope)
    q_c, k_c, v_c = mla_prep(cols_ctx, g_cq, w_uq, g_ckv, w_ukv, g_qn, g_kn, None)
    k_all = jnp.concatenate([k_c, k_l], axis=2)
    v_all = jnp.concatenate([v_c, v_l], axis=2)
    out_lat = merge_heads(attend_blocked(q_l, k_all, v_all))
    out_ctx = merge_heads(attend(q_c, k_c, v_c)) if need_ctx_out else None
    return out_lat, out_ctx

def centred_conv(u, w):
    k = w.shape[0]
    p = k // 2
    n = u.shape[1]
    up = jnp.pad(u, ((0, 0), (p, p), (0, 0)))
    return sum(up[:, j:j + n] * w[j] for j in range(k))

def mlstm_prep(cols, conv_w, b_i, b_f):
    b, n, _ = cols.shape
    n_qk = ML_HEADS * ML_QK
    n_v = ML_HEADS * ML_V
    qk = jax.nn.silu(centred_conv(cols[..., :2 * n_qk], conv_w))
    q = split_heads(qk[..., :n_qk], ML_HEADS).astype(jnp.float32) * (ML_QK ** -0.5)
    k = split_heads(qk[..., n_qk:], ML_HEADS).astype(jnp.float32)
    v = split_heads(cols[..., 2 * n_qk:2 * n_qk + n_v], ML_HEADS).astype(jnp.float32)
    o = cols[..., 2 * n_qk + n_v:2 * n_qk + 2 * n_v]
    gates = cols[..., 2 * n_qk + 2 * n_v:].astype(jnp.float32).reshape(b, n, 2, 2, ML_HEADS)
    ig = (gates[:, :, 0] + b_i.astype(jnp.float32)).transpose(2, 0, 3, 1)
    lf = jax.nn.log_sigmoid(gates[:, :, 1] + b_f.astype(jnp.float32)).transpose(2, 0, 3, 1)
    return q, k, v, o, ig, lf

def mlstm_scan(q, k, v, ig, lf, state, need_out):
    b, h, n_tok, _ = q.shape
    nc = n_tok // ML_CHUNK

    def chunks(a):
        return jnp.moveaxis(a.reshape(a.shape[:2] + (nc, ML_CHUNK) + a.shape[3:]), 2, 0)

    tri = jnp.tril(jnp.ones((ML_CHUNK, ML_CHUNK), dtype=bool))

    def body(carry, inp):
        c_mat, n_vec, m_prev = carry
        qc, kc, vc, ic, fc = inp
        cum_f = jnp.cumsum(fc, axis=-1)
        dmat = jnp.where(tri, cum_f[..., :, None] - cum_f[..., None, :] + ic[..., None, :], -jnp.inf)
        inter = cum_f + m_prev[..., None]
        m_t = jnp.maximum(inter, jnp.max(dmat, axis=-1))
        m_new = m_t[..., -1]
        w_s = jnp.exp(dmat[..., -1, :] - m_new[..., None])
        decay = jnp.exp(inter[..., -1] - m_new)
        c_new = decay[..., None, None] * c_mat + jnp.einsum('bhs,bhsv,bhsd->bhvd', w_s, vc, kc)
        n_new = decay[..., None] * n_vec + jnp.einsum('bhs,bhsd->bhd', w_s, kc)
        if not need_out:
            return (c_new, n_new, m_new), None
        wmat = jnp.exp(dmat - m_t[..., None]) * jnp.einsum('bhtd,bhsd->bhts', qc, kc)
        scale_inter = jnp.exp(inter - m_t)
        num = jnp.einsum('bhts,bhsv->bhtv', wmat, vc) + scale_inter[..., None] * jnp.einsum('bhvd,bhtd->bhtv', c_mat, qc)
        den = jnp.sum(wmat, axis=-1) + scale_inter * jnp.einsum('bhd,bhtd->bht', n_vec, qc)
        h_out = num / jnp.maximum(jnp.abs(den), jnp.exp(-m_t))[..., None]
        return (c_new, n_new, m_new), h_out

    state, hs = lax.scan(body, state, (chunks(q), chunks(k), chunks(v), chunks(ig), chunks(lf)))
    h_seq = jnp.moveaxis(hs, 0, 2).reshape(b, h, n_tok, -1) if need_out else None
    return state, h_seq

def mlstm_output(h_sum, o, g_out):
    b, h, n, dv = h_sum.shape
    hn = rmsnorm(h_sum.transpose(0, 2, 1, 3), g_out.reshape(h, dv)).reshape(b, n, h * dv)
    return (jax.nn.sigmoid(o.astype(jnp.float32)) * hn).astype(o.dtype)

def mlstm_mixer(cols_lat, cols_ctx, conv_w, b_i, b_f, g_out, need_ctx_out):
    q_l, k_l, v_l, o_l, ig_l, lf_l = mlstm_prep(cols_lat, conv_w, b_i, b_f)
    q_c, k_c, v_c, o_c, ig_c, lf_c = mlstm_prep(cols_ctx, conv_w, b_i, b_f)
    b = q_l.shape[0]
    outs_lat, outs_ctx = [], []
    for d in range(2):
        rev = d == 1

        def fl(a):
            return jnp.flip(a, axis=2) if rev else a

        state0 = (jnp.zeros((b, ML_HEADS, ML_V, ML_QK), jnp.float32),
                  jnp.zeros((b, ML_HEADS, ML_QK), jnp.float32),
                  jnp.zeros((b, ML_HEADS), jnp.float32))
        st_ctx, h_c = mlstm_scan(fl(q_c), fl(k_c), fl(v_c), fl(ig_c[d]), fl(lf_c[d]), state0, need_ctx_out)
        _, h_l = mlstm_scan(fl(q_l), fl(k_l), fl(v_l), fl(ig_l[d]), fl(lf_l[d]), st_ctx, True)
        outs_lat.append(fl(h_l))
        if need_ctx_out:
            outs_ctx.append(fl(h_c))
    out_lat = mlstm_output(outs_lat[0] + outs_lat[1], o_l, g_out)
    out_ctx = mlstm_output(outs_ctx[0] + outs_ctx[1], o_c, g_out) if need_ctx_out else None
    return out_lat, out_ctx

def peer(h, w_pq, sub_keys, expert_u, expert_v):
    b, n, d = h.shape
    xb_all = h.reshape(-1, PEER_BLOCK, d)

    def one(xb):
        q = (xb @ w_pq).reshape(PEER_BLOCK, PEER_HEADS, 2, PEER_DKH)
        s = jnp.einsum('thpd,hpkd->thpk', q, sub_keys).astype(jnp.float32)
        sv, si = lax.top_k(s, PEER_TOPK)
        cand = (sv[:, :, 0, :, None] + sv[:, :, 1, None, :]).reshape(PEER_BLOCK, PEER_HEADS, -1)
        cidx = (si[:, :, 0, :, None] * N_KEYS + si[:, :, 1, None, :]).reshape(PEER_BLOCK, PEER_HEADS, -1)
        best, pos = lax.top_k(cand, PEER_TOPK)
        eidx = jnp.take_along_axis(cidx, pos, axis=-1)
        g = jax.nn.softmax(best, axis=-1)
        act = jax.nn.gelu(jnp.einsum('thkd,td->thk', expert_u[eidx], xb).astype(jnp.float32), approximate=False)
        return jnp.einsum('thk,thkd->td', (g * act).astype(xb.dtype), expert_v[eidx])

    return lax.map(one, xb_all).reshape(b, n, d)

def first_inputs(seed: int = 0) -> dict:
    key = jax.random.key(seed)
    ks = jax.random.split(key, 24)

    def nrm(k, shape, s):
        return jax.random.normal(k, shape, jnp.float32) * s

    def gain(k, shape):
        return 1.0 + nrm(k, shape, 0.01)

    D, L = D_MODEL, DEPTH
    fgate = jnp.linspace(FGATE_BIAS_LO, FGATE_BIAS_HI, ML_HEADS, dtype=jnp.float32)
    return {
        'x': nrm(ks[0], (BATCH, SEQ, D), 1.0),
        'c': nrm(ks[1], (BATCH, D), 1.0),
        'ctx': nrm(ks[2], (BATCH, CTX_LEN, D), 1.0),
        'c_ctx': nrm(ks[3], (D,), 1.0),
        'w_ada': nrm(ks[4], (L, D, N_MOD * D), 0.5 * D ** -0.5),
        'b_ada': nrm(ks[5], (L, N_MOD * D), 0.01),
        'g_norm1': gain(ks[6], (L, D)),
        'w_in': nrm(ks[7], (L, D, IN_COLS), D ** -0.5),
        'g_cq': gain(ks[8], (L, MLA_Q_RANK)),
        'w_uq': nrm(ks[9], (L, MLA_Q_RANK, MLA_HEADS * MLA_QK), MLA_Q_RANK ** -0.5),
        'g_ckv': gain(ks[10], (L, MLA_KV_RANK)),
        'w_ukv': nrm(ks[11], (L, MLA_KV_RANK, MLA_HEADS * (MLA_NOPE + MLA_V)), MLA_KV_RANK ** -0.5),
        'g_qn': gain(ks[12], (L, MLA_QK)),
        'g_kn': gain(ks[13], (L, MLA_QK)),
        'conv_qk': nrm(ks[14], (L, CONV_W, 2 * ML_HEADS * ML_QK), CONV_W ** -0.5),
        'b_igate': nrm(ks[15], (L, 2, ML_HEADS), 0.01),
        'b_fgate': fgate[None, None, :] + nrm(ks[16], (L, 2, ML_HEADS), 0.01),
        'g_mlstm': gain(ks[17], (L, ML_HEADS * ML_V)),
        'w_out': nrm(ks[18], (L, MIX_WIDTH, D), MIX_WIDTH ** -0.5),
        'g_norm2': gain(ks[19], (L, D)),
        'w_pq': nrm(ks[20], (L, D, PEER_HEADS * PEER_DK), D ** -0.5),
        'sub_keys': nrm(ks[21], (L, PEER_HEADS, 2, N_KEYS, PEER_DKH), PEER_DKH ** -0.5),
        'expert_u': nrm(ks[22], (L, N_EXPERTS, D), D ** -0.5),
        'expert_v': nrm(ks[23], (L, N_EXPERTS, D), PEER_HEADS ** -0.5),
    }

def first_block(x, c, ctx, c_ctx, w_ada, b_ada, g_norm1, w_in, g_cq, w_uq, g_ckv, w_ukv, g_qn, g_kn,
              conv_qk, b_igate, b_fgate, g_mlstm, w_out, g_norm2, w_pq, sub_keys, expert_u, expert_v):
    n_lat = x.shape[1]
    ROWS = n_lat // GRID_W
    rope = rope_tables(ROWS)
    s_c = jax.nn.silu(c)
    s_cc = jax.nn.silu(c_ctx)
    for l in range(DEPTH):
        last = l == DEPTH - 1
        mod_lat = (s_c @ w_ada[l] + b_ada[l])[:, None, :]
        mod_ctx = s_cc @ w_ada[l] + b_ada[l]
        sh1, sc1, gt1, sh2, sc2, gt2 = jnp.split(mod_lat, N_MOD, axis=-1)
        csh1, csc1, cgt1, csh2, csc2, cgt2 = jnp.split(mod_ctx, N_MOD, axis=-1)
        h_lat = rmsnorm(x, g_norm1[l]) * (1.0 + sc1) + sh1
        h_ctx = rmsnorm(ctx, g_norm1[l]) * (1.0 + csc1) + csh1
        cols_lat = h_lat @ w_in[l]
        cols_ctx = h_ctx @ w_in[l]
        mla_lat, mla_ctx = mla_mixer(cols_lat[..., :MLA_COLS], cols_ctx[..., :MLA_COLS],
                                     g_cq[l], w_uq[l], g_ckv[l], w_ukv[l], g_qn[l], g_kn[l], rope, not last)
        ml_lat, ml_ctx = mlstm_mixer(cols_lat[..., MLA_COLS:], cols_ctx[..., MLA_COLS:],
                                     conv_qk[l], b_igate[l], b_fgate[l], g_mlstm[l], not last)
        x = x + gt1 * (jnp.concatenate([mla_lat, ml_lat], axis=-1) @ w_out[l])
        h2 = rmsnorm(x, g_norm2[l]) * (1.0 + sc2) + sh2
        x = x + gt2 * peer(h2, w_pq[l], sub_keys[l], expert_u[l], expert_v[l])
        if not last:
            ctx = ctx + cgt1 * (jnp.concatenate([mla_ctx, ml_ctx], axis=-1) @ w_out[l])
            hc2 = rmsnorm(ctx, g_norm2[l]) * (1.0 + csc2) + csh2
            ctx = ctx + cgt2 * peer(hc2, w_pq[l], sub_keys[l], expert_u[l], expert_v[l])
    return x


DEPTH_2 = 2

HEAD_DIM = 64
N_ATTN_HEADS = 8
ATTN_WIDTH = N_ATTN_HEADS * HEAD_DIM
DILATED_PATTERNS = ((128, 1), (512, 4), (2048, 16))
ROPE_THETA = 10000.0
NEG_INF = -1e30

N_DELTA_HEADS = 4
DELTA_DK = 128
DELTA_DV = 128
DELTA_K_WIDTH = N_DELTA_HEADS * DELTA_DK
DELTA_V_WIDTH = N_DELTA_HEADS * DELTA_DV
DELTA_CONV = 4
DELTA_CHUNK = 64

MIX_WIDTH_2 = ATTN_WIDTH + DELTA_V_WIDTH
IN_COLS_2 = 3 * ATTN_WIDTH + 2 * DELTA_K_WIDTH + 2 * DELTA_V_WIDTH + 2 * N_DELTA_HEADS

D_FF = 2816
FFN_CONV = 3


def rms_norm(x, w):
    xf = x.astype(jnp.float32)
    y = xf * lax.rsqrt(jnp.mean(xf * xf, axis=-1, keepdims=True) + EPS)
    return (y * w.astype(jnp.float32)).astype(x.dtype)

def rope_tables_2(seq, dim):
    inv = 1.0 / (ROPE_THETA ** (jnp.arange(0, dim, 2, dtype=jnp.float32) / dim))
    ang = jnp.arange(seq, dtype=jnp.float32)[:, None] * inv[None, :]
    return jnp.cos(ang), jnp.sin(ang)

def apply_rope(x, cos, sin):
    x1, x2 = jnp.split(x, 2, axis=-1)
    c = cos[None, :, None, :]
    s = sin[None, :, None, :]
    return jnp.concatenate([x1 * c - x2 * s, x1 * s + x2 * c], axis=-1)

def causal_dwconv(x, w):
    K, C = w.shape
    return lax.conv_general_dilated(
        x, w[:, None, :].astype(x.dtype), window_strides=(1,), padding=[(K - 1, 0)],
        dimension_numbers=('NWC', 'WIO', 'NWC'), feature_group_count=C)

def dilated_branch(q, k, v, window, dilation):
    B, S, H, D = q.shape
    n = window // dilation
    L = S // dilation
    nb = -(-L // n)
    Lp = nb * n

    def split(t):
        return t.reshape(B, L, dilation, H, D).transpose(0, 2, 3, 1, 4)

    qs = jnp.pad(split(q), ((0, 0), (0, 0), (0, 0), (0, Lp - L), (0, 0)))
    qs = qs.reshape(B, dilation, H, nb, n, D)

    def kv_blocks(t):
        tp = jnp.pad(split(t), ((0, 0), (0, 0), (0, 0), (n, Lp - L), (0, 0)))
        prev = tp[:, :, :, :Lp].reshape(B, dilation, H, nb, n, D)
        cur = tp[:, :, :, n:].reshape(B, dilation, H, nb, n, D)
        return jnp.concatenate([prev, cur], axis=4)

    kb = kv_blocks(k)
    vb = kv_blocks(v)
    s = jnp.einsum('brhnqd,brhnkd->brhnqk', qs, kb) * (D ** -0.5)
    a = jnp.arange(n)[:, None]
    c = jnp.arange(2 * n)[None, :]
    key_pos = (jnp.arange(nb)[:, None, None] - 1) * n + c[None]
    valid = ((c >= a) & (c <= a + n))[None] & (key_pos >= 0)
    s = jnp.where(valid, s, NEG_INF)
    m = jnp.max(s, axis=-1, keepdims=True)
    e = jnp.exp(s - m)
    l = jnp.sum(e, axis=-1, keepdims=True)
    o = jnp.einsum('brhnqk,brhnkd->brhnqd', e, vb) / l
    lse = (m + jnp.log(l))[..., 0]

    o = o.reshape(B, dilation, H, Lp, D)[:, :, :, :L]
    o = o.transpose(0, 3, 1, 2, 4).reshape(B, S, H, D)
    lse = lse.reshape(B, dilation, H, Lp)[:, :, :, :L]
    lse = lse.transpose(0, 3, 1, 2).reshape(B, S, H)
    return o, lse

def dilated_attention(q, k, v):
    outs, lses = [], []
    for window, dilation in DILATED_PATTERNS:
        o, lse = dilated_branch(q, k, v, window, dilation)
        outs.append(o)
        lses.append(lse)
    wts = jax.nn.softmax(jnp.stack(lses, axis=0), axis=0)
    return jnp.sum(wts[..., None] * jnp.stack(outs, axis=0), axis=0)

def gated_delta_rule(q, k, v, beta, g):
    B, S, H, K = q.shape
    V = v.shape[-1]
    C = DELTA_CHUNK
    N = S // C
    q = q * lax.rsqrt(jnp.sum(q * q, axis=-1, keepdims=True) + EPS) * (K ** -0.5)
    k = k * lax.rsqrt(jnp.sum(k * k, axis=-1, keepdims=True) + EPS)

    def chunk(t):
        return jnp.moveaxis(t.reshape((B, N, C, H) + t.shape[3:]), 3, 1)

    q, k, v, beta, g = chunk(q), chunk(k), chunk(v), chunk(beta), chunk(g)
    g = jnp.cumsum(g, axis=-1)
    tril = jnp.tril(jnp.ones((C, C), dtype=bool))
    strict = jnp.tril(jnp.ones((C, C), dtype=bool), -1)
    decay = jnp.exp(jnp.where(tril, g[..., :, None] - g[..., None, :], -jnp.inf))
    kb = k * beta[..., None]
    A = jnp.where(strict, jnp.einsum('bhnik,bhnjk->bhnij', kb, k) * decay, 0.0)
    eye = jnp.eye(C, dtype=A.dtype)
    T = lax.linalg.triangular_solve(A + eye, jnp.broadcast_to(eye, A.shape), left_side=True,
                                    lower=True, unit_diagonal=True)
    u = jnp.einsum('bhnij,bhnjv->bhniv', T, v * beta[..., None])
    w = jnp.einsum('bhnij,bhnjk->bhnik', T, kb * jnp.exp(g)[..., None])
    qk = jnp.einsum('bhnik,bhnjk->bhnij', q, k) * decay
    q_dec = q * jnp.exp(g)[..., None]
    k_dec = k * jnp.exp(g[..., -1:] - g)[..., None]
    g_last = jnp.exp(g[..., -1])

    def step(state, xs):
        q_i, k_i, u_i, w_i, qk_i, gl = xs
        v_new = u_i - jnp.einsum('bhck,bhkv->bhcv', w_i, state)
        o = jnp.einsum('bhck,bhkv->bhcv', q_i, state) + jnp.einsum('bhij,bhjv->bhiv', qk_i, v_new)
        state = state * gl[..., None, None] + jnp.einsum('bhck,bhcv->bhkv', k_i, v_new)
        return state, o

    xs = (jnp.moveaxis(q_dec, 2, 0), jnp.moveaxis(k_dec, 2, 0), jnp.moveaxis(u, 2, 0),
          jnp.moveaxis(w, 2, 0), jnp.moveaxis(qk, 2, 0), jnp.moveaxis(g_last, 2, 0))
    _, o = lax.scan(step, jnp.zeros((B, H, K, V), jnp.float32), xs)
    return jnp.transpose(o, (1, 0, 3, 2, 4)).reshape(B, S, H, V)

def hybrid_mixer(h, w_in, dn_conv_w, dn_a_log, dn_dt_bias, dn_norm_w, w_out, cos, sin):
    B, S, _ = h.shape
    proj = h @ w_in
    cuts = [ATTN_WIDTH, 2 * ATTN_WIDTH, 3 * ATTN_WIDTH,
            3 * ATTN_WIDTH + 2 * DELTA_K_WIDTH + DELTA_V_WIDTH,
            3 * ATTN_WIDTH + 2 * DELTA_K_WIDTH + 2 * DELTA_V_WIDTH,
            3 * ATTN_WIDTH + 2 * DELTA_K_WIDTH + 2 * DELTA_V_WIDTH + N_DELTA_HEADS]
    aq, ak, av, dn_qkv, dn_z, dn_b, dn_a = jnp.split(proj, cuts, axis=-1)

    aq = apply_rope(aq.reshape(B, S, N_ATTN_HEADS, HEAD_DIM).astype(jnp.float32), cos, sin)
    ak = apply_rope(ak.reshape(B, S, N_ATTN_HEADS, HEAD_DIM).astype(jnp.float32), cos, sin)
    av = av.reshape(B, S, N_ATTN_HEADS, HEAD_DIM).astype(jnp.float32)
    attn_out = dilated_attention(aq, ak, av).reshape(B, S, ATTN_WIDTH).astype(h.dtype)

    qkv = jax.nn.silu(causal_dwconv(dn_qkv, dn_conv_w)).astype(jnp.float32)
    dq, dk, dv = jnp.split(qkv, [DELTA_K_WIDTH, 2 * DELTA_K_WIDTH], axis=-1)
    beta = jax.nn.sigmoid(dn_b.astype(jnp.float32))
    g = -jnp.exp(dn_a_log.astype(jnp.float32)) * jax.nn.softplus(
        dn_a.astype(jnp.float32) + dn_dt_bias.astype(jnp.float32))
    o = gated_delta_rule(dq.reshape(B, S, N_DELTA_HEADS, DELTA_DK),
                         dk.reshape(B, S, N_DELTA_HEADS, DELTA_DK),
                         dv.reshape(B, S, N_DELTA_HEADS, DELTA_DV), beta, g)
    z = dn_z.reshape(B, S, N_DELTA_HEADS, DELTA_DV).astype(jnp.float32)
    dn_out = (rms_norm(o, dn_norm_w) * jax.nn.silu(z)).reshape(B, S, DELTA_V_WIDTH).astype(h.dtype)

    return jnp.concatenate([attn_out, dn_out], axis=-1) @ w_out

def conv_glu_ffn(h, ffn_w_in, ffn_conv_w, ffn_conv_b, ffn_w_out):
    u = causal_dwconv(h @ ffn_w_in, ffn_conv_w) + ffn_conv_b
    gate, up = jnp.split(u, 2, axis=-1)
    return (jax.nn.gelu(gate, approximate=True) * up) @ ffn_w_out

def second_inputs(seed: int = 0) -> dict:
    key = jax.random.key(seed)
    ks = jax.random.split(key, 16)
    f32 = jnp.float32
    nrm = lambda k, shape, scale: jax.random.normal(k, shape, f32) * scale
    dt = jnp.exp(jax.random.uniform(ks[4], (DEPTH_2, N_DELTA_HEADS), f32) *
                 (jnp.log(0.1) - jnp.log(0.001)) + jnp.log(0.001))
    return {
        'x': nrm(ks[0], (BATCH, SEQ, D_MODEL), 1.0),
        'w_in': nrm(ks[1], (DEPTH_2, D_MODEL, IN_COLS_2), D_MODEL ** -0.5),
        'dn_conv_w': nrm(ks[2], (DEPTH_2, DELTA_CONV, 2 * DELTA_K_WIDTH + DELTA_V_WIDTH), DELTA_CONV ** -0.5),
        'dn_a_log': jnp.log(jax.random.uniform(ks[3], (DEPTH_2, N_DELTA_HEADS), f32, 1.0, 16.0)),
        'dn_dt_bias': dt + jnp.log(-jnp.expm1(-dt)),
        'dn_norm_w': 1.0 + nrm(ks[5], (DEPTH_2, DELTA_DV), 0.05),
        'w_out': nrm(ks[6], (DEPTH_2, MIX_WIDTH_2, D_MODEL), MIX_WIDTH_2 ** -0.5),
        'ffn_w_in': nrm(ks[7], (DEPTH_2, D_MODEL, 2 * D_FF), D_MODEL ** -0.5),
        'ffn_conv_w': nrm(ks[8], (DEPTH_2, FFN_CONV, 2 * D_FF), FFN_CONV ** -0.5),
        'ffn_conv_b': nrm(ks[9], (DEPTH_2, 2 * D_FF), 0.01),
        'ffn_w_out': nrm(ks[10], (DEPTH_2, D_FF, D_MODEL), D_FF ** -0.5),
        'norm_pre_mix': 1.0 + nrm(ks[11], (DEPTH_2, D_MODEL), 0.05),
        'norm_post_mix': 1.0 + nrm(ks[12], (DEPTH_2, D_MODEL), 0.05),
        'norm_pre_ffn': 1.0 + nrm(ks[13], (DEPTH_2, D_MODEL), 0.05),
        'norm_post_ffn': 1.0 + nrm(ks[14], (DEPTH_2, D_MODEL), 0.05),
    }

def second_block(x, w_in, dn_conv_w, dn_a_log, dn_dt_bias, dn_norm_w, w_out, ffn_w_in, ffn_conv_w,
              ffn_conv_b, ffn_w_out, norm_pre_mix, norm_post_mix, norm_pre_ffn, norm_post_ffn):
    cos, sin = rope_tables_2(x.shape[1], HEAD_DIM)
    for l in range(DEPTH_2):
        h = rms_norm(x, norm_pre_mix[l])
        mix = hybrid_mixer(h, w_in[l], dn_conv_w[l], dn_a_log[l], dn_dt_bias[l], dn_norm_w[l],
                           w_out[l], cos, sin)
        x = x + rms_norm(mix, norm_post_mix[l]).astype(x.dtype)
        h = rms_norm(x, norm_pre_ffn[l])
        f = conv_glu_ffn(h, ffn_w_in[l], ffn_conv_w[l], ffn_conv_b[l], ffn_w_out[l])
        x = x + rms_norm(f, norm_post_ffn[l]).astype(x.dtype)
    return x


def setup_inputs(seed=0):
    out = dict(first_inputs(seed))
    for name, value in second_inputs(seed + 1).items():
        if name != "x":
            out[name + "_2"] = value
    return out


def reference(
    x, c, ctx, c_ctx, w_ada, b_ada, g_norm1, w_in, g_cq, w_uq, g_ckv, w_ukv, g_qn, g_kn,
    conv_qk, b_igate, b_fgate, g_mlstm, w_out, g_norm2, w_pq, sub_keys, expert_u, expert_v,
    w_in_2, dn_conv_w_2, dn_a_log_2, dn_dt_bias_2, dn_norm_w_2, w_out_2, ffn_w_in_2,
    ffn_conv_w_2, ffn_conv_b_2, ffn_w_out_2, norm_pre_mix_2, norm_post_mix_2, norm_pre_ffn_2,
    norm_post_ffn_2,
):
    x = first_block(
        x, c, ctx, c_ctx, w_ada, b_ada, g_norm1, w_in, g_cq, w_uq, g_ckv, w_ukv, g_qn, g_kn,
        conv_qk, b_igate, b_fgate, g_mlstm, w_out, g_norm2, w_pq, sub_keys, expert_u, expert_v,
    )
    return second_block(
        x, w_in_2, dn_conv_w_2, dn_a_log_2, dn_dt_bias_2, dn_norm_w_2, w_out_2, ffn_w_in_2,
        ffn_conv_w_2, ffn_conv_b_2, ffn_w_out_2, norm_pre_mix_2, norm_post_mix_2,
        norm_pre_ffn_2, norm_post_ffn_2,
    )


_drawn_inputs = setup_inputs


def setup_inputs(seed=0):
    import zlib

    import numpy as np

    out = dict(_drawn_inputs(seed))
    spreads = {}
    factors = {'g_norm1': 8.0,
     'g_cq': 8.0,
     'g_ckv': 8.0,
     'g_qn': 8.0,
     'g_kn': 8.0,
     'b_igate': 64.0,
     'g_mlstm': 51.064,
     'g_norm2': 22.992,
     'ffn_conv_b_2': 26.751,
     'dn_norm_w_2': 8.0,
     'norm_pre_mix_2': 4.618,
     'norm_post_mix_2': 7.254,
     'norm_pre_ffn_2': 5.313,
     'norm_post_ffn_2': 7.549}
    for name, (base, spread) in spreads.items():
        noise = np.random.default_rng([zlib.crc32(name.encode()), seed]).standard_normal(out[name].shape)
        drawn = base * np.exp(spread * noise) if base else spread * noise
        out[name] = __import__('jax').numpy.asarray(drawn.astype(out[name].dtype))
    for name, factor in factors.items():
        out[name] = (out[name] * factor).astype(out[name].dtype)
    return out
```

```python
from contextlib import ExitStack

import numpy as np

import concourse.bass as bass
from concourse import mybir

F32 = mybir.dt.float32
U32 = mybir.dt.uint32
ALU = mybir.AluOpType
ACT = mybir.ActivationFunctionType
AX = mybir.AxisListType

P = 128
D = 1024
KT = D // P
SEQ, CTX = 256, 256
ALL = SEQ + CTX
EPS = 1e-6
NEG = -1e30

QR, KVR, ROPE, NOPE, VD, HEADS = 256, 128, 64, 128, 128, 4
QK = NOPE + ROPE
MLQK = 64
MLA_COLS = QR + KVR + ROPE
PH, NKEYS, TOPK = 8, 128, 16
PICKS = PH * TOPK
DEPTH = 2
AH, AD = 8, 64
DH = 4
DFF = 2816
FBLK = DFF // 256

WSLOTS = 4
WCOLS = 520
SLOT = KT * WCOLS

IDENT = 0
TRI = IDENT + P
ONES = TRI + 4 * P
LEVEL = ONES + 2 * P
DECM = LEVEL + 7 * P
DILM = DECM + P
ROPE1 = DILM + 3 * P
ROPE2 = ROPE1 + 4 * ROPE
IOTA = ROPE2 + 4 * AD
NCONST = IOTA + TOPK
BASE = NCONST


def constants():
    f = np.float32
    r = np.arange(P)
    out = np.zeros((P, NCONST), f)
    out[:, IDENT:IDENT + P] = np.eye(P)
    le = (r[:, None] <= r[None, :]).astype(f)
    tri = [le, -(1 - le), (r[:, None] >= r[None, :]).astype(f), -(r[:, None] < r[None, :]).astype(f)]
    for n, m in enumerate(tri):
        out[:, TRI + n * P:TRI + (n + 1) * P] = m
    out[:, ONES:ONES + P] = 1.0
    out[:, ONES + P:ONES + 2 * P] = -1.0
    for n in range(7):
        b = 1 << n
        m = (r[None, :] // (2 * b) == r[:, None] // (2 * b)) & (r[None, :] // b % 2 == 1) & (r[:, None] // b % 2 == 0)
        out[:, LEVEL + n * P:LEVEL + (n + 1) * P] = m
    out[:, DECM:DECM + P] = np.where(r[None, :] > r[:, None], f(1e30), f(0))
    t = np.arange(SEQ)
    diff = t[:, None] - t[None, :]
    count = np.zeros((SEQ, SEQ))
    for window, dil in ((128, 1), (512, 4), (2048, 16)):
        count += (diff >= 0) & (diff <= window) & (diff % dil == 0)
    m = np.where(count > 0, 8.0 * np.log(np.maximum(count, 1)), NEG).astype(f)
    out[:, DILM:DILM + P] = m[:P, :P]
    out[:, DILM + P:DILM + 3 * P] = m[P:, :]
    half = ROPE // 4
    inv = (f(10000.0) ** (-np.arange(half, dtype=f) * f(2.0 / (ROPE // 2)))).astype(f)
    row, col = (t // 64).astype(f), (t % 64).astype(f)
    ar, ac = row[:, None] * inv, col[:, None] * inv
    cos = np.concatenate([np.cos(ar), np.cos(ar), np.cos(ac), np.cos(ac)], 1)
    sin = np.concatenate([-np.sin(ar), np.sin(ar), -np.sin(ac), np.sin(ac)], 1)
    inv2 = (f(1.0) / (f(10000.0) ** (np.arange(0, AD, 2, dtype=f) / f(AD)))).astype(f)
    a2 = t.astype(f)[:, None] * inv2[None, :]
    cos2 = np.concatenate([np.cos(a2), np.cos(a2)], 1)
    sin2 = np.concatenate([-np.sin(a2), np.sin(a2)], 1)
    for at, table in ((ROPE1, cos), (ROPE1 + 2 * ROPE, sin), (ROPE2, cos2), (ROPE2 + 2 * AD, sin2)):
        out[:, at:at + 2 * ROPE] = table.reshape(2, P, ROPE).transpose(1, 0, 2).reshape(P, 2 * ROPE)
    out[:, IOTA:IOTA + TOPK] = np.arange(TOPK)
    return out


def mlstm_masks():
    t = np.arange(SEQ)
    out = np.zeros((P, 2, 2, ALL), np.float32)
    for i in range(2):
        q = t[i * P:(i + 1) * P]
        out[:, i, 0, CTX:] = np.where(t[None, :] > q[:, None], NEG, 0)
        out[:, i, 1, CTX:] = np.where(t[None, :] < q[:, None], NEG, 0)
    return out.reshape(P, 4 * ALL)


def program(nc, a, out):
    with ExitStack() as ctx:
        sems = {}

        def sem(name):
            if name not in sems:
                sems[name] = ctx.enter_context(nc.semaphore(name))
            return sems[name]

        X = ctx.enter_context(nc.sbuf_tensor("residual", [P, 2, D], F32))
        XT = ctx.enter_context(nc.sbuf_tensor("activations_T", [P, KT * ALL], F32))
        RING = ctx.enter_context(nc.sbuf_tensor("weight_ring", [P, WSLOTS, SLOT], F32))
        SMALL = ctx.enter_context(nc.sbuf_tensor("small", [P, 1280], F32))
        IDX = ctx.enter_context(nc.sbuf_tensor("indices", [P, 3, 256], U32))
        AR_N = (nc.sbuf_bytes_remaining - 512) // 4
        AR = ctx.enter_context(nc.sbuf_tensor("arena", [P, AR_N], F32))
        PS = ctx.enter_context(nc.psum_tensor("psum", [P, 8, 512], F32))

        def v(at, *dims, of=AR, parts=P):
            n = int(np.prod(dims))
            assert at + n <= of.shape[-1], (at, dims)
            ap = of[0:parts, at:at + n]
            names = "abcd"[:len(dims)]
            if len(dims) == 1:
                return ap
            return ap.rearrange(f"p ({' '.join(names)}) -> p {' '.join(names)}", **dict(zip(names[1:], dims[1:])))

        small_at = [0]

        def small(*dims):
            n = int(np.prod(dims))
            small_at[0] += n
            assert small_at[0] <= 1280
            return v(small_at[0] - n, *dims, of=SMALL)

        ident = v(IDENT, P)
        tri = v(TRI, 4, P)
        ones = v(ONES, 2, P)
        level = v(LEVEL, 7, P)
        rope1 = v(ROPE1, 2, 2, ROPE)
        rope2 = v(ROPE2, 2, 2, AD)
        iota = v(IOTA, TOPK)

        MODA = v(BASE, 4, D)
        MODB = v(BASE + 4096, 4, D)
        R3, R4 = BASE + 8192, BASE + 10240
        R5 = BASE + 12288
        R6 = R5 + 4416
        R7 = R6 + 3072
        R8 = R7 + 2048
        R9 = R8 + 1536
        XC = v(R3, 2, D)
        GN = v(R4, 2, D)
        HN = v(R7, 2, D)
        XTv = XT[:, :].rearrange("p (k t) -> p k t", k=KT)
        CQKV = v(R5, 4, MLA_COLS)
        OML = v(R5 + 1792, 2, 512)
        GATE = v(R5 + 2816, 4, 16)
        CN = v(R5 + 2880, 1024)
        GOUT = v(R5 + 3904, 512)
        VML = v(R9, 4, 512)
        QF = v(R8, 2, SEQ)
        KF = v(R8 + 512, 2, ALL)
        CNT = v(R7, 1024)
        QM = v(0, 2, HEADS, QK, of=XT)
        KM = v(R6, 4, HEADS, QK)
        VM = v(R3, 4, HEADS, VD)
        QTN = v(1536, HEADS, SEQ, of=XT)
        QTR = v(2560, HEADS, SEQ, of=XT, parts=ROPE)
        KTN = v(BASE, HEADS, ALL)
        KTR = v(BASE + 2048, HEADS, ALL, parts=ROPE)
        MIXT = v(R4, KT, SEQ)
        GAIN = v(R4 + 1024, 768)
        JUNK = v(R4 + 1792, 256)
        SWAP = v(R7 + 1024, 2, HEADS, ROPE)
        EXPS = v(R7, 2, 512)
        PT = v(R7 + 1024, 2, 4, P)
        MMASK = v(R6, 4, ALL)
        TMP = v(BASE, 4, ALL)
        COMB = v(BASE + 2048, 2, ALL)
        HML = v(BASE + 3072, 2, 512)
        MLPT = v(R3, 2, 4, P)
        HMT = v(R3 + 1024, 2, 512)
        MTMP = v(R7, 2, 512)
        H2 = v(BASE, 2, D)
        CANDR = v(BASE + 2048, PH, 256)
        SC = v(BASE + 8192, 2, 16, NKEYS)
        SCR = v(BASE + 12288, 16, NKEYS)
        CAND = v(BASE + 14336, PH, 256)
        EQ = v(BASE + 16384, PH, TOPK, TOPK)
        PX = BASE + 18432
        PQT = v(PX, 16, SEQ)
        GROWS = [v(PX + n * D, D) for n in range((AR_N - PX) // D)] + [v(BASE + 4096 + n * D, D) for n in range(3)]
        NG = len(GROWS)
        PROD = v(BASE + 12288, D)
        DIAG = v(BASE + 13312, 4, P)
        HP2 = v(BASE + 2048, 2, 512)
        EIDX = IDX[:, 0, :].rearrange("p (i m) -> p i m", i=2)
        XTP = v(0, KT, SEQ, of=XT)
        NW = v(BASE, 2, D)
        HN2 = v(BASE + 2048, 2, D)
        MIX2 = v(BASE + 2048, KT, SEQ)
        V2 = v(BASE + 4096, 2, 512)
        Z2 = v(BASE + 5120, 2, 512)
        CV = v(BASE + 6144, 12, SEQ)
        DQF = v(BASE + 6144, 4, SEQ)
        DKF = v(BASE + 7168, 4, SEQ)
        UU = v(BASE + 8192, 2, 512)
        TQ = v(BASE + 9216, 3, 2, 512)
        C0 = BASE + 12288
        QKR = v(C0, 2, 2, 512)
        RTMP = v(C0 + 2048, 2, 512)
        TI = v(C0, 8, P)
        TU = v(C0 + 1024, 8, P)
        TW = v(C0 + 2048, 8, P)
        QKT2 = v(C0 + 3072, 2, 4, SEQ)
        AM = v(C0 + 3072, 2, 8, P)
        DEC = v(C0 + 5120, 4, 3, P)
        QKD = v(C0 + 6656, 4, 3, P)
        AA = v(C0 + 8192, 4, 3, P)
        AT = v(C0 + 9728, 3, 4, P)
        ETMP = v(C0 + 11264, 2, SEQ)
        EPT = v(2048, 2, 6, P, of=XT)
        QKDT = v(2048, 4, 3, P, of=XT)
        WO2 = v(BASE + 6144, 2, 2, D)
        MO = v(C0, 2, D)
        YSQ = v(C0 + 3072, D)
        YG = v(C0, 4, 2, SEQ)
        GU = v(C0 + 2048, 2, 2, SEQ)
        assert C0 + 11776 <= AR_N

        SS, MS, RS, HALF, MX, SM, RC, MN = (small(32) for _ in range(8))
        SILC = small(KT, 2)
        CCOL = small(KT, 2)
        CONVW = small(4, 3)
        GB = small(16)
        LF, LT1, LT2, FCOL, BCOL, IG = (small(4, 8) for _ in range(6))
        FLO, DEN = small(4), small(4)
        CW2 = small(DEPTH, 12, 4)
        FW2 = small(DEPTH, 2 * DFF // P, 3)
        FB2 = small(DEPTH, 2 * DFF // P)
        AB2 = small(DEPTH, 8)
        AE, GT, BT, GC, ST1, ST2 = small(4), *(small(2, 4) for _ in range(5))
        SV = v(2048, 16, TOPK, of=XT)
        SIF = v(2304, 16, TOPK, of=XT)
        BEST = v(2560, PH, TOPK, of=XT)
        POSF = v(2688, 2, PH, TOPK, of=XT)
        SEL = v(2944, 2, PH, TOPK, of=XT)
        GW = v(3200, 2, PICKS, of=XT)
        DOT = v(3456, 2, PICKS, of=XT)
        SUM8 = v(3712, PH, of=XT)
        DNW = v(3728, DEPTH, P, of=XT)
        SIU = IDX[:, 1, :].rearrange("p (c k) -> p c k", c=16)
        POSU = IDX[:, 2, 0:128].rearrange("p (c k) -> p c k", c=PH)
        PA = IDX[:, 2, 128:256].rearrange("p (c k) -> p c k", c=PH)

        def cols(w, lo, hi):
            return w.rearrange("(k p) n -> p k n", p=P)[:, :, lo:hi]

        def slot8(n, width):
            return RING[:, n % WSLOTS, 0:KT * width].rearrange("p (k n) -> p k n", k=KT)

        loads = []
        for b in range(12):
            loads.append(lambda n, b=b: [(slot8(n, 512), cols(a["w_ada"][0], b * 512, b * 512 + 512))])
        loads.append(lambda n: [(slot8(n, 464)[:, :, 0:448], cols(a["w_in"][0], 0, 448)),
                                (slot8(n, 464)[:, :, 448:464], cols(a["w_in"][0], 1984, 2000))])
        for lo in (448, 960, 1472):
            loads.append(lambda n, lo=lo: [(slot8(n, 512), cols(a["w_in"][0], lo, lo + 512))])
        loads.append(lambda n: [
            (RING[:, n % WSLOTS, 0:1536].rearrange("p (k n) -> p k n", k=2), a["w_uq"][0].rearrange("(k p) n -> p k n", p=P)),
            (RING[:, n % WSLOTS, 1536:2560], a["w_ukv"][0])])
        for b in range(2):
            loads.append(lambda n, b=b: [(slot8(n, 512), cols(a["w_out"][0], b * 512, b * 512 + 512))])
        for b in range(4):
            loads.append(lambda n, b=b: [(slot8(n, 512), cols(a["w_pq"][0], b * 512, b * 512 + 512))])
        loads.append(lambda n: [(RING[:, n % WSLOTS, 0:2048], a["sub_keys_T"])])
        FIRST = len(loads)
        WIN2 = [(0, 512), (512, 1024), (1024, 1536), (1536, 2048), (2048, 2560), (2560, 3072), (3072, 3592)]
        for L in range(DEPTH):
            for lo, hi in WIN2:
                loads.append(lambda n, L=L, lo=lo, hi=hi: [(slot8(n, hi - lo), cols(a["w_in_2"][L], lo, hi))])
            for b in range(2):
                loads.append(lambda n, L=L, b=b: [(slot8(n, 512), cols(a["w_out_2"][L], b * 512, b * 512 + 512))])
            for b in range(FBLK):
                loads.append(lambda n, L=L, b=b: [
                    (slot8(n, 512)[:, :, 0:256], cols(a["ffn_w_in_2"][L], b * 256, b * 256 + 256)),
                    (slot8(n, 512)[:, :, 256:512], cols(a["ffn_w_in_2"][L], DFF + b * 256, DFF + b * 256 + 256))])
        landed, count = [], [0] * WSLOTS
        for n, fn in enumerate(loads):
            count[n % WSLOTS] += 16 * len(fn(n))
            landed.append(count[n % WSLOTS])
        last_read = {}
        at = {}

        d_full, d_free, a_full, a_free = sem("d_full"), sem("d_free"), sem("a_full"), sem("a_free")
        block = ctx.enter_context(nc.Block())

        @block.tensor
        def _(pe):
            mm, turn = nc.tensor.matmul, nc.tensor.transpose
            c = {"d": 0, "a": 0, "w": 0}

            def bank_d():
                c["d"] += 1
                if c["d"] > 4:
                    pe.wait_ge(d_free, c["d"] - 4)
                return PS[:, (c["d"] - 1) % 4, :]

            def bank_a():
                c["a"] += 1
                if c["a"] > 4:
                    pe.wait_ge(a_free, c["a"] - 4)
                return PS[:, 4 + (c["a"] - 1) % 4, :]

            def weights(width=None):
                n = c["w"]
                c["w"] += 1
                pe.wait_ge(sem(f"w_in{n % WSLOTS}"), landed[n])
                return RING[:, n % WSLOTS, :] if width is None else slot8(n, width)

            def was_read(ring):
                last_read[c["w"] - 1] = (ring, c[ring])

            pe.wait_ge(sem("consts"), 16)
            pe.wait_ge(sem("silu_c"), 1)
            for b in range(12):
                w = weights(512)
                for which in (0, 1) if b < 4 else (0,):
                    o = bank_d()
                    for k in range(KT):
                        ins = mm(o, SILC[:, k, which:which + 1].to_broadcast([P, P]), w[:, k, :], start=k == 0, stop=k == KT - 1)
                    ins.then_inc(d_full, 1)
                was_read("d")
            for n in range(4):
                pe.wait_ge(sem("hn_ready"), n + 1)
                for h in range(2):
                    o = bank_a()
                    for q in range(4):
                        ins = turn(o[:, q * P:(q + 1) * P], HN[:, n % 2, (4 * h + q) * P:(4 * h + q + 1) * P], ident)
                    ins.then_inc(a_full, 1)
            pe.wait_ge(a_free, c["a"])
            w = weights(464)
            for j in (2, 3, 0, 1):
                lo = 0 if j >= 2 else QR
                o = bank_a()
                for k in range(KT):
                    ins = mm(o[:, lo:464], XTv[:, k, j * P:(j + 1) * P], w[:, k, lo:464], start=k == 0, stop=k == KT - 1)
                ins.then_inc(a_full, 1)
            was_read("a")
            at["cqkv"] = c["a"]
            w = weights(512)
            at["ml_qk"] = []
            for f in range(4):
                lo = CTX if f < 2 else 0
                o = bank_d()
                for k in range(KT):
                    ins = mm(o[:, 0:ALL - lo], w[:, k, f * P:(f + 1) * P], XTv[:, k, lo:ALL], start=k == 0, stop=k == KT - 1)
                ins.then_inc(d_full, 1)
                at["ml_qk"].append(c["d"])
            was_read("d")
            w = weights(512)
            for j in range(4):
                o = bank_a()
                for k in range(KT):
                    ins = mm(o, XTv[:, k, j * P:(j + 1) * P], w[:, k, :], start=k == 0, stop=k == KT - 1)
                ins.then_inc(a_full, 1)
            was_read("a")
            w = weights(512)
            for j in (2, 3):
                o = bank_a()
                for k in range(KT):
                    ins = mm(o, XTv[:, k, j * P:(j + 1) * P], w[:, k, :], start=k == 0, stop=k == KT - 1)
                ins.then_inc(a_full, 1)
            was_read("a")
            at["xt_read"] = c["a"]
            pe.wait_ge(sem("cn_ready"), 1)
            o = bank_a()
            for i in range(2):
                for k in range(2):
                    ins = turn(o[:, (k * 2 + i) * P:(k * 2 + i + 1) * P], CN[:, i * QR + k * P:i * QR + (k + 1) * P], ident)
            ins.then_inc(a_full, 1)
            o = bank_a()
            for j in range(4):
                ins = turn(o[:, j * P:(j + 1) * P], CN[:, 512 + j * P:512 + (j + 1) * P], ident)
            ins.then_inc(a_full, 1)
            pe.wait_ge(a_free, c["a"])
            w = weights()
            uq = w[:, 0:1536].rearrange("p (k n) -> p k n", k=2)
            for i in range(2):
                for h in range(2):
                    o = bank_a()
                    for k in range(2):
                        ins = mm(o[:, 0:384], CNT[:, (k * 2 + i) * P:(k * 2 + i + 1) * P], uq[:, k, h * 384:h * 384 + 384], start=k == 0, stop=k == 1)
                    ins.then_inc(a_full, 1)
            at["qm"] = c["a"]
            for j in range(4):
                for h in range(2):
                    o = bank_d()
                    mm(o, CNT[:, 512 + j * P:512 + (j + 1) * P], w[:, 1536 + h * 512:2048 + h * 512], start=True, stop=True).then_inc(d_full, 1)
            was_read("d")
            pe.wait_ge(sem("qk_roped"), 1)
            for hp in range(2):
                o, o2 = bank_d(), bank_a()
                for q in range(4):
                    ins = turn(o[:, q * P:(q + 1) * P], QM[:, q % 2, 2 * hp + q // 2, 0:NOPE], ident)
                ins.then_inc(d_full, 1)
                for q in range(4):
                    ins = turn(o2[0:ROPE, q * P:(q + 1) * P], QM[:, q % 2, 2 * hp + q // 2, NOPE:QK], ident)
                ins.then_inc(a_full, 1)
            for h in range(HEADS):
                o, o2 = bank_d(), bank_a()
                for j in range(4):
                    ins = turn(o[:, j * P:(j + 1) * P], KM[:, j, h, 0:NOPE], ident)
                ins.then_inc(d_full, 1)
                for j in range(4):
                    ins = turn(o2[0:ROPE, j * P:(j + 1) * P], KM[:, j, h, NOPE:QK], ident)
                ins.then_inc(a_full, 1)
            pe.wait_ge(d_free, c["d"])
            pe.wait_ge(a_free, c["a"])
            at["km_read_d"], at["km_read_a"] = c["d"], c["a"]
            units = [(h, i) for h in range(HEADS) for i in range(2)]
            at["mla_s"], at["mla_t"], at["mla_pv"] = [], [], []
            for u in range(len(units) + 2):
                if u < len(units):
                    h, i = units[u]
                    o = bank_a()
                    mm(o, QTN[:, h, i * P:(i + 1) * P], KTN[:, h, :], start=True, stop=False)
                    mm(o, QTR[:, h, i * P:(i + 1) * P], KTR[:, h, :], start=False, stop=True).then_inc(a_full, 1)
                    at["mla_s"].append(c["a"])
                if 1 <= u <= len(units):
                    pe.wait_ge(sem("mla_p"), u)
                    o = bank_a()
                    for s in range(4):
                        ins = turn(o[:, s * P:(s + 1) * P], EXPS[:, (u - 1) % 2, s * P:(s + 1) * P], ident)
                    ins.then_inc(a_full, 1)
                    at["mla_t"].append(c["a"])
                if u >= 2:
                    h, i = units[u - 2]
                    pe.wait_ge(a_free, at["mla_t"][u - 2])
                    if i == 0:
                        o_pv = bank_d()
                    for s in range(4):
                        ins = mm(o_pv[:, i * P:(i + 1) * P], VM[:, s, h, :], PT[:, (u - 2) % 2, s, :], start=s == 0, stop=s == 3)
                    if i == 1:
                        ins.then_inc(d_full, 1)
            pe.wait_ge(sem("lf_ready"), 1)
            o = bank_d()
            LE, NGT, GE, NLT = (tri[:, n, :] for n in range(4))
            ONE, NONE = ones[:, 0, :], ones[:, 1, :]
            sums = [[[(1, NONE), (0, NGT)], [(1, NGT)], [(2, LE)], [(2, ONE), (3, LE)]],
                    [[(0, NLT)], [(0, NONE), (1, NLT)], [(3, ONE), (2, GE)], [(3, GE)]]]
            for d in range(2):
                for j in range(4):
                    for n, (src, m) in enumerate(sums[d][j]):
                        ins = mm(o[:, j * 8 + d * 4:j * 8 + d * 4 + 4], m, LF[:, src, d * 4:d * 4 + 4], start=n == 0, stop=n == len(sums[d][j]) - 1)
            ins.then_inc(d_full, 1)
            pe.wait_ge(sem("bcol_ready"), 1)
            pe.wait_ge(sem("mconv"), 4)
            at["ml_v"] = []
            for h in range(HEADS):
                p0 = (h % 2) * MLQK
                for d in range(2):
                    o = bank_d()
                    for j in range(4):
                        ins = turn(o[:, j * P:(j + 1) * P], BCOL[:, j, d * 4 + h:d * 4 + h + 1].to_broadcast([P, P]), ident)
                    ins.then_inc(d_full, 1)
                for i in range(2):
                    o = bank_d()
                    mm(o, QF[p0:p0 + MLQK, h // 2, i * P:(i + 1) * P], KF[p0:p0 + MLQK, h // 2, :], start=True, stop=True).then_inc(d_full, 1)
                for i in range(2):
                    pe.wait_ge(sem("ml_p"), 2 * h + i + 1)
                    o = bank_a()
                    for s in range(4):
                        ins = turn(o[:, s * P:(s + 1) * P], COMB[:, i, s * P:(s + 1) * P], ident)
                    ins.then_inc(a_full, 1)
                pe.wait_ge(a_free, c["a"])
                o = bank_a()
                for i in range(2):
                    for s in range(4):
                        ins = mm(o[:, i * VD:(i + 1) * VD], MLPT[:, i, s, :], VML[:, s, h * VD:(h + 1) * VD], start=s == 0, stop=s == 3)
                ins.then_inc(a_full, 1)
            pe.wait_ge(sem("hml_gated"), 1)
            for h in range(2):
                o = bank_a()
                for q in range(4):
                    hd = 2 * h + q // 2
                    ins = turn(o[:, q * P:(q + 1) * P], HMT[:, q % 2, hd * VD:(hd + 1) * VD], ident)
                ins.then_inc(a_full, 1)
            pe.wait_ge(a_free, c["a"])
            pe.wait_ge(d_free, c["d"])
            for b in range(2):
                w = weights(512)
                for i in range(2):
                    o = bank_d()
                    for k in range(KT):
                        ins = mm(o, MIXT[:, k, i * P:(i + 1) * P], w[:, k, :], start=k == 0, stop=k == KT - 1)
                    ins.then_inc(d_full, 1)
                was_read("d")
            for i in range(2):
                pe.wait_ge(sem("h2_ready"), i + 1)
                for h in range(2):
                    o = bank_a()
                    for q in range(4):
                        ins = turn(o[:, q * P:(q + 1) * P], H2[:, i, (4 * h + q) * P:(4 * h + q + 1) * P], ident)
                    ins.then_inc(a_full, 1)
            pe.wait_ge(a_free, c["a"])
            for b in range(4):
                w = weights(512)
                for g in range(2):
                    o = bank_a()
                    for f in (2 * g, 2 * g + 1):
                        for k in range(KT):
                            ins = mm(o[:, (f % 2) * SEQ:(f % 2 + 1) * SEQ], w[:, k, f * P:(f + 1) * P], XTP[:, k, :], start=k == 0, stop=k == KT - 1)
                    ins.then_inc(a_full, 1)
                was_read("a")
            w = weights()
            pe.wait_ge(a_free, c["a"])
            at["sc"] = []
            for i in range(2):
                for g in range(4):
                    o = bank_a()
                    for q in range(4):
                        n = 4 * g + q
                        ins = mm(o[:, q * P:(q + 1) * P], PQT[:, n, i * P:(i + 1) * P], w[:, n * P:(n + 1) * P], start=True, stop=True)
                    ins.then_inc(a_full, 1)
                at["sc"].append(c["a"])
            was_read("a")
            for i in range(2):
                o0, o1 = bank_d(), bank_d()
                for m in range(PICKS):
                    g = 2 * PICKS + i * PICKS + m
                    pe.wait_ge(sem("diag"), i * PICKS + m + 1)
                    pe.wait_ge(sem(f"row{g % NG}"), 16 * (g // NG + 1))
                    mm(o0, DIAG[:, m % 4, :], GROWS[g % NG][:, 0:512], start=m == 0, stop=m == PICKS - 1)
                    mm(o1, DIAG[:, m % 4, :], GROWS[g % NG][:, 512:1024], start=m == 0, stop=m == PICKS - 1).then_inc(sem("v_used"), 1)
                pe.drain().then_inc(d_full, 2)
            at["L"] = []
            for L in range(DEPTH):
                m = {}
                at["L"].append(m)
                for i in range(2):
                    pe.wait_ge(sem("hn2_ready"), 4 * L + i + 1)
                    for h in range(2):
                        o = bank_a()
                        for q in range(4):
                            ins = turn(o[:, q * P:(q + 1) * P], HN2[:, i, (4 * h + q) * P:(4 * h + q + 1) * P], ident)
                        ins.then_inc(a_full, 1)
                pe.wait_ge(a_free, c["a"])
                for b in range(3):
                    w = weights(512)
                    for i in range(2):
                        o = bank_d() if b < 2 else bank_a()
                        for k in range(KT):
                            ins = mm(o, XTP[:, k, i * P:(i + 1) * P], w[:, k, :], start=k == 0, stop=k == KT - 1)
                        ins.then_inc(d_full if b < 2 else a_full, 1)
                    was_read("d" if b < 2 else "a")
                m["conv"] = []
                for b in range(3):
                    w = weights(512)
                    for g in range(2):
                        o = bank_d()
                        for f in (2 * g, 2 * g + 1):
                            for k in range(KT):
                                ins = mm(o[:, (f % 2) * SEQ:(f % 2 + 1) * SEQ], w[:, k, f * P:(f + 1) * P], XTP[:, k, :], start=k == 0, stop=k == KT - 1)
                        ins.then_inc(d_full, 1)
                        m["conv"].append(c["d"])
                    was_read("d")
                w = weights(520)
                for i in range(2):
                    o = bank_a()
                    for k in range(KT):
                        ins = mm(o, XTP[:, k, i * P:(i + 1) * P], w[:, k, 0:512], start=k == 0, stop=k == KT - 1)
                    ins.then_inc(a_full, 1)
                o = bank_a()
                for i in range(2):
                    for k in range(KT):
                        ins = mm(o[:, i * 8:i * 8 + 8], XTP[:, k, i * P:(i + 1) * P], w[:, k, 512:520], start=k == 0, stop=k == KT - 1)
                ins.then_inc(a_full, 1)
                m["ba"] = c["a"]
                was_read("a")
                pe.wait_ge(sem("rot2"), L + 1)
                for wh in range(2):
                    for g in range(2):
                        o = bank_a()
                        for q in range(4):
                            f, i = 2 * g + q // 2, q % 2
                            ins = turn(o[:, q * P:(q + 1) * P], QKR[:, wh, i, f * P:(f + 1) * P], ident)
                        ins.then_inc(a_full, 1)
                pe.wait_ge(a_free, c["a"])
                m["at_t"] = []
                units = [(h, i) for h in range(AH) for i in range(2)]
                for u in range(len(units) + 2):
                    if u < len(units):
                        h, i = units[u]
                        p0 = (h % 2) * AD
                        o = bank_d()
                        mm(o[:, 0:(i + 1) * P], QKT2[p0:p0 + AD, 0, h // 2, i * P:(i + 1) * P], QKT2[p0:p0 + AD, 1, h // 2, 0:(i + 1) * P],
                           start=True, stop=True).then_inc(d_full, 1)
                    if 1 <= u <= len(units):
                        h, i = units[u - 1]
                        pe.wait_ge(sem("at_p"), 16 * L + u)
                        o = bank_a()
                        for s in range(i + 1):
                            ins = turn(o[:, s * P:(s + 1) * P], ETMP[:, (u - 1) % 2, s * P:(s + 1) * P], ident)
                        ins.then_inc(a_full, 1)
                        m["at_t"].append(c["a"])
                    if u >= 5 and u % 4 == 1:
                        pe.wait_ge(a_free, m["at_t"][u - 2])
                        o = bank_d()
                        for n in range(u - 5, u - 1):
                            h, i = units[n]
                            p0 = (h % 2) * AD
                            for s in range(i + 1):
                                ins = mm(o[p0:p0 + AD, i * P:(i + 1) * P], V2[:, s, h * AD:(h + 1) * AD], EPT[:, n // 4 % 2, n % 4 // 2 * 3 + i + s, :], start=s == 0, stop=s == i)
                        ins.then_inc(d_full, 1)
                pe.wait_ge(sem("cv_silu"), 6 * (L + 1))
                for wh in range(3):
                    for i in range(2):
                        o = bank_a()
                        for h in range(DH):
                            ins = turn(o[:, h * P:(h + 1) * P], CV[:, wh * 4 + h, i * P:(i + 1) * P], ident)
                        ins.then_inc(a_full, 1)
                m["tq"] = c["a"]
                for wh in range(2):
                    pe.wait_ge(sem("dn_normed"), 2 * L + wh + 1)
                    for g in range(2):
                        o = bank_a()
                        for q in range(4):
                            h, i = 2 * g + q // 2, q % 2
                            ins = turn(o[:, q * P:(q + 1) * P], TQ[:, wh, i, h * P:(h + 1) * P], ident)
                        ins.then_inc(a_full, 1)
                pe.wait_ge(sem("g_ready"), L + 1)
                o = bank_d()
                mm(o[:, 0:4], tri[:, 1, :], GT[:, 0, :], start=True, stop=True)
                mm(o[:, 4:8], tri[:, 0, :], GT[:, 1, :], start=True, stop=True).then_inc(d_full, 1)
                pe.wait_ge(d_free, c["d"])
                for g in range(2):
                    o = bank_d()
                    for q in range(4):
                        h, i = 2 * g + q // 2, q % 2
                        ins = turn(o[:, q * P:(q + 1) * P], GC[:, i, h:h + 1].to_broadcast([P, P]), ident)
                    ins.then_inc(d_full, 1)
                pe.wait_ge(a_free, c["a"])
                for which, F in ((0, DQF), (1, DKF)):
                    for seg, (i, j) in enumerate(((0, 0), (1, 0), (1, 1))):
                        o = bank_d()
                        for h in range(DH):
                            ins = mm(o[:, h * P:(h + 1) * P], F[:, h, i * P:(i + 1) * P], DKF[:, h, j * P:(j + 1) * P], start=True, stop=True)
                        ins.then_inc(d_full, 1)
                pe.wait_ge(sem("aa_ready"), L + 1)
                for seg in (0, 2, 1):
                    o = bank_a()
                    for h in range(DH):
                        ins = turn(o[:, h * P:(h + 1) * P], AA[:, h, seg, :], ident)
                    ins.then_inc(a_full, 1)
                for seg in range(3):
                    o = bank_a()
                    for h in range(DH):
                        ins = turn(o[:, h * P:(h + 1) * P], QKD[:, h, seg, :], ident)
                    ins.then_inc(a_full, 1)
                m["at_aT"] = c["a"] - 4
                pe.wait_ge(sem("t_init"), L + 1)
                m["level"] = []
                for lv in range(7):
                    pe.wait_ge(sem("am_ready"), 7 * L + lv + 1)
                    pe.wait_ge(d_free, c["d"])
                    for half in range(2):
                        o = bank_a()
                        for h in range(DH):
                            n = half * 4 + h
                            ins = mm(o[:, h * P:(h + 1) * P], AM[:, lv % 2, n, :], TI[:, n, :], start=True, stop=True)
                        ins.then_inc(a_full, 1)
                    pe.wait_ge(a_free, c["a"])
                    for half in range(2):
                        if lv < 6:
                            o = bank_d()
                            for h in range(DH):
                                n = half * 4 + h
                                ins = mm(o[:, h * P:(h + 1) * P], TU[:, n, :], TW[:, n, :], start=True, stop=True)
                            ins.then_inc(d_full, 1)
                        o = bank_d()
                        for h in range(DH):
                            n = half * 4 + h
                            ins = mm(o[:, h * P:(h + 1) * P], TW[:, n, :], TU[:, n, :], start=True, stop=True)
                        ins.then_inc(d_full, 1)
                    m["level"].append(c["d"])
                pe.wait_ge(d_free, c["d"])
                pe.wait_ge(sem("vb_ready"), L + 1)
                o = bank_d()
                for h in range(DH):
                    ins = mm(o[:, h * P:(h + 1) * P], TU[:, h, :], TQ[:, 2, 0, h * P:(h + 1) * P], start=True, stop=True)
                ins.then_inc(d_full, 1)
                pe.wait_ge(d_free, c["d"])
                o = bank_d()
                for h in range(DH):
                    ins = mm(o[:, h * P:(h + 1) * P], AT[:, 2, h, :], UU[:, 0, h * P:(h + 1) * P], start=True, stop=True)
                ins.then_inc(d_full, 1)
                pe.wait_ge(d_free, c["d"])
                o = bank_d()
                for h in range(DH):
                    ins = mm(o[:, h * P:(h + 1) * P], TU[:, 4 + h, :], TQ[:, 2, 1, h * P:(h + 1) * P], start=True, stop=True)
                ins.then_inc(d_full, 1)
                pe.wait_ge(d_free, c["d"])
                o = bank_a()
                for h in range(DH):
                    ins = mm(o[:, h * P:(h + 1) * P], QKDT[:, h, 0, :], UU[:, 0, h * P:(h + 1) * P], start=True, stop=True)
                ins.then_inc(a_full, 1)
                o = bank_a()
                for h in range(DH):
                    mm(o[:, h * P:(h + 1) * P], QKDT[:, h, 1, :], UU[:, 0, h * P:(h + 1) * P], start=True, stop=False)
                    ins = mm(o[:, h * P:(h + 1) * P], QKDT[:, h, 2, :], UU[:, 1, h * P:(h + 1) * P], start=False, stop=True)
                ins.then_inc(a_full, 1)
                m["o"] = c["a"]
                pe.wait_ge(sem("do_gated"), L + 1)
                for g in range(2):
                    o = bank_a()
                    for q in range(4):
                        h, i = 2 * g + q // 2, q % 2
                        ins = turn(o[:, q * P:(q + 1) * P], TQ[:, 0, i, h * P:(h + 1) * P], ident)
                    ins.then_inc(a_full, 1)
                pe.wait_ge(a_free, c["a"])
                pe.wait_ge(d_free, c["d"])
                for b in range(2):
                    w = weights(512)
                    for i in range(2):
                        o = bank_d()
                        for k in range(KT):
                            ins = mm(o, MIX2[:, k, i * P:(i + 1) * P], w[:, k, :], start=k == 0, stop=k == KT - 1)
                        ins.then_inc(d_full, 1)
                    was_read("d")
                m["mix"] = c["d"]
                for i in range(2):
                    pe.wait_ge(sem("hn2_ready"), 4 * L + 2 + i + 1)
                    for h in range(2):
                        o = bank_a()
                        for q in range(4):
                            ins = turn(o[:, q * P:(q + 1) * P], HN2[:, i, (4 * h + q) * P:(4 * h + q + 1) * P], ident)
                        ins.then_inc(a_full, 1)
                pe.wait_ge(a_free, c["a"])
                acc = [bank_a() for _ in range(4)]
                m["ffn"] = []
                for b in range(FBLK + 1):
                    if b < FBLK:
                        w = weights(512)
                        for g in range(2):
                            o = bank_d()
                            for wh in range(2):
                                for k in range(KT):
                                    ins = mm(o[:, wh * SEQ:(wh + 1) * SEQ], w[:, k, wh * 256 + g * P:wh * 256 + (g + 1) * P], XTP[:, k, :], start=k == 0, stop=k == KT - 1)
                            ins.then_inc(d_full, 1)
                            m["ffn"].append(c["d"])
                        was_read("d")
                    if b >= 1:
                        n = FBLK * L + b - 1
                        pe.wait_ge(sem("gu_ready"), 2 * n + 2)
                        pe.wait_ge(sem(f"wo2_in{n % 2}"), 16 * (n // 2 + 1))
                        for g in range(2):
                            for i in range(2):
                                for h in range(2):
                                    ins = mm(acc[2 * i + h], GU[:, (b - 1) % 2, g, i * P:(i + 1) * P], WO2[:, n % 2, g, h * 512:(h + 1) * 512],
                                             start=b == 1 and g == 0, stop=b == FBLK and g == 1)
                                    if b == FBLK and g == 1:
                                        ins.then_inc(a_full, 1)
                        if b < FBLK:
                            ins.then_inc(sem("wo2_read"), 1)
                m["end"] = c["a"]


        @block.sync
        def _(sp):
            def load(n):
                if n >= WSLOTS:
                    ring, value = last_read[n - WSLOTS]
                    sp.wait_ge(d_full if ring == "d" else a_full, value)
                for dst, src in loads[n](n):
                    sp.dma_start(dst, src).then_inc(sem(f"w_in{n % WSLOTS}"), 16)

            sp.dma_start(CCOL[:, :, :], a["cc"].rearrange("p (k w) -> p k w", w=2)).then_inc(sem("cc_in"), 16)
            sp.dma_start(v(0, NCONST), a["consts"]).then_inc(sem("consts"), 16)
            load(0)
            ba = a["b_ada"]
            for dst, piece in ((MODA[:, 0, :], 0), (MODA[:, 2, :], 0), (MODA[:, 1, :], 1), (MODA[:, 3, :], 1)):
                sp.dma_start(dst, ba[:, piece * D:(piece + 1) * D].to_broadcast([P, D])).then_inc(sem("moda_in"), 16)
            load(1)
            sp.dma_start(X[:, :, :], a["x"][0].rearrange("(t p) d -> p t d", p=P)).then_inc(sem("x_in"), 16)
            sp.dma_start(XC[:, :, :], a["ctx"][0].rearrange("(t p) d -> p t d", p=P)).then_inc(sem("xc_in"), 16)
            load(2)
            for dst, piece in ((MODB[:, 0, :], 2), (MODB[:, 1, :], 3), (MODB[:, 2, :], 4), (MODB[:, 3, :], 5)):
                sp.dma_start(dst, ba[:, piece * D:(piece + 1) * D].to_broadcast([P, D])).then_inc(sem("modb_in"), 16)
            for n, name in enumerate(("g_norm1", "g_norm2")):
                sp.dma_start(GN[:, n, :], a[name].to_broadcast([P, D])).then_inc(sem("gn_in"), 16)
            sp.dma_start(CONVW[:, :, :], a["conv1"].rearrange("p (f j) -> p f j", j=3)).then_inc(sem("small_in"), 16)
            sp.dma_start(GB[:, :], a["gate_bias"].to_broadcast([P, 16])).then_inc(sem("small_in"), 16)
            sp.dma_start(CW2[:, :, :, :], a["conv2"].rearrange("p (l f j) -> p l f j", l=DEPTH, j=4)).then_inc(sem("small_in"), 16)
            sp.dma_start(FW2[:, :, :, :], a["ffn_conv"].rearrange("p (l f j) -> p l f j", l=DEPTH, j=3)).then_inc(sem("small_in"), 16)
            sp.dma_start(FB2[:, :, :], a["ffn_bias"].rearrange("p (l f) -> p l f", l=DEPTH)).then_inc(sem("small_in"), 16)
            sp.dma_start(AB2[:, :, :], a["decay"].to_broadcast([P, 16]).rearrange("p (l n) -> p l n", l=DEPTH)).then_inc(sem("small_in"), 16)
            for n in range(3, len(loads)):
                load(n)
            sp.wait_ge(sem("x_ready"), 2 + 2 * DEPTH)
            sp.dma_start(out[0].rearrange("(t p) d -> p t d", p=P), X[:, :, :]).then_inc(sem("stored"), 16)
            sp.wait_ge(sem("stored"), 16)

        @block.gpsimd
        def _(pool):
            nc.gpsimd.memset(HALF[:, :], -0.5).then_inc(sem("half"), 1)
            pool.wait_ge(sem("half"), 1)

            def rsqrt(step, n):
                pool.wait_ge(sem("ms_ready"), step)
                nc.gpsimd.tensor_tensor(RS[:, 0:n], MS[:, 0:n], HALF[:, 0:n], ALU.pow).then_inc(sem("rs_ready"), 1)

            rsqrt(1, 4)
            pool.wait_ge(sem("hn_ready"), 4)
            for lo, hi, name in ((0, QR, "g_cq"), (QR, QR + KVR, "g_ckv"), (384, 576, "g_qn"), (576, 768, "g_kn")):
                pool.dma_start(GAIN[:, lo:hi], a[name].to_broadcast([P, hi - lo])).then_inc(sem("gain_in"), 16)
            pool.dma_start(GOUT[:, :], a["g_mlstm"].to_broadcast([P, 512])).then_inc(sem("gout_in"), 16)
            rsqrt(2, 6)
            rsqrt(3, 24)
            pool.wait_ge(d_full, at["km_read_d"])
            pool.wait_ge(a_full, at["km_read_a"])
            pool.dma_start(MMASK[:, :, :], a["mmask"].rearrange("p (a t) -> p a t", a=4)).then_inc(sem("mmask_in"), 16)
            rsqrt(4, 8)
            rsqrt(5, 2)
            for g in range(4 * PICKS):
                which, i, m = g // (2 * PICKS), g // PICKS % 2, g % PICKS
                if m == 0 and which == 0:
                    pool.wait_ge(sem("eidx"), i + 1)
                if g == 0:
                    pool.wait_ge(a_full, at["sc"][1])
                old = g - NG
                if 0 <= old < 2 * PICKS:
                    pool.wait_ge(sem("u_used"), old + 1)
                elif old >= 0:
                    pool.wait_ge(sem("v_used"), old - 2 * PICKS + 1)
                nc.gpsimd.indirect_dma_start(
                    GROWS[g % NG], None, a["expert_u" if which == 0 else "expert_v"],
                    bass.IndirectOffsetOnAxis(ap=EIDX[:, i, m:m + 1], axis=0)).then_inc(sem(f"row{g % NG}"), 16)
            for L in range(DEPTH):
                m = at["L"][L]

                def gains(slot, name):
                    pool.dma_start(NW[:, slot, :], a[name][L:L + 1, :].to_broadcast([P, D])).then_inc(sem(f"nw_in{slot}"), 16)

                if L == 0:
                    pool.wait_ge(sem("u_used"), 2 * PICKS)
                    pool.dma_start(DNW[:, :, :], a["dn_norm"].to_broadcast([P, DEPTH * P]).rearrange("p (l n) -> p l n", l=DEPTH)).then_inc(sem("dnw_in"), 16)
                else:
                    pool.wait_ge(sem("x_ready"), 2 + 2 * L)
                gains(0, "norm_pre_mix_2")
                gains(1, "norm_post_mix_2")
                rsqrt(6 + 6 * L, 2)
                rsqrt(7 + 6 * L, 16)
                pool.wait_ge(a_free, m["at_aT"])
                for lv in range(7):
                    if lv >= 2:
                        pool.wait_ge(d_full, m["level"][lv - 2])
                    nc.gpsimd.tensor_tensor(AM[:, lv % 2, :, :], AT[:, 0:2, :, :].rearrange("p s h j -> p (s h) j"),
                                            level[:, lv, :].unsqueeze(1).to_broadcast([P, 8, P]), ALU.mult).then_inc(sem("am_ready"), 1)
                rsqrt(8 + 6 * L, 8)
                rsqrt(9 + 6 * L, 2)
                pool.wait_ge(sem("x_ready"), 3 + 2 * L)
                gains(0, "norm_pre_ffn_2")
                gains(1, "norm_post_ffn_2")
                rsqrt(10 + 6 * L, 2)
                for b in range(FBLK):
                    n = FBLK * L + b
                    if b == 0:
                        pool.wait_ge(d_full, m["mix"])
                    if b >= 2:
                        pool.wait_ge(sem("wo2_read"), (FBLK - 1) * L + b - 1)
                    pool.dma_start(WO2[:, n % 2, :, :], a["ffn_w_out_2"][L].rearrange("(b g p) n -> b p g n", g=2, p=P)[b]).then_inc(sem(f"wo2_in{n % 2}"), 16)
                rsqrt(11 + 6 * L, 2)

        @block.scalar
        def _(act):
            af = nc.scalar.activation
            c = {"a": 0}

            def full():
                c["a"] += 1
                act.wait_ge(a_full, c["a"])
                return PS[:, 4 + (c["a"] - 1) % 4, :]

            def squares(jobs):
                for k, (junk, src, n) in enumerate(jobs):
                    if k:
                        act.drain()
                    ins = af(junk, src, ACT.Square, accum_out=SS[:, n:n + 1])
                ins.then_inc(sem("ss_ready"), 1)

            act.wait_ge(sem("cc_in"), 16)
            af(SILC[:, :, :], CCOL[:, :, :], ACT.Silu).then_inc(sem("silu_c"), 1)
            act.wait_ge(sem("x_in"), 16)
            act.wait_ge(sem("xc_in"), 16)
            squares([(HN[:, 0, :], X[:, n, :] if n < 2 else XC[:, n - 2, :], n) for n in range(4)])
            for n, j in enumerate((2, 3, 0, 1)):
                for h in range(2):
                    o = full()
                    act.copy(XTv[:, 4 * h:4 * h + 4, j * P:(j + 1) * P], o.rearrange("p (k t) -> p k t", k=4)).then_inc(a_free, 1)
            for j in (2, 3, 0, 1):
                lo = 0 if j >= 2 else QR
                o = full()
                act.copy(CQKV[:, j, lo:448], o[:, lo:448])
                act.copy(GATE[:, j, :], o[:, 448:464]).then_inc(a_free, 1)
            act.drain()
            squares([(JUNK[:, 0:QR], CQKV[:, 2 + n, 0:QR], n) for n in range(2)]
                    + [(JUNK[:, 0:KVR], CQKV[:, j, QR:QR + KVR], 2 + j) for j in range(4)])
            act.wait_ge(sem("small_in"), 6 * 16)
            qkf = [QF[:, 0, :], QF[:, 1, :], KF[:, 0, :], KF[:, 1, :]]
            for f in range(4):
                n = at["ml_qk"][f]
                act.wait_ge(d_full, n)
                act.mul(qkf[f], PS[:, (n - 1) % 4, 0:SEQ if f < 2 else ALL], CONVW[:, f, 1:2]).then_inc(sem("centre_tap"), 1)
            for j in range(4):
                o = full()
                act.copy(VML[:, j, :], o).then_inc(a_free, 1)
            for i in range(2):
                o = full()
                af(OML[:, i, :], o, ACT.Sigmoid).then_inc(a_free, 1)
            for f in range(4):
                act.wait_ge(d_free, at["ml_qk"][f])
                af(qkf[f], qkf[f], ACT.Silu).then_inc(sem("mconv"), 1)
            for n in range(2):
                o = full()
                act.copy(CNT[:, n * 512:(n + 1) * 512], o).then_inc(a_free, 1)
            for i in range(2):
                for h in range(2):
                    o = full()
                    act.copy(QM[:, i, 2 * h:2 * h + 2, :], o[:, 0:384].rearrange("p (h d) -> p h d", h=2)).then_inc(a_free, 1)
            act.drain()
            act.wait_ge(sem("km_ready"), 1)
            squares([(JUNK[:, 0:QK], (QM[:, n, h, :] if n < 2 else KM[:, n - 2, h, :]), 4 * n + h) for n in range(6) for h in range(HEADS)])
            act.wait_ge(sem("fx_ready"), 1)
            af(LT1[:, :, :], LT2[:, :, :], ACT.Abs)
            act.drain()
            af(LT1[:, :, :], LT1[:, :, :], ACT.Exp, scale=-1.0).then_inc(sem("lf_exp"), 1)
            act.wait_ge(sem("lf_plus1"), 1)
            af(LT1[:, :, :], LT1[:, :, :], ACT.Ln).then_inc(sem("lf_ln"), 1)
            for hp in range(2):
                o = full()
                act.copy(QTR[:, 2 * hp:2 * hp + 2, :], o[0:ROPE, :].rearrange("p (h t) -> p h t", h=2)).then_inc(a_free, 1)
            for h in range(HEADS):
                o = full()
                act.copy(KTR[:, h, :], o[0:ROPE, :]).then_inc(a_free, 1)
            for u in range(9):
                if u < 8:
                    o = full()
                    act.wait_ge(sem("mla_max"), u + 1)
                    af(EXPS[:, u % 2, :], o, ACT.Exp, bias=MX[:, u:u + 1], scale=float(QK) ** -0.5, accum_out=SM[:, u:u + 1]).then_inc(a_free, 1)
                if u >= 1:
                    o = full()
                    act.copy(PT[:, (u - 1) % 2, :, :], o.rearrange("p (s q) -> p s q", s=4)).then_inc(a_free, 1)
            for h in range(HEADS):
                act.wait_ge(sem("ml_max"), h + 1)
                for n in range(4):
                    af(TMP[:, n, :], TMP[:, n, :], ACT.Exp, bias=MX[:, 8 + n:9 + n])
                af(FLO[:, :], FLO[:, :], ACT.Exp).then_inc(sem("ml_exp"), 1)
                for i in range(2):
                    o = full()
                    act.copy(MLPT[:, i, :, :], o.rearrange("p (s q) -> p s q", s=4)).then_inc(a_free, 1)
                o = full()
                act.copy(HML[:, :, h * VD:(h + 1) * VD], o[:, 0:2 * VD].rearrange("p (i e) -> p i e", i=2)).then_inc(a_free, 1)
            act.drain()
            squares([(JUNK[:, 0:VD], HML[:, i, h * VD:(h + 1) * VD], 4 * i + h) for i in range(2) for h in range(HEADS)])
            for h in range(2):
                o = full()
                act.copy(MIXT[:, 4 + 2 * h:6 + 2 * h, :], o.rearrange("p (k t) -> p k t", k=2)).then_inc(a_free, 1)
            act.wait_ge(sem("x_ready"), 1)
            squares([(v(R7 + 1024, D), X[:, i, :], i) for i in range(2)])
            for i in range(2):
                for h in range(2):
                    o = full()
                    act.copy(XTP[:, 4 * h:4 * h + 4, i * P:(i + 1) * P], o.rearrange("p (k t) -> p k t", k=4)).then_inc(a_free, 1)
            for g in range(8):
                o = full()
                act.copy(PQT[:, 2 * g:2 * g + 2, :], o.rearrange("p (f t) -> p f t", f=2)).then_inc(a_free, 1)
            for i in range(2):
                for g in range(4):
                    o = full()
                    act.copy(SC[:, i, 4 * g:4 * g + 4, :], o.rearrange("p (c k) -> p c k", c=4)).then_inc(a_free, 1)
            for i in range(2):
                act.wait_ge(sem("best_ready"), i + 1)
                af(GW[:, i, :], GW[:, i, :], ACT.Exp).then_inc(sem("best_exp"), 1)
            for i in range(2):
                act.wait_ge(sem("u_used"), (i + 1) * PICKS)
                af(DOT[:, i, :], DOT[:, i, :], ACT.Gelu).then_inc(sem("gelu_done"), 1)
            for i in range(2):
                act.wait_ge(sem("gw_ready"), i + 1)
                for m in range(PICKS):
                    n = i * PICKS + m
                    if n >= 4:
                        act.wait_ge(sem("v_used"), n - 3)
                    act.mul(DIAG[:, n % 4, :], ident, GW[:, i, m:m + 1]).then_inc(sem("diag"), 1)
            for L in range(DEPTH):
                m = at["L"][L]

                def x_squares(count):
                    act.wait_ge(sem("x_ready"), count)
                    squares([(MO[:, i, :], X[:, i, :], i) for i in range(2)])

                def turned():
                    for i in range(2):
                        for h in range(2):
                            o = full()
                            act.copy(XTP[:, 4 * h:4 * h + 4, i * P:(i + 1) * P], o.rearrange("p (k t) -> p k t", k=4)).then_inc(a_free, 1)

                x_squares(2 + 2 * L)
                turned()
                for i in range(2):
                    o = full()
                    act.copy(V2[:, i, :], o).then_inc(a_free, 1)
                for g in range(6):
                    n = m["conv"][g]
                    act.wait_ge(d_full, n)
                    for f in range(2):
                        ins = act.mul(CV[:, 2 * g + f, :], PS[:, (n - 1) % 4, f * SEQ:(f + 1) * SEQ], CW2[:, L, 2 * g + f, 3:4])
                    ins.then_inc(sem("cv_tap"), 1)
                for g in range(6):
                    act.wait_ge(d_free, m["conv"][g])
                    af(CV[:, 2 * g:2 * g + 2, :], CV[:, 2 * g:2 * g + 2, :], ACT.Silu).then_inc(sem("cv_silu"), 1)
                for i in range(2):
                    o = full()
                    af(Z2[:, i, :], o, ACT.Silu).then_inc(a_free, 1)
                o = full()
                ob = o[:, 0:16].rearrange("p (i n) -> p i n", i=2)
                af(BT[:, :, :], ob[:, :, 0:4], ACT.Sigmoid)
                act.copy(ST1[:, :, :], ob[:, :, 4:8]).then_inc(a_free, 1)
                act.wait_ge(sem("sp_in"), L + 1)
                af(ST2[:, :, :], ST1[:, :, :], ACT.Abs)
                act.drain()
                af(AE[:, :], AB2[:, L, 0:4], ACT.Exp)
                af(ST2[:, :, :], ST2[:, :, :], ACT.Exp, scale=-1.0).then_inc(sem("sp_exp"), 1)
                act.wait_ge(sem("sp_plus1"), L + 1)
                af(ST2[:, :, :], ST2[:, :, :], ACT.Ln).then_inc(sem("sp_ln"), 1)
                for wh in range(2):
                    for g in range(2):
                        o = full()
                        act.copy(QKT2[:, wh, 2 * g:2 * g + 2, :], o.rearrange("p (f t) -> p f t", f=2)).then_inc(a_free, 1)
                for u in range(17):
                    if u < 16:
                        w = (u % 2 + 1) * P
                        act.wait_ge(sem("at_max"), 16 * L + u + 1)
                        af(ETMP[:, u % 2, 0:w], ETMP[:, u % 2, 0:w], ACT.Exp, bias=MX[:, u:u + 1], accum_out=SM[:, u:u + 1]).then_inc(sem("at_exp"), 1)
                    if u >= 1:
                        s = (u - 1) % 2 + 1
                        o = full()
                        at_ = (u - 1) % 4 // 2 * 3 + s - 1
                        act.copy(EPT[:, (u - 1) // 4 % 2, at_:at_ + s, :], o[:, 0:s * P].rearrange("p (s q) -> p s q", s=s)).then_inc(a_free, 1)
                for wh in range(3):
                    for i in range(2):
                        o = full()
                        act.copy(TQ[:, wh, i, :], o).then_inc(a_free, 1)
                act.drain()
                squares([(v(C0 + 3072, P), TQ[:, wh, i, h * P:(h + 1) * P], wh * 8 + i * 4 + h)
                         for wh in range(2) for i in range(2) for h in range(DH)])
                for F in (DQF, DKF):
                    for g in range(2):
                        o = full()
                        act.copy(F[:, 2 * g:2 * g + 2, :], o.rearrange("p (h t) -> p h t", h=2)).then_inc(a_free, 1)
                act.wait_ge(sem("dec_in"), L + 1)
                af(DEC[:, :, :, :], DEC[:, :, :, :], ACT.Exp, scale=-1.0).then_inc(sem("dec_exp"), 1)
                for n in range(3):
                    o = full()
                    act.copy(AT[:, n, :, :], o.rearrange("p (h j) -> p h j", h=4)).then_inc(a_free, 1)
                for seg in range(3):
                    o = full()
                    act.copy(QKDT[:, :, seg, :], o.rearrange("p (h j) -> p h j", h=4)).then_inc(a_free, 1)
                for lv in range(7):
                    for half in range(2):
                        o = full()
                        act.copy(TW[:, 4 * half:4 * half + 4, :], o.rearrange("p (h j) -> p h j", h=4)).then_inc(a_free, 1)
                for i in range(2):
                    o = full()
                    act.copy(TQ[:, 1, i, :], o).then_inc(a_free, 1)
                act.drain()
                squares([(v(C0 + 3072, P), TQ[:, 1, i, h * P:(h + 1) * P], i * 4 + h) for i in range(2) for h in range(DH)])
                for g in range(2):
                    o = full()
                    act.copy(MIX2[:, 4 + 2 * g:6 + 2 * g, :], o.rearrange("p (k t) -> p k t", k=2)).then_inc(a_free, 1)
                act.wait_ge(d_free, m["mix"])
                squares([(YSQ, MO[:, i, :], i) for i in range(2)])
                act.wait_ge(sem("x_ready"), 3 + 2 * L)
                squares([(YSQ, X[:, i, :], i) for i in range(2)])
                turned()
                for n in range(2 * FBLK + 1):
                    if n < 2 * FBLK:
                        bank = m["ffn"][n]
                        act.wait_ge(d_full, bank)
                        N = 2 * FBLK * L + n
                        if N >= 4:
                            act.wait_ge(sem("gu_ready"), N - 3)
                        for wh in range(2):
                            f = wh * DFF // P + n
                            ins = af(YG[:, n % 4, wh, :], PS[:, (bank - 1) % 4, wh * SEQ:(wh + 1) * SEQ], ACT.Identity,
                                     scale=FW2[:, L, f, 2:3], bias=FB2[:, L, f:f + 1])
                        ins.then_inc(sem("ffn_tap"), 1)
                    if n >= 1:
                        act.wait_ge(d_free, m["ffn"][n - 1])
                        af(YG[:, (n - 1) % 4, 0, :], YG[:, (n - 1) % 4, 0, :], ACT.Gelu_apprx_tanh).then_inc(sem("ffn_gelu"), 1)
                for i in range(2):
                    for h in range(2):
                        o = full()
                        act.copy(MO[:, i, h * 512:(h + 1) * 512], o).then_inc(a_free, 1)
                act.drain()
                squares([(YSQ, MO[:, i, :], i) for i in range(2)])

        @block.vector
        def _(dve):
            tt, ts, stt, ttr = nc.vector.tensor_tensor, nc.vector.tensor_scalar, nc.vector.scalar_tensor_tensor, nc.vector.tensor_tensor_reduce
            copy = nc.vector.tensor_copy
            c = {"d": 0, "norm": 0}

            def full():
                c["d"] += 1
                dve.wait_ge(d_full, c["d"])
                return PS[:, (c["d"] - 1) % 4, :]

            def rsqrt_of_mean(parts, eps_only=False):
                c["norm"] += 1
                dve.wait_ge(sem("ss_ready"), c["norm"])
                for lo, hi, width in parts:
                    ins = ts(MS[:, lo:hi], SS[:, lo:hi], 1.0 / width, EPS, ALU.mult, ALU.add)
                ins.then_inc(sem("ms_ready"), 1)
                dve.wait_ge(sem("rs_ready"), c["norm"])

            def bcast(ap, at_, shape):
                return ap.unsqueeze(at_).to_broadcast(shape)

            dve.wait_ge(sem("moda_in"), 4 * 16)

            def normed(n):
                src = X[:, n, :] if n < 2 else XC[:, n - 2, :]
                if n >= 2:
                    dve.wait_ge(a_full, 2 * (n - 1))
                which = 0 if n < 2 else 2
                stt(HN[:, n % 2, :], src, RS[:, n:n + 1], MODA[:, which + 1, :], ALU.mult, ALU.mult)
                dve.drain()
                tt(HN[:, n % 2, :], HN[:, n % 2, :], MODA[:, which, :], ALU.add).then_inc(sem("hn_ready"), 1)

            for b in range(12):
                if b == 4:
                    dve.wait_ge(sem("gn_in"), 2 * 16)
                    dve.wait_ge(sem("modb_in"), 4 * 16)
                    dve.drain()
                    for n in (1, 3):
                        stt(MODA[:, n, :], MODA[:, n, :], 1.0, GN[:, 0, :], ALU.add, ALU.mult)
                    rsqrt_of_mean([(0, 4, D)])
                    dve.drain()
                    normed(0)
                    normed(1)
                half = slice(b % 2 * 512, b % 2 * 512 + 512)
                for dst in ([MODA[:, b // 2, half], MODA[:, 2 + b // 2, half]] if b < 4 else [MODB[:, b // 2 - 2, half]]):
                    o = full()
                    tt(dst, o, dst, ALU.add).then_inc(d_free, 1)
            dve.drain()
            stt(MODB[:, 2, :], MODB[:, 2, :], 1.0, GN[:, 1, :], ALU.add, ALU.mult)
            normed(2)
            normed(3)
            dve.wait_ge(sem("gain_in"), 4 * 16)
            rsqrt_of_mean([(0, 2, QR), (2, 6, KVR)])
            for i in range(2):
                stt(CN[:, i * QR:(i + 1) * QR], CQKV[:, 2 + i, 0:QR], RS[:, i:i + 1], GAIN[:, 0:QR], ALU.mult, ALU.mult)
            for j in range(4):
                ins = stt(CN[:, 512 + j * P:512 + (j + 1) * P], CQKV[:, j, QR:QR + KVR], RS[:, 2 + j:3 + j], GAIN[:, QR:QR + KVR], ALU.mult, ALU.mult)
            ins.then_inc(sem("cn_ready"), 1)
            for f in range(4):
                o = full()
                dve.wait_ge(sem("centre_tap"), f + 1)
                n = 1 if f < 2 else 2
                y = (QF[:, f, :] if f < 2 else KF[:, f - 2, :]).rearrange("p (s t) -> p s t", s=n)
                x = o[:, 0:n * SEQ].rearrange("p (s t) -> p s t", s=n)
                stt(y[:, :, 1:SEQ], x[:, :, 0:SEQ - 1], CONVW[:, f, 0:1], y[:, :, 1:SEQ], ALU.mult, ALU.add)
                dve.drain()
                stt(y[:, :, 0:SEQ - 1], x[:, :, 1:SEQ], CONVW[:, f, 2:3], y[:, :, 0:SEQ - 1], ALU.mult, ALU.add).then_inc(d_free, 1)
            dve.wait_ge(sem("small_in"), 6 * 16)
            dve.wait_ge(a_free, at["cqkv"])
            tt(IG[:, :, :], GATE[:, :, 0:8], bcast(GB[:, 0:8], 1, [P, 4, 8]), ALU.add)
            tt(LT2[:, :, :], GATE[:, :, 8:16], bcast(GB[:, 8:16], 1, [P, 4, 8]), ALU.add).then_inc(sem("fx_ready"), 1)
            for j in range(4):
                for h in range(2):
                    o = full().rearrange("p (h e) -> p h e", h=2)
                    copy(KM[:, j, 2 * h:2 * h + 2, 0:NOPE], o[:, :, 0:NOPE])
                    copy(VM[:, j, 2 * h:2 * h + 2, :], o[:, :, NOPE:NOPE + VD]).then_inc(d_free, 1)
            for j in range(4):
                ins = copy(KM[:, j, :, NOPE:QK], bcast(CQKV[:, j, QR + KVR:448], 1, [P, HEADS, ROPE]))
            ins.then_inc(sem("km_ready"), 1)
            rsqrt_of_mean([(0, 24, QK)])
            for n in range(6):
                for h in range(HEADS):
                    t = QM[:, n, h, :] if n < 2 else KM[:, n - 2, h, :]
                    stt(t, t, RS[:, 4 * n + h:4 * n + h + 1], GAIN[:, 384:576] if n < 2 else GAIN[:, 576:768], ALU.mult, ALU.mult)
            dve.drain()
            for n in range(4):
                t = QM[:, n, :, NOPE:QK] if n < 2 else KM[:, n, :, NOPE:QK]
                i = n % 2
                t5 = t.rearrange("p h (a f e) -> p h a f e", a=2, f=2)
                s5 = SWAP[:, n % 2, :, :].rearrange("p h (a f e) -> p h a f e", a=2, f=2)
                sin = rope1[:, 1, i, :].rearrange("p (a f e) -> p a f e", a=2, f=2)
                for f in range(2):
                    tt(s5[:, :, :, f, :], t5[:, :, :, 1 - f, :], bcast(sin[:, :, f, :], 1, [P, HEADS, 2, 16]), ALU.mult)
                dve.drain()
                tt(t, t, bcast(rope1[:, 0, i, :], 1, [P, HEADS, ROPE]), ALU.mult)
                dve.drain()
                ins = tt(t, t, SWAP[:, n % 2, :, :], ALU.add)
            ins.then_inc(sem("qk_roped"), 1)
            dve.wait_ge(sem("lf_exp"), 1)
            ts(LT1[:, :, :], LT1[:, :, :], 1.0, None, ALU.add).then_inc(sem("lf_plus1"), 1)
            ts(LT2[:, :, :], LT2[:, :, :], 0.0, None, ALU.min)
            dve.wait_ge(sem("lf_ln"), 1)
            dve.drain()
            tt(LF[:, :, :], LT2[:, :, :], LT1[:, :, :], ALU.subtract).then_inc(sem("lf_ready"), 1)
            for hp in range(2):
                o = full()
                copy(QTN[:, 2 * hp:2 * hp + 2, :], o.rearrange("p (h t) -> p h t", h=2)).then_inc(d_free, 1)
            for h in range(HEADS):
                o = full()
                copy(KTN[:, h, :], o).then_inc(d_free, 1)
            for u in range(10):
                if u < 8:
                    n = at["mla_s"][u]
                    dve.wait_ge(a_full, n)
                    nc.vector.reduce_max(MN[:, u:u + 1], PS[:, 4 + (n - 1) % 4, :], AX.X)
                    dve.drain()
                    ts(MX[:, u:u + 1], MN[:, u:u + 1], -float(QK) ** -0.5, None, ALU.mult).then_inc(sem("mla_max"), 1)
                if 1 <= u <= 8:
                    dve.wait_ge(a_free, at["mla_s"][u - 1])
                    nc.vector.reciprocal(RC[:, u - 1:u], SM[:, u - 1:u])
                    dve.drain()
                    ts(EXPS[:, (u - 1) % 2, :], EXPS[:, (u - 1) % 2, :], RC[:, u - 1:u], None, ALU.mult).then_inc(sem("mla_p"), 1)
                if u >= 2 and u % 2 == 1:
                    o = full()
                    copy(MIXT[:, (u - 3) // 2, :], o[:, 0:SEQ]).then_inc(d_free, 1)
            o = full()
            copy(FCOL[:, :, :], o[:, 0:32].rearrange("p (j n) -> p j n", j=4)).then_inc(d_free, 1)
            dve.drain()
            tt(BCOL[:, :, :], IG[:, :, :], FCOL[:, :, :], ALU.subtract).then_inc(sem("bcol_ready"), 1)
            dve.wait_ge(sem("mmask_in"), 16)
            for h in range(HEADS):
                for d in range(2):
                    o = full()
                    for i in range(2):
                        n = 2 * i + d
                        ins = ttr(out=TMP[:, n, :], in0=o, in1=MMASK[:, n, :], scale=1.0, scalar=0.0, op0=ALU.add, op1=ALU.max, accum_out=MN[:, 8 + n:9 + n])
                    ins.then_inc(d_free, 1)
                dve.drain()
                ts(MX[:, 8:12], MN[:, 8:12], -1.0, None, ALU.mult)
                stt(FLO[:, :].rearrange("p (i d) -> p i d", i=2), MN[:, 8:12].rearrange("p (i d) -> p i d", i=2), -1.0,
                    FCOL[:, 2:4, h::4], ALU.mult, ALU.subtract)
                dve.drain()
                ts(FLO[:, :], FLO[:, :], 88.0, None, ALU.min).then_inc(sem("ml_max"), 1)
                dve.wait_ge(sem("ml_exp"), h + 1)
                for i in range(2):
                    o = full()
                    for d in range(2):
                        n = 2 * i + d
                        ins = ttr(out=TMP[:, n, :], in0=TMP[:, n, :], in1=o, scale=float(MLQK) ** -0.5, scalar=0.0, op0=ALU.mult, op1=ALU.add, accum_out=DEN[:, n:n + 1])
                    ins.then_inc(d_free, 1)
                dve.drain()
                stt(FLO[:, :], DEN[:, :], -1.0, FLO[:, :], ALU.mult, ALU.max)
                dve.drain()
                tt(DEN[:, :], DEN[:, :], FLO[:, :], ALU.max)
                dve.drain()
                nc.vector.reciprocal(RC[:, 8:12], DEN[:, :])
                dve.drain()
                for i in range(2):
                    ts(COMB[:, i, :], TMP[:, 2 * i, :], RC[:, 8 + 2 * i:9 + 2 * i], None, ALU.mult)
                dve.drain()
                for i in range(2):
                    stt(COMB[:, i, :], TMP[:, 2 * i + 1, :], RC[:, 9 + 2 * i:10 + 2 * i], COMB[:, i, :], ALU.mult, ALU.add).then_inc(sem("ml_p"), 1)
            dve.wait_ge(sem("gout_in"), 16)
            rsqrt_of_mean([(0, 8, VD)])
            for i in range(2):
                for h in range(HEADS):
                    e = slice(h * VD, (h + 1) * VD)
                    stt(HMT[:, i, e], HML[:, i, e], RS[:, 4 * i + h:4 * i + h + 1], GOUT[:, e], ALU.mult, ALU.mult)
            dve.drain()
            tt(HMT[:, :, :], HMT[:, :, :], OML[:, :, :], ALU.mult).then_inc(sem("hml_gated"), 1)
            for b in range(2):
                e = slice(b * 512, (b + 1) * 512)
                for i in range(2):
                    o = full()
                    tt(MTMP[:, i, :], o, MODB[:, 0, e], ALU.mult).then_inc(d_free, 1)
                    dve.drain()
                    ins = tt(X[:, i, e], X[:, i, e], MTMP[:, i, :], ALU.add)
            ins.then_inc(sem("x_ready"), 1)
            rsqrt_of_mean([(0, 2, D)])
            for i in range(2):
                stt(H2[:, i, :], X[:, i, :], RS[:, i:i + 1], MODB[:, 2, :], ALU.mult, ALU.mult)
                dve.drain()
                tt(H2[:, i, :], H2[:, i, :], MODB[:, 1, :], ALU.add).then_inc(sem("h2_ready"), 1)

            def top16(values, best, index, rest, n):
                for k in range(n):
                    nc.vector.max(best[:, k, 0:8], values[:, k, :])
                dve.drain()
                for k in range(n):
                    nc.vector.max_index(index[:, k, 0:8], best[:, k, 0:8], values[:, k, :])
                    nc.vector.match_replace(out=rest[:, k, :], in_to_replace=best[:, k, 0:8], in_values=values[:, k, :], imm_value=-3e38)
                dve.drain()
                for k in range(n):
                    nc.vector.max(best[:, k, 8:16], rest[:, k, :])
                dve.drain()
                for k in range(n):
                    nc.vector.max_index(index[:, k, 8:16], best[:, k, 8:16], rest[:, k, :])
                dve.drain()

            for i in range(2):
                dve.wait_ge(a_free, at["sc"][i])
                top16(SC[:, i, :, :], SV, SIU, SCR, 16)
                copy(SIF[:, :, :], SIU[:, :, :])
                sv = SV.rearrange("p (h w) k -> p h w k", w=2)
                sf = SIF.rearrange("p (h w) k -> p h w k", w=2)
                full4 = [P, PH, TOPK, TOPK]
                tt(CAND.rearrange("p h (x y) -> p h x y", x=TOPK), bcast(sv[:, :, 0, :], 3, full4), bcast(sv[:, :, 1, :], 2, full4), ALU.add)
                dve.drain()
                top16(CAND, BEST, POSU, CANDR, PH)
                ts(PA, POSU, 4, None, ALU.logical_shift_right)
                dve.drain()
                copy(POSF[:, 0, :, :], PA)
                dve.drain()
                ts(PA, POSU, TOPK - 1, None, ALU.bitwise_and)
                dve.drain()
                copy(POSF[:, 1, :, :], PA)
                dve.drain()
                for w in range(2):
                    tt(EQ[:, :, :, :], bcast(POSF[:, w, :, :], 3, full4), iota.unsqueeze(1).unsqueeze(1).to_broadcast(full4), ALU.is_equal)
                    dve.drain()
                    tt(EQ[:, :, :, :], EQ[:, :, :, :], bcast(sf[:, :, w, :], 2, full4), ALU.mult)
                    dve.drain()
                    nc.vector.tensor_reduce(SEL[:, w, :, :], EQ[:, :, :, :], AX.X, ALU.add)
                    dve.drain()
                stt(EIDX[:, i, :].rearrange("p (h k) -> p h k", h=PH), SEL[:, 0, :, :], float(NKEYS), SEL[:, 1, :, :], ALU.mult, ALU.add).then_inc(sem("eidx"), 1)
                gw = GW[:, i, :].rearrange("p (h k) -> p h k", h=PH)
                tt(gw, BEST[:, :, :], BEST[:, :, 0:1].to_broadcast([P, PH, TOPK]), ALU.subtract).then_inc(sem("best_ready"), 1)
                dve.wait_ge(sem("best_exp"), i + 1)
                nc.vector.tensor_reduce(SUM8[:, :], gw, AX.X, ALU.add)
                dve.drain()
                nc.vector.reciprocal(SUM8[:, :], SUM8[:, :])
                dve.drain()
                tt(gw, gw, bcast(SUM8[:, :], 2, [P, PH, TOPK]), ALU.mult)
            for i in range(2):
                for m in range(PICKS):
                    g = i * PICKS + m
                    dve.wait_ge(sem(f"row{g % NG}"), 16 * (g // NG + 1))
                    dve.drain()
                    ttr(out=PROD, in0=GROWS[g % NG], in1=H2[:, i, :], scale=1.0, scalar=0.0, op0=ALU.mult, op1=ALU.add,
                        accum_out=DOT[:, i, m:m + 1]).then_inc(sem("u_used"), 1)
                dve.wait_ge(sem("gelu_done"), i + 1)
                tt(GW[:, i, :], GW[:, i, :], DOT[:, i, :], ALU.mult).then_inc(sem("gw_ready"), 1)
            for i in range(2):
                for h in range(2):
                    e = slice(h * 512, (h + 1) * 512)
                    o = full()
                    tt(HP2[:, h, :], o, MODB[:, 3, e], ALU.mult).then_inc(d_free, 1)
                    dve.drain()
                    ins = tt(X[:, i, e], X[:, i, e], HP2[:, h, :], ALU.add)
            ins.then_inc(sem("x_ready"), 1)
            for L in range(DEPTH):
                m = at["L"][L]

                def pre_norm():
                    rsqrt_of_mean([(0, 2, D)])
                    for i in range(2):
                        stt(HN2[:, i, :], X[:, i, :], RS[:, i:i + 1], NW[:, 0, :], ALU.mult, ALU.mult).then_inc(sem("hn2_ready"), 1)

                def post_norm():
                    rsqrt_of_mean([(0, 2, D)])
                    for i in range(2):
                        stt(MO[:, i, :], MO[:, i, :], RS[:, i:i + 1], NW[:, 1, :], ALU.mult, ALU.mult)
                    dve.drain()
                    tt(X[:, :, :], X[:, :, :], MO[:, :, :], ALU.add).then_inc(sem("x_ready"), 1)

                dve.wait_ge(sem("nw_in0"), 16 * (2 * L + 1))
                dve.wait_ge(sem("nw_in1"), 16 * (2 * L + 1))
                pre_norm()
                for wh in range(2):
                    for i in range(2):
                        o = full().rearrange("p (h f e) -> p h f e", h=AH, f=2)
                        r = RTMP[:, i, :].rearrange("p (h f e) -> p h f e", h=AH, f=2)
                        q = QKR[:, wh, i, :]
                        sin = rope2[:, 1, i, :].rearrange("p (f e) -> p f e", f=2)
                        for f in range(2):
                            tt(r[:, :, f, :], o[:, :, 1 - f, :], bcast(sin[:, f, :], 1, [P, AH, AD // 2]), ALU.mult)
                        tt(q.rearrange("p (h e) -> p h e", h=AH), o.rearrange("p h f e -> p h (f e)"), bcast(rope2[:, 0, i, :], 1, [P, AH, AD]), ALU.mult).then_inc(d_free, 1)
                        dve.drain()
                        ins = tt(q, q, RTMP[:, i, :], ALU.add)
                ins.then_inc(sem("rot2"), 1)
                for g in range(6):
                    o = full()
                    dve.wait_ge(sem("cv_tap"), 6 * L + g + 1)
                    for s in range(1, 4):
                        for f in range(2):
                            y = CV[:, 2 * g + f, s:SEQ]
                            ins = stt(y, o[:, f * SEQ:(f + 1) * SEQ - s], CW2[:, L, 2 * g + f, 3 - s:4 - s], y, ALU.mult, ALU.add)
                        if s < 3:
                            dve.drain()
                    ins.then_inc(d_free, 1)
                dve.wait_ge(a_free, m["ba"])
                tt(ST1[:, :, :], ST1[:, :, :], bcast(AB2[:, L, 4:8], 1, [P, 2, 4]), ALU.add).then_inc(sem("sp_in"), 1)
                dve.wait_ge(sem("sp_exp"), L + 1)
                ts(ST2[:, :, :], ST2[:, :, :], 1.0, None, ALU.add).then_inc(sem("sp_plus1"), 1)
                ts(ST1[:, :, :], ST1[:, :, :], 0.0, None, ALU.max)
                dve.wait_ge(sem("sp_ln"), L + 1)
                dve.drain()
                tt(ST1[:, :, :], ST1[:, :, :], ST2[:, :, :], ALU.add)
                dve.drain()
                stt(GT[:, :, :], ST1[:, :, :], -1.0, bcast(AE[:, :], 1, [P, 2, 4]), ALU.mult, ALU.mult).then_inc(sem("g_ready"), 1)
                for u in range(18):
                    if u < 16:
                        o = full()
                        i = u % 2
                        w = (i + 1) * P
                        mask = v(DILM + i * P, w)
                        ttr(out=ETMP[:, i, 0:w], in0=o[:, 0:w], in1=mask, scale=float(AD) ** -0.5, scalar=-3e38, op0=ALU.add, op1=ALU.max,
                            accum_out=MN[:, u:u + 1]).then_inc(d_free, 1)
                        dve.drain()
                        ts(MX[:, u:u + 1], MN[:, u:u + 1], -1.0, None, ALU.mult).then_inc(sem("at_max"), 1)
                    if 1 <= u <= 16:
                        w = ((u - 1) % 2 + 1) * P
                        dve.wait_ge(sem("at_exp"), 16 * L + u)
                        nc.vector.reciprocal(RC[:, u - 1:u], SM[:, u - 1:u])
                        dve.drain()
                        ts(ETMP[:, (u - 1) % 2, 0:w], ETMP[:, (u - 1) % 2, 0:w], RC[:, u - 1:u], None, ALU.mult).then_inc(sem("at_p"), 1)
                    if u >= 5 and u % 4 == 1:
                        o = full()
                        copy(MIX2[:, (u - 5) // 4, :], o[:, 0:SEQ]).then_inc(d_free, 1)
                c["norm"] += 1
                dve.wait_ge(sem("ss_ready"), c["norm"])
                ts(MS[:, 0:16], SS[:, 0:16], EPS, None, ALU.add).then_inc(sem("ms_ready"), 1)
                for i in range(2):
                    for h in range(DH):
                        e = TQ[:, 2, i, h * P:(h + 1) * P]
                        ins = ts(e, e, BT[:, i, h:h + 1], None, ALU.mult)
                ins.then_inc(sem("vb_ready"), 1)
                dve.wait_ge(sem("rs_ready"), c["norm"])
                for wh in range(2):
                    for i in range(2):
                        for h in range(DH):
                            e = TQ[:, wh, i, h * P:(h + 1) * P]
                            n = wh * 8 + i * 4 + h
                            ins = ts(e, e, RS[:, n:n + 1], float(P) ** -0.5 if wh == 0 else 1.0, ALU.mult, ALU.mult)
                    ins.then_inc(sem("dn_normed"), 1)
                for T in (TI, TU):
                    ins = copy(T[:, :, :], bcast(ident, 1, [P, 8, P]))
                ins.then_inc(sem("t_init"), 1)
                o = full()
                copy(GC[:, :, :], o[:, 0:8].rearrange("p (i h) -> p i h", i=2)).then_inc(d_free, 1)
                dve.drain()
                for g in range(2):
                    o = full().rearrange("p (h i j) -> p h i j", h=2, i=2)
                    for hh in range(2):
                        h = 2 * g + hh
                        stt(DEC[:, h, 0, :], o[:, hh, 0, :], GC[:, 0, h:h + 1], v(DECM, P), ALU.subtract, ALU.add)
                        ts(DEC[:, h, 1, :], o[:, hh, 0, :], GC[:, 1, h:h + 1], None, ALU.subtract)
                        ins = stt(DEC[:, h, 2, :], o[:, hh, 1, :], GC[:, 1, h:h + 1], v(DECM, P), ALU.subtract, ALU.add)
                    ins.then_inc(d_free, 1)
                dve.drain().then_inc(sem("dec_in"), 1)
                dve.wait_ge(sem("dec_exp"), L + 1)
                for seg in range(3):
                    o = full()
                    tt(QKD[:, :, seg, :], o.rearrange("p (h j) -> p h j", h=4), DEC[:, :, seg, :], ALU.mult).then_inc(d_free, 1)
                for seg in range(3):
                    o = full()
                    for h in range(DH):
                        ins = stt(AA[:, h, seg, :], o[:, h * P:(h + 1) * P], BT[:, (seg + 1) // 2, h:h + 1], DEC[:, h, seg, :], ALU.mult, ALU.mult)
                    ins.then_inc(d_free, 1)
                dve.drain().then_inc(sem("aa_ready"), 1)
                for lv in range(7):
                    for half in range(2):
                        s = slice(4 * half, 4 * half + 4)
                        for T in ((TI, TU) if lv < 6 else (TU,)):
                            o = full()
                            tt(T[:, s, :], T[:, s, :], o.rearrange("p (h j) -> p h j", h=4), ALU.subtract).then_inc(d_free, 1)
                    if lv < 6:
                        dve.drain()
                o = full()
                copy(UU[:, 0, :], o).then_inc(d_free, 1)
                o = full()
                tt(TQ[:, 2, 1, :], TQ[:, 2, 1, :], o, ALU.subtract).then_inc(d_free, 1)
                o = full()
                copy(UU[:, 1, :], o).then_inc(d_free, 1)
                dve.wait_ge(sem("dnw_in"), 16)
                rsqrt_of_mean([(0, 8, P)])
                for i in range(2):
                    for h in range(DH):
                        e = slice(h * P, (h + 1) * P)
                        stt(TQ[:, 0, i, e], TQ[:, 1, i, e], RS[:, 4 * i + h:4 * i + h + 1], DNW[:, L, :], ALU.mult, ALU.mult)
                dve.drain()
                tt(TQ[:, 0, :, :], TQ[:, 0, :, :], Z2[:, :, :], ALU.mult).then_inc(sem("do_gated"), 1)
                for b in range(2):
                    for i in range(2):
                        o = full()
                        copy(MO[:, i, b * 512:(b + 1) * 512], o).then_inc(d_free, 1)
                post_norm()
                dve.wait_ge(sem("nw_in0"), 16 * (2 * L + 2))
                dve.wait_ge(sem("nw_in1"), 16 * (2 * L + 2))
                pre_norm()
                for n in range(2 * FBLK + 1):
                    N = 2 * FBLK * L + n
                    if n < 2 * FBLK:
                        o = full()
                        dve.wait_ge(sem("ffn_tap"), N + 1)
                        for s in range(1, 3):
                            for wh in range(2):
                                f = wh * DFF // P + n
                                y = YG[:, n % 4, wh, s:SEQ]
                                ins = stt(y, o[:, wh * SEQ:(wh + 1) * SEQ - s], FW2[:, L, f, 2 - s:3 - s], y, ALU.mult, ALU.add)
                            if s == 1:
                                dve.drain()
                        ins.then_inc(d_free, 1)
                    if n >= 1:
                        dve.wait_ge(sem("ffn_gelu"), N)
                        q = n - 1
                        tt(GU[:, q // 2 % 2, q % 2, :], YG[:, q % 4, 0, :], YG[:, q % 4, 1, :], ALU.mult).then_inc(sem("gu_ready"), 1)
                post_norm()



def kernel(**inputs):
    import concourse.bacc as _bacc
    from concourse.bass_utils import run_bass_kernel_spmd as _run

    def col(x):
        x = np.asarray(x)
        x = x.reshape(x.shape[:-1] + (x.shape[-1] // P, P))
        return np.ascontiguousarray(np.moveaxis(x, -1, 0))

    i = {k: np.ascontiguousarray(x) for k, x in inputs.items()}
    arrays = {k: i[k] for k in ("x", "ctx", "w_ada", "b_ada", "g_norm1", "g_norm2", "w_in", "g_cq", "g_ckv", "g_qn", "g_kn",
                                "w_uq", "w_ukv", "w_out", "w_pq", "g_mlstm", "w_in_2", "w_out_2", "ffn_w_in_2", "ffn_w_out_2")}
    for k in ("pre_mix", "post_mix", "pre_ffn", "post_ffn"):
        arrays[f"norm_{k}_2"] = i[f"norm_{k}_2"]
    arrays["expert_u"] = i["expert_u"][0]
    arrays["expert_v"] = i["expert_v"][0]
    arrays["cc"] = np.ascontiguousarray(np.stack([col(i["c"][0]), col(i["c_ctx"])], -1).reshape(P, 2 * KT))
    arrays["sub_keys_T"] = np.ascontiguousarray(i["sub_keys"][0].transpose(3, 0, 1, 2).reshape(P, 2 * PH * NKEYS))
    arrays["conv1"] = np.ascontiguousarray(col(i["conv_qk"][0]).transpose(0, 2, 1).reshape(P, 12))
    arrays["gate_bias"] = np.concatenate([i["b_igate"].reshape(1, 8), i["b_fgate"].reshape(1, 8)], 1)
    arrays["conv2"] = np.ascontiguousarray(col(i["dn_conv_w_2"]).transpose(0, 1, 3, 2).reshape(P, DEPTH * 48))
    arrays["ffn_conv"] = np.ascontiguousarray(col(i["ffn_conv_w_2"]).transpose(0, 1, 3, 2).reshape(P, DEPTH * 132))
    arrays["ffn_bias"] = np.ascontiguousarray(col(i["ffn_conv_b_2"]).reshape(P, DEPTH * 44))
    arrays["decay"] = np.stack([i["dn_a_log_2"], i["dn_dt_bias_2"]], 1).reshape(1, DEPTH * 8)
    arrays["dn_norm"] = i["dn_norm_w_2"].reshape(1, DEPTH * P)
    arrays["consts"] = constants()
    arrays["mmask"] = mlstm_masks()

    nc = _bacc.Bacc("TRN2", target_bir_lowering=False, num_devices=1)
    aps = {k: nc.dram_tensor(f"in_{k}", x.shape, mybir.dt.from_np(x.dtype), kind="ExternalInput").ap() for k, x in arrays.items()}
    out = nc.dram_tensor("out_0", (1, SEQ, D), F32, kind="ExternalOutput").ap()
    program(nc, aps, out)
    r = _run(nc, [{f"in_{k}": x for k, x in arrays.items()}], core_ids=[0])
    return r.results[0]["out_0"]
```

```python
from contextlib import ExitStack

import numpy as np

import concourse.bass as bass
from concourse import mybir

F32 = mybir.dt.float32
U32 = mybir.dt.uint32
ALU = mybir.AluOpType
ACT = mybir.ActivationFunctionType
AX = mybir.AxisListType

P = 128
D = 1024
KT = D // P
SEQ, CTX = 256, 256
ALL = SEQ + CTX
EPS = 1e-6
NEG = -1e30

QR, KVR, ROPE, NOPE, VD, HEADS = 256, 128, 64, 128, 128, 4
QK = NOPE + ROPE
MLQK = 64
MLA_COLS = QR + KVR + ROPE
PH, NKEYS, TOPK = 8, 128, 16
PICKS = PH * TOPK
DEPTH = 2
AH, AD = 8, 64
DH = 4
DFF = 2816
FBLK = DFF // 256

WSLOTS = 4
WCOLS = 520
SLOT = KT * WCOLS

IDENT = 0
TRI = IDENT + P
ONES = TRI + 4 * P
LEVEL = ONES + 2 * P
DECM = LEVEL + 7 * P
DILM = DECM + P
ROPE1 = DILM + 3 * P
ROPE2 = ROPE1 + 4 * ROPE
IOTA = ROPE2 + 4 * AD
NCONST = IOTA + TOPK
BASE = NCONST


def constants():
    f = np.float32
    r = np.arange(P)
    out = np.zeros((P, NCONST), f)
    out[:, IDENT:IDENT + P] = np.eye(P)
    le = (r[:, None] <= r[None, :]).astype(f)
    tri = [le, -(1 - le), (r[:, None] >= r[None, :]).astype(f), -(r[:, None] < r[None, :]).astype(f)]
    for n, m in enumerate(tri):
        out[:, TRI + n * P:TRI + (n + 1) * P] = m
    out[:, ONES:ONES + P] = 1.0
    out[:, ONES + P:ONES + 2 * P] = -1.0
    for n in range(7):
        b = 1 << n
        m = (r[None, :] // (2 * b) == r[:, None] // (2 * b)) & (r[None, :] // b % 2 == 1) & (r[:, None] // b % 2 == 0)
        out[:, LEVEL + n * P:LEVEL + (n + 1) * P] = m
    out[:, DECM:DECM + P] = np.where(r[None, :] > r[:, None], f(1e30), f(0))
    t = np.arange(SEQ)
    diff = t[:, None] - t[None, :]
    count = np.zeros((SEQ, SEQ))
    for window, dil in ((128, 1), (512, 4), (2048, 16)):
        count += (diff >= 0) & (diff <= window) & (diff % dil == 0)
    m = np.where(count > 0, 8.0 * np.log(np.maximum(count, 1)), NEG).astype(f)
    out[:, DILM:DILM + P] = m[:P, :P]
    out[:, DILM + P:DILM + 3 * P] = m[P:, :]
    half = ROPE // 4
    inv = (f(10000.0) ** (-np.arange(half, dtype=f) * f(2.0 / (ROPE // 2)))).astype(f)
    row, col = (t // 64).astype(f), (t % 64).astype(f)
    ar, ac = row[:, None] * inv, col[:, None] * inv
    cos = np.concatenate([np.cos(ar), np.cos(ar), np.cos(ac), np.cos(ac)], 1)
    sin = np.concatenate([-np.sin(ar), np.sin(ar), -np.sin(ac), np.sin(ac)], 1)
    inv2 = (f(1.0) / (f(10000.0) ** (np.arange(0, AD, 2, dtype=f) / f(AD)))).astype(f)
    a2 = t.astype(f)[:, None] * inv2[None, :]
    cos2 = np.concatenate([np.cos(a2), np.cos(a2)], 1)
    sin2 = np.concatenate([-np.sin(a2), np.sin(a2)], 1)
    for at, table in ((ROPE1, cos), (ROPE1 + 2 * ROPE, sin), (ROPE2, cos2), (ROPE2 + 2 * AD, sin2)):
        out[:, at:at + 2 * ROPE] = table.reshape(2, P, ROPE).transpose(1, 0, 2).reshape(P, 2 * ROPE)
    out[:, IOTA:IOTA + TOPK] = np.arange(TOPK)
    return out


def mlstm_masks():
    t = np.arange(SEQ)
    out = np.zeros((P, 2, 2, ALL), np.float32)
    for i in range(2):
        q = t[i * P:(i + 1) * P]
        out[:, i, 0, CTX:] = np.where(t[None, :] > q[:, None], NEG, 0)
        out[:, i, 1, CTX:] = np.where(t[None, :] < q[:, None], NEG, 0)
    return out.reshape(P, 4 * ALL)


def program(nc, a, out):
    with ExitStack() as ctx:
        sems = {}

        def sem(name):
            if name not in sems:
                sems[name] = ctx.enter_context(nc.semaphore(name))
            return sems[name]

        X = ctx.enter_context(nc.sbuf_tensor("residual", [P, 2, D], F32))
        XT = ctx.enter_context(nc.sbuf_tensor("activations_T", [P, KT * ALL], F32))
        RING = ctx.enter_context(nc.sbuf_tensor("weight_ring", [P, WSLOTS, SLOT], F32))
        SMALL = ctx.enter_context(nc.sbuf_tensor("small", [P, 1280], F32))
        IDX = ctx.enter_context(nc.sbuf_tensor("indices", [P, 3, 256], U32))
        AR_N = (nc.sbuf_bytes_remaining - 512) // 4
        AR = ctx.enter_context(nc.sbuf_tensor("arena", [P, AR_N], F32))
        PS = ctx.enter_context(nc.psum_tensor("psum", [P, 8, 512], F32))

        def v(at, *dims, of=AR, parts=P):
            n = int(np.prod(dims))
            assert at + n <= of.shape[-1], (at, dims)
            ap = of[0:parts, at:at + n]
            names = "abcd"[:len(dims)]
            if len(dims) == 1:
                return ap
            return ap.rearrange(f"p ({' '.join(names)}) -> p {' '.join(names)}", **dict(zip(names[1:], dims[1:])))

        small_at = [0]

        def small(*dims):
            n = int(np.prod(dims))
            small_at[0] += n
            assert small_at[0] <= 1280
            return v(small_at[0] - n, *dims, of=SMALL)

        ident = v(IDENT, P)
        tri = v(TRI, 4, P)
        ones = v(ONES, 2, P)
        level = v(LEVEL, 7, P)
        rope1 = v(ROPE1, 2, 2, ROPE)
        rope2 = v(ROPE2, 2, 2, AD)
        iota = v(IOTA, TOPK)

        MODA = v(BASE, 4, D)
        MODB = v(BASE + 4096, 4, D)
        R3, R4 = BASE + 8192, BASE + 10240
        R5 = BASE + 12288
        R6 = R5 + 4416
        R7 = R6 + 3072
        R8 = R7 + 2048
        R9 = R8 + 1536
        XC = v(R3, 2, D)
        GN = v(R4, D)
        G2 = v(R8, D)
        KEYS = v(R9, 16, NKEYS)
        HN = v(R7, 2, D)
        XTv = XT[:, :].rearrange("p (k t) -> p k t", k=KT)
        CQKV = v(R5, 4, MLA_COLS)
        OML = v(R5 + 1792, 2, 512)
        GATE = v(R5 + 2816, 4, 16)
        CN = v(R5 + 2880, 1024)
        GOUT = v(R5 + 3904, 512)
        VML = v(R9, 4, 512)
        QF = v(R8, 2, SEQ)
        KF = v(R8 + 512, 2, ALL)
        CNT = v(R7, 1024)
        QM = v(0, 2, HEADS, QK, of=XT)
        KM = v(R6, 4, HEADS, QK)
        VM = v(R3, 4, HEADS, VD)
        QTN = v(1536, HEADS, SEQ, of=XT)
        QTR = v(2560, HEADS, SEQ, of=XT, parts=ROPE)
        KTN = v(BASE, HEADS, ALL)
        KTR = v(BASE + 2048, HEADS, ALL, parts=ROPE)
        MIXT = v(R4, KT, SEQ)
        GAIN = v(R4 + 1024, 768)
        JUNK = v(R4 + 1792, 256)
        SWAP = v(R7 + 1024, 2, HEADS, ROPE)
        EXPS = v(R7, 2, 512)
        PT = v(R7 + 1024, 2, 4, P)
        MMASK = v(R6, 4, ALL)
        TMP = [v(R5 + n * ALL, ALL) for n in range(3)] + [v(0, ALL, of=XT)]
        COMB = v(R5 + 2880, 2, ALL)
        HML = v(R6 + 2048, 2, 512)
        MLPT = v(512, 2, 4, P, of=XT)
        HMT = v(R3 + 1024, 2, 512)
        MTMP = v(R7, 2, 512)
        H2 = v(BASE, 2, D)
        CANDR = v(BASE + 2048, PH, 256)
        SC = v(BASE + 8192, 2, 16, NKEYS)
        SCR = v(BASE + 12288, 16, NKEYS)
        CAND = v(BASE + 14336, PH, 256)
        EQ = v(BASE + 16384, PH, TOPK, TOPK)
        PX = BASE + 18432
        PQT = v(PX, 16, SEQ)
        GROWS = [v(PX + n * D, D) for n in range((AR_N - PX) // D)] + [v(BASE + 4096 + n * D, D) for n in range(3)]
        NG = len(GROWS)
        PROD = v(BASE + 8192, D)
        ACC = v(BASE + 9216, D)
        DIAG = v(PX + (AR_N - PX) // D * D, 4, P)
        EIDX = IDX[:, 0, :].rearrange("p (i m) -> p i m", i=2)
        XTP = v(0, KT, SEQ, of=XT)
        NW = v(BASE, 2, D)
        HN2 = v(BASE + 2048, 2, D)
        MIX2 = v(BASE + 2048, KT, SEQ)
        V2 = v(BASE + 4096, 2, 512)
        Z2 = v(BASE + 5120, 2, 512)
        CV = v(BASE + 6144, 12, SEQ)
        DQF = v(BASE + 6144, 4, SEQ)
        DKF = v(BASE + 7168, 4, SEQ)
        UU = v(BASE + 8192, 2, 512)
        TQ = v(BASE + 9216, 3, 2, 512)
        C0 = BASE + 12288
        QKR = v(C0, 2, 2, 512)
        RTMP = v(C0 + 2048, 2, 512)
        TI = v(C0, 8, P)
        TU = v(C0 + 1024, 8, P)
        TW = v(C0 + 2048, 8, P)
        QKT2 = v(C0 + 3072, 2, 4, SEQ)
        MO1 = v(0, 2, D, of=XT)
        AM = v(C0 + 3072, 2, 8, P)
        DEC = v(C0 + 5120, 4, 3, P)
        QKD = v(C0 + 6656, 4, 3, P)
        AA = v(C0 + 8192, 4, 3, P)
        AT = v(C0 + 9728, 3, 4, P)
        ETMP = v(C0 + 11264, 2, 3, P)
        EPT = v(C0 + 12032, 2, 3, P)
        QKDT = v(2048, 4, 3, P, of=XT)
        WO2 = v(BASE + 6144, 2, 2, D)
        MO = v(C0, 2, D)
        YSQ = v(C0 + 3072, D)
        YG = v(C0, 4, 2, SEQ)
        GU = v(C0 + 2048, 2, 2, SEQ)
        assert C0 + 12800 <= AR_N

        SS, MS, RS, HALF, MX, SM, RC, MN = (small(32) for _ in range(8))
        SILC = small(KT, 2)
        CCOL = small(KT, 2)
        CONVW = small(4, 3)
        GB = small(16)
        LF, LT1, LT2, FCOL, BCOL, IG = (small(4, 8) for _ in range(6))
        FLO, DEN = small(4), small(4)
        CW2 = small(DEPTH, 12, 4)
        FW2 = small(DEPTH, 2 * DFF // P, 3)
        FB2 = small(DEPTH, 2 * DFF // P)
        AB2 = small(DEPTH, 8)
        AE, GT, BT, GC, ST1, ST2 = small(4), *(small(2, 4) for _ in range(5))
        SV = v(2048, 16, TOPK, of=XT)
        SIF = v(2304, 16, TOPK, of=XT)
        BEST = v(2560, PH, TOPK, of=XT)
        POSF = v(2688, 2, PH, TOPK, of=XT)
        SEL = v(2944, 2, PH, TOPK, of=XT)
        GW = v(3200, 2, PICKS, of=XT)
        DOT = v(3456, 2, PICKS, of=XT)
        SUM8 = v(3712, PH, of=XT)
        DNW = v(3728, DEPTH, P, of=XT)
        SIU = IDX[:, 1, :].rearrange("p (c k) -> p c k", c=16)
        POSU = IDX[:, 2, 0:128].rearrange("p (c k) -> p c k", c=PH)
        PA = IDX[:, 2, 128:256].rearrange("p (c k) -> p c k", c=PH)

        def cols(w, lo, hi):
            return w.rearrange("(k p) n -> p k n", p=P)[:, :, lo:hi]

        def slot8(n, width):
            return RING[:, n % WSLOTS, 0:KT * width].rearrange("p (k n) -> p k n", k=KT)

        loads = []
        def ada_loads(lo, hi):
            for b in range(lo, hi):
                loads.append(lambda n, b=b: [(slot8(n, 512), cols(a["w_ada"][0], b * 512, b * 512 + 512))])

        ada_loads(0, 6)
        loads.append(lambda n: [(slot8(n, 464)[:, :, 0:448], cols(a["w_in"][0], 0, 448)),
                                (slot8(n, 464)[:, :, 448:464], cols(a["w_in"][0], 1984, 2000))])
        for lo in (448, 960, 1472):
            loads.append(lambda n, lo=lo: [(slot8(n, 512), cols(a["w_in"][0], lo, lo + 512))])
        ada_loads(6, 8)
        loads.append(lambda n: [
            (RING[:, n % WSLOTS, 0:1536].rearrange("p (k n) -> p k n", k=2), a["w_uq"][0].rearrange("(k p) n -> p k n", p=P)),
            (RING[:, n % WSLOTS, 1536:2560], a["w_ukv"][0])])
        ada_loads(8, 12)
        for b in range(2):
            loads.append(lambda n, b=b: [(slot8(n, 512), cols(a["w_out"][0], b * 512, b * 512 + 512))])
        for b in range(4):
            loads.append(lambda n, b=b: [(slot8(n, 512), cols(a["w_pq"][0], b * 512, b * 512 + 512))])
        ATT_STEPS = AH + 2
        WIN2 = [(0, 512), (512, 1024), (1024, 1536), (1536, 2048), (2048, 2560), (2560, 3072), (3072, 3592)]
        for L in range(DEPTH):
            for lo, hi in WIN2:
                loads.append(lambda n, L=L, lo=lo, hi=hi: [(slot8(n, hi - lo), cols(a["w_in_2"][L], lo, hi))])
            for b in range(2):
                loads.append(lambda n, L=L, b=b: [(slot8(n, 512), cols(a["w_out_2"][L], b * 512, b * 512 + 512))])
            for b in range(FBLK):
                loads.append(lambda n, L=L, b=b: [
                    (slot8(n, 512)[:, :, 0:256], cols(a["ffn_w_in_2"][L], b * 256, b * 256 + 256)),
                    (slot8(n, 512)[:, :, 256:512], cols(a["ffn_w_in_2"][L], DFF + b * 256, DFF + b * 256 + 256))])
        landed, count = [], [0] * WSLOTS
        for n, fn in enumerate(loads):
            count[n % WSLOTS] += 16 * len(fn(n))
            landed.append(count[n % WSLOTS])
        last_read = {}
        at = {}

        d_full, d_free, a_full, a_free = sem("d_full"), sem("d_free"), sem("a_full"), sem("a_free")
        block = ctx.enter_context(nc.Block())

        def on_dve(m):
            return m % 4 == 3

        def used(g):
            i, which, m = g // (2 * PICKS), g // PICKS % 2, g % PICKS
            if which == 0:
                return sem("u_used"), i * PICKS + m + 1
            if on_dve(m):
                return sem("v_added"), i * PICKS // 4 + m // 4 + 1
            return sem("v_used"), i * PICKS * 3 // 4 + m - m // 4 + 1

        @block.tensor
        def _(pe):
            mm, turn = nc.tensor.matmul, nc.tensor.transpose
            c = {"d": 0, "a": 0, "w": 0}

            def bank_d():
                c["d"] += 1
                if c["d"] > 4:
                    pe.wait_ge(d_free, c["d"] - 4)
                return PS[:, (c["d"] - 1) % 4, :]

            def bank_a():
                c["a"] += 1
                if c["a"] > 4:
                    pe.wait_ge(a_free, c["a"] - 4)
                return PS[:, 4 + (c["a"] - 1) % 4, :]

            def weights(width=None):
                n = c["w"]
                c["w"] += 1
                pe.wait_ge(sem(f"w_in{n % WSLOTS}"), landed[n])
                return RING[:, n % WSLOTS, :] if width is None else slot8(n, width)

            def was_read(ring, back=0):
                last_read[c["w"] - 1 - back] = (ring, c[ring])

            pe.wait_ge(sem("silu_c"), 1)
            def modulation(lo, hi):
                for b in range(lo, hi):
                    w = weights(512)
                    for which in (0, 1) if b < 4 else (0,):
                        o = bank_d()
                        for k in range(KT):
                            ins = mm(o, SILC[:, k, which:which + 1].to_broadcast([P, P]), w[:, k, :], start=k == 0, stop=k == KT - 1)
                        ins.then_inc(d_full, 1)
                    was_read("d")

            modulation(0, 6)
            pe.wait_ge(sem("consts"), 16)
            for n in range(4):
                pe.wait_ge(sem("hn_ready"), n + 1)
                for h in range(2):
                    o = bank_a()
                    for q in range(4):
                        ins = turn(o[:, q * P:(q + 1) * P], HN[:, n % 2, (4 * h + q) * P:(4 * h + q + 1) * P], ident)
                    ins.then_inc(a_full, 1)
            pe.wait_ge(a_free, c["a"])
            w = weights(464)
            for j in (2, 3, 0, 1):
                lo = 0 if j >= 2 else QR
                o = bank_a()
                for k in range(KT):
                    ins = mm(o[:, lo:464], XTv[:, k, j * P:(j + 1) * P], w[:, k, lo:464], start=k == 0, stop=k == KT - 1)
                ins.then_inc(a_full, 1)
            was_read("a")
            at["cqkv"] = c["a"]
            w = weights(512)
            at["ml_qk"] = []
            for f in range(4):
                lo = CTX if f < 2 else 0
                o = bank_d()
                for k in range(KT):
                    ins = mm(o[:, 0:ALL - lo], w[:, k, f * P:(f + 1) * P], XTv[:, k, lo:ALL], start=k == 0, stop=k == KT - 1)
                ins.then_inc(d_full, 1)
                at["ml_qk"].append(c["d"])
            was_read("d")
            w = weights(512)
            for j in range(4):
                o = bank_a()
                for k in range(KT):
                    ins = mm(o, XTv[:, k, j * P:(j + 1) * P], w[:, k, :], start=k == 0, stop=k == KT - 1)
                ins.then_inc(a_full, 1)
            was_read("a")
            w = weights(512)
            for j in (2, 3):
                o = bank_a()
                for k in range(KT):
                    ins = mm(o, XTv[:, k, j * P:(j + 1) * P], w[:, k, :], start=k == 0, stop=k == KT - 1)
                ins.then_inc(a_full, 1)
            was_read("a")
            at["xt_read"] = c["a"]
            modulation(6, 8)
            pe.wait_ge(sem("cn_ready"), 1)
            o = bank_a()
            for i in range(2):
                for k in range(2):
                    ins = turn(o[:, (k * 2 + i) * P:(k * 2 + i + 1) * P], CN[:, i * QR + k * P:i * QR + (k + 1) * P], ident)
            ins.then_inc(a_full, 1)
            o = bank_a()
            for j in range(4):
                ins = turn(o[:, j * P:(j + 1) * P], CN[:, 512 + j * P:512 + (j + 1) * P], ident)
            ins.then_inc(a_full, 1)
            pe.wait_ge(a_free, c["a"])
            w = weights()
            uq = w[:, 0:1536].rearrange("p (k n) -> p k n", k=2)
            for i in range(2):
                for h in range(2):
                    o = bank_a()
                    for k in range(2):
                        ins = mm(o[:, 0:384], CNT[:, (k * 2 + i) * P:(k * 2 + i + 1) * P], uq[:, k, h * 384:h * 384 + 384], start=k == 0, stop=k == 1)
                    ins.then_inc(a_full, 1)
            at["qm"] = c["a"]
            for j in range(4):
                for h in range(2):
                    o = bank_d()
                    mm(o, CNT[:, 512 + j * P:512 + (j + 1) * P], w[:, 1536 + h * 512:2048 + h * 512], start=True, stop=True).then_inc(d_full, 1)
            was_read("d")
            modulation(8, 12)
            pe.wait_ge(sem("qk_roped"), 1)
            for hp in range(2):
                o, o2 = bank_d(), bank_a()
                for q in range(4):
                    ins = turn(o[:, q * P:(q + 1) * P], QM[:, q % 2, 2 * hp + q // 2, 0:NOPE], ident)
                ins.then_inc(d_full, 1)
                for q in range(4):
                    ins = turn(o2[0:ROPE, q * P:(q + 1) * P], QM[:, q % 2, 2 * hp + q // 2, NOPE:QK], ident)
                ins.then_inc(a_full, 1)
            for h in range(HEADS):
                o, o2 = bank_d(), bank_a()
                for j in range(4):
                    ins = turn(o[:, j * P:(j + 1) * P], KM[:, j, h, 0:NOPE], ident)
                ins.then_inc(d_full, 1)
                for j in range(4):
                    ins = turn(o2[0:ROPE, j * P:(j + 1) * P], KM[:, j, h, NOPE:QK], ident)
                ins.then_inc(a_full, 1)
            pe.wait_ge(d_free, c["d"])
            pe.wait_ge(a_free, c["a"])
            at["km_read_d"], at["km_read_a"] = c["d"], c["a"]
            units = [(h, i) for h in range(HEADS) for i in range(2)]
            at["mla_s"], mla_t, mla_step = [], [], iter(range(len(units) + 2))

            def mla():
                u = next(mla_step)
                if 1 <= u <= len(units):
                    pe.wait_ge(sem("mla_p"), u)
                    o = bank_a()
                    for s in range(4):
                        ins = turn(o[:, s * P:(s + 1) * P], EXPS[:, (u - 1) % 2, s * P:(s + 1) * P], ident)
                    ins.then_inc(a_full, 1)
                    mla_t.append(c["a"])
                if u < len(units):
                    h, i = units[u]
                    o = bank_a()
                    mm(o, QTN[:, h, i * P:(i + 1) * P], KTN[:, h, :], start=True, stop=False)
                    mm(o, QTR[:, h, i * P:(i + 1) * P], KTR[:, h, :], start=False, stop=True).then_inc(a_full, 1)
                    at["mla_s"].append(c["a"])
                if u >= 2:
                    h, i = units[u - 2]
                    pe.wait_ge(a_free, mla_t[u - 2])
                    o = bank_d()
                    for s in range(4):
                        ins = mm(o[:, 0:P], VM[:, s, h, :], PT[:, (u - 2) % 2, s, :], start=s == 0, stop=s == 3)
                    ins.then_inc(d_full, 1)

            pe.wait_ge(sem("lf_ready"), 1)
            o = bank_d()
            LE, NGT, GE, NLT = (tri[:, n, :] for n in range(4))
            ONE, NONE = ones[:, 0, :], ones[:, 1, :]
            sums = [[[(1, NONE), (0, NGT)], [(1, NGT)], [(2, LE)], [(2, ONE), (3, LE)]],
                    [[(0, NLT)], [(0, NONE), (1, NLT)], [(3, ONE), (2, GE)], [(3, GE)]]]
            for d in range(2):
                for j in range(4):
                    for n, (src, m) in enumerate(sums[d][j]):
                        ins = mm(o[:, j * 8 + d * 4:j * 8 + d * 4 + 4], m, LF[:, src, d * 4:d * 4 + 4], start=n == 0, stop=n == len(sums[d][j]) - 1)
            ins.then_inc(d_full, 1)
            mla()
            mla()
            pe.wait_ge(sem("bcol_ready"), 1)
            pe.wait_ge(sem("mconv"), 4)
            for h in range(HEADS):
                p0 = (h % 2) * MLQK
                for d in range(2):
                    o = bank_d()
                    for j in range(4):
                        ins = turn(o[:, j * P:(j + 1) * P], BCOL[:, j, d * 4 + h:d * 4 + h + 1].to_broadcast([P, P]), ident)
                    ins.then_inc(d_full, 1)
                mla()
                for i in range(2):
                    o = bank_d()
                    mm(o, QF[p0:p0 + MLQK, h // 2, i * P:(i + 1) * P], KF[p0:p0 + MLQK, h // 2, :], start=True, stop=True).then_inc(d_full, 1)
                mla()
                for i in range(2):
                    pe.wait_ge(sem("ml_p"), 2 * h + i + 1)
                    o = bank_a()
                    for s in range(4):
                        ins = turn(o[:, s * P:(s + 1) * P], COMB[:, i, s * P:(s + 1) * P], ident)
                    ins.then_inc(a_full, 1)
                pe.wait_ge(a_free, c["a"])
                o = bank_a()
                for i in range(2):
                    for s in range(4):
                        ins = mm(o[:, i * VD:(i + 1) * VD], MLPT[:, i, s, :], VML[:, s, h * VD:(h + 1) * VD], start=s == 0, stop=s == 3)
                ins.then_inc(a_full, 1)
            at["ml_qk_read"], at["ml_v_read"] = c["d"], c["a"]
            pe.wait_ge(d_free, c["d"])
            wout = [weights(512), weights(512)]
            outputs = [(bank_d(), i, wout[b]) for b in range(2) for i in range(2)]
            for o, i, w in outputs:
                for k in range(4):
                    mm(o, MIXT[:, k, i * P:(i + 1) * P], w[:, k, :], start=k == 0, stop=False)
            pe.wait_ge(sem("hml_gated"), 1)
            for h in range(2):
                o = bank_a()
                for q in range(4):
                    hd = 2 * h + q // 2
                    ins = turn(o[:, q * P:(q + 1) * P], HMT[:, q % 2, hd * VD:(hd + 1) * VD], ident)
                ins.then_inc(a_full, 1)
            pe.wait_ge(a_free, c["a"])
            for o, i, w in outputs:
                for k in range(4, KT):
                    ins = mm(o, MIXT[:, k, i * P:(i + 1) * P], w[:, k, :], start=False, stop=k == KT - 1)
                ins.then_inc(d_full, 1)
            was_read("d", 1)
            was_read("d")
            for i in range(2):
                pe.wait_ge(sem("h2_ready"), i + 1)
                for h in range(2):
                    o = bank_a()
                    for q in range(4):
                        ins = turn(o[:, q * P:(q + 1) * P], H2[:, i, (4 * h + q) * P:(4 * h + q + 1) * P], ident)
                    ins.then_inc(a_full, 1)
            pe.wait_ge(a_free, c["a"])
            at["sc"], at["pqt"] = [], []
            for b in range(5):
                if b < 4:
                    w = weights(512)
                    for g in range(2):
                        o = bank_a()
                        for f in (2 * g, 2 * g + 1):
                            for k in range(KT):
                                ins = mm(o[:, (f % 2) * SEQ:(f % 2 + 1) * SEQ], w[:, k, f * P:(f + 1) * P], XTP[:, k, :], start=k == 0, stop=k == KT - 1)
                        ins.then_inc(a_full, 1)
                    was_read("a")
                    at["pqt"].append(c["a"])
                if b == 1:
                    pe.wait_ge(sem("keys_in"), 16)
                if b >= 1:
                    pe.wait_ge(a_free, at["pqt"][b - 1])
                    for i in range(2):
                        o = bank_a()
                        for q in range(4):
                            n = 4 * (b - 1) + q
                            ins = mm(o[:, q * P:(q + 1) * P], PQT[:, n, i * P:(i + 1) * P], KEYS[:, n, :], start=True, stop=True)
                        ins.then_inc(a_full, 1)
                        at["sc"].append(c["a"])
            n = 0
            for i in range(2):
                o0, o1 = bank_d(), bank_d()
                mine = [m for m in range(PICKS) if not on_dve(m)]
                for m in mine:
                    g = (2 * i + 1) * PICKS + m
                    n += 1
                    pe.wait_ge(sem("diag"), n)
                    pe.wait_ge(sem(f"row{g % NG}"), 16 * (g // NG + 1))
                    mm(o0, DIAG[:, (n - 1) % 4, :], GROWS[g % NG][:, 0:512], start=m == mine[0], stop=m == mine[-1])
                    mm(o1, DIAG[:, (n - 1) % 4, :], GROWS[g % NG][:, 512:1024], start=m == mine[0], stop=m == mine[-1]).then_inc(sem("v_used"), 1)
                pe.drain().then_inc(d_full, 2)
            at["L"] = []
            for L in range(DEPTH):
                m = {}
                at["L"].append(m)
                def transposed(i, count):
                    pe.wait_ge(sem("hn2_ready"), count)
                    for h in range(2):
                        o = bank_a()
                        for q in range(4):
                            ins = turn(o[:, q * P:(q + 1) * P], HN2[:, i, (4 * h + q) * P:(4 * h + q + 1) * P], ident)
                        ins.then_inc(a_full, 1)
                    m["turned"] = c["a"]

                transposed(0, 4 * L + 1)
                for b in range(3):
                    w = weights(512)
                    for i in range(2):
                        if b == 0:
                            if i == 1:
                                transposed(1, 4 * L + 2)
                            pe.wait_ge(a_free, m["turned"])
                        o = bank_d() if b < 2 else bank_a()
                        for k in range(KT):
                            ins = mm(o, XTP[:, k, i * P:(i + 1) * P], w[:, k, :], start=k == 0, stop=k == KT - 1)
                        ins.then_inc(d_full if b < 2 else a_full, 1)
                    was_read("d" if b < 2 else "a")
                pe.wait_ge(sem("rot2"), L + 1)
                for wh in range(2):
                    for g in range(2):
                        o = bank_a()
                        for q in range(4):
                            f, i = 2 * g + q // 2, q % 2
                            ins = turn(o[:, q * P:(q + 1) * P], QKR[:, wh, i, f * P:(f + 1) * P], ident)
                        ins.then_inc(a_full, 1)
                pe.wait_ge(a_free, c["a"])
                step, turned = iter(range(ATT_STEPS)), []

                def attend():
                    h = next(step)
                    if h < AH:
                        p0 = (h % 2) * AD
                        o = bank_d()
                        for i in range(2):
                            ins = mm(o[:, i * P:(1 + 2 * i) * P], QKT2[p0:p0 + AD, 0, h // 2, i * P:(i + 1) * P],
                                     QKT2[p0:p0 + AD, 1, h // 2, 0:(i + 1) * P], start=True, stop=True)
                        ins.then_inc(d_full, 1)
                    if 1 <= h <= AH:
                        pe.wait_ge(sem("at_p"), AH * L + h)
                        o = bank_a()
                        for s in range(3):
                            ins = turn(o[:, s * P:(s + 1) * P], ETMP[:, (h - 1) % 2, s, :], ident)
                        ins.then_inc(a_full, 1)
                        turned.append(c["a"])
                    if h >= 2:
                        h -= 2
                        pe.wait_ge(a_free, turned[h])
                        p0 = (h % 2) * AD
                        o = bank_d()
                        for i in range(2):
                            for s in range(i + 1):
                                ins = mm(o[p0:p0 + AD, i * P:(i + 1) * P], V2[:, s, h * AD:(h + 1) * AD], EPT[:, h % 2, i + s, :], start=s == 0, stop=s == i)
                        ins.then_inc(d_full, 1)

                attend()
                m["conv"] = []
                for b in range(3):
                    w = weights(512)
                    for g in range(2):
                        o = bank_d()
                        for f in (2 * g, 2 * g + 1):
                            for k in range(KT):
                                ins = mm(o[:, (f % 2) * SEQ:(f % 2 + 1) * SEQ], w[:, k, f * P:(f + 1) * P], XTP[:, k, :], start=k == 0, stop=k == KT - 1)
                        ins.then_inc(d_full, 1)
                        m["conv"].append(c["d"])
                        if g == 1:
                            was_read("d")
                        attend()
                w = weights(520)
                o = bank_a()
                for i in range(2):
                    for k in range(KT):
                        ins = mm(o[:, i * 8:i * 8 + 8], XTP[:, k, i * P:(i + 1) * P], w[:, k, 512:520], start=k == 0, stop=k == KT - 1)
                ins.then_inc(a_full, 1)
                m["ba"] = c["a"]
                attend()
                for i in range(2):
                    o = bank_a()
                    for k in range(KT):
                        ins = mm(o, XTP[:, k, i * P:(i + 1) * P], w[:, k, 0:512], start=k == 0, stop=k == KT - 1)
                    ins.then_inc(a_full, 1)
                    if i == 1:
                        was_read("a")
                    attend()
                wout = [weights(512), weights(512)]
                piece = iter([(b, 1) for b in range(2)])

                def project():
                    b, i = next(piece)
                    o = bank_d()
                    for k in range(4):
                        ins = mm(o, MIX2[:, k, i * P:(i + 1) * P], wout[b][:, k, :], start=k == 0, stop=k == 3)
                    ins.then_inc(d_full, 1)

                pe.wait_ge(sem("cv_silu"), 6 * (L + 1))
                for wh in range(3):
                    for i in range(2):
                        o = bank_a()
                        for h in range(DH):
                            ins = turn(o[:, h * P:(h + 1) * P], CV[:, wh * 4 + h, i * P:(i + 1) * P], ident)
                        ins.then_inc(a_full, 1)
                pe.wait_ge(d_free, c["d"])
                project()
                project()
                for wh in range(2):
                    pe.wait_ge(sem("dn_normed"), 2 * L + wh + 1)
                    for g in range(2):
                        o = bank_a()
                        for q in range(4):
                            h, i = 2 * g + q // 2, q % 2
                            ins = turn(o[:, q * P:(q + 1) * P], TQ[:, wh, i, h * P:(h + 1) * P], ident)
                        ins.then_inc(a_full, 1)
                m["qkf"] = c["a"]
                pe.wait_ge(sem("g_ready"), L + 1)
                o = bank_d()
                mm(o[:, 0:4], tri[:, 1, :], GT[:, 0, :], start=True, stop=True)
                mm(o[:, 4:8], tri[:, 0, :], GT[:, 1, :], start=True, stop=True).then_inc(d_full, 1)
                m["gc"] = c["d"]
                pe.wait_ge(d_free, m["gc"])
                for g in range(2):
                    o = bank_d()
                    for q in range(4):
                        h, i = 2 * g + q // 2, q % 2
                        ins = turn(o[:, q * P:(q + 1) * P], GC[:, i, h:h + 1].to_broadcast([P, P]), ident)
                    ins.then_inc(d_full, 1)
                pe.wait_ge(a_free, m["qkf"])
                for which, F in ((0, DQF), (1, DKF)):
                    for seg, (i, j) in enumerate(((0, 0), (1, 0), (1, 1))):
                        o = bank_d()
                        for h in range(DH):
                            ins = mm(o[:, h * P:(h + 1) * P], F[:, h, i * P:(i + 1) * P], DKF[:, h, j * P:(j + 1) * P], start=True, stop=True)
                        ins.then_inc(d_full, 1)
                pe.wait_ge(sem("aa_ready"), L + 1)
                for seg in (0, 2, 1):
                    o = bank_a()
                    for h in range(DH):
                        ins = turn(o[:, h * P:(h + 1) * P], AA[:, h, seg, :], ident)
                    ins.then_inc(a_full, 1)
                m["at_aT"] = c["a"] - 1
                pe.wait_ge(sem("t_init"), L + 1)
                m["level"] = []
                t_done, tw = [0, 0], [0, 0]
                for lv in range(7):
                    pe.wait_ge(sem("am_ready"), 7 * L + lv + 1)
                    for half in range(2):
                        if lv:
                            pe.wait_ge(d_free, t_done[half])
                        o = bank_a()
                        for h in range(DH):
                            n = half * 4 + h
                            ins = mm(o[:, h * P:(h + 1) * P], AM[:, lv % 2, n, :], TI[:, n, :], start=True, stop=True)
                        ins.then_inc(a_full, 1)
                        tw[half] = c["a"]
                    if lv < 3:
                        o = bank_a()
                        for h in range(DH):
                            ins = turn(o[:, h * P:(h + 1) * P], QKD[:, h, lv, :], ident)
                        ins.then_inc(a_full, 1)
                    for half in range(2):
                        pe.wait_ge(a_free, tw[half])
                        if lv < 6:
                            o = bank_d()
                            for h in range(DH):
                                n = half * 4 + h
                                ins = mm(o[:, h * P:(h + 1) * P], TU[:, n, :], TW[:, n, :], start=True, stop=True)
                            ins.then_inc(d_full, 1)
                        o = bank_d()
                        for h in range(DH):
                            n = half * 4 + h
                            ins = mm(o[:, h * P:(h + 1) * P], TW[:, n, :], TU[:, n, :], start=True, stop=True)
                        ins.then_inc(d_full, 1)
                        t_done[half] = c["d"]
                    m["level"].append(c["d"])
                pe.wait_ge(d_free, c["d"])
                pe.wait_ge(sem("vb_ready"), L + 1)
                o = bank_d()
                for h in range(DH):
                    ins = mm(o[:, h * P:(h + 1) * P], TU[:, h, :], TQ[:, 2, 0, h * P:(h + 1) * P], start=True, stop=True)
                ins.then_inc(d_full, 1)
                pe.wait_ge(d_free, c["d"])
                o = bank_d()
                for h in range(DH):
                    ins = mm(o[:, h * P:(h + 1) * P], AT[:, 2, h, :], UU[:, 0, h * P:(h + 1) * P], start=True, stop=True)
                ins.then_inc(d_full, 1)
                pe.wait_ge(d_free, c["d"])
                o = bank_d()
                for h in range(DH):
                    ins = mm(o[:, h * P:(h + 1) * P], TU[:, 4 + h, :], TQ[:, 2, 1, h * P:(h + 1) * P], start=True, stop=True)
                ins.then_inc(d_full, 1)
                pe.wait_ge(d_free, c["d"])
                o = bank_a()
                for h in range(DH):
                    ins = mm(o[:, h * P:(h + 1) * P], QKDT[:, h, 0, :], UU[:, 0, h * P:(h + 1) * P], start=True, stop=True)
                ins.then_inc(a_full, 1)
                o = bank_a()
                for h in range(DH):
                    mm(o[:, h * P:(h + 1) * P], QKDT[:, h, 1, :], UU[:, 0, h * P:(h + 1) * P], start=True, stop=False)
                    ins = mm(o[:, h * P:(h + 1) * P], QKDT[:, h, 2, :], UU[:, 1, h * P:(h + 1) * P], start=False, stop=True)
                ins.then_inc(a_full, 1)
                m["o"] = c["a"]
                held = [bank_d(), bank_d()]
                for b in range(2):
                    for k in range(4):
                        mm(held[b], MIX2[:, k, 0:P], wout[b][:, k, :], start=k == 0, stop=False)
                pe.wait_ge(sem("do_gated"), L + 1)
                for g in range(2):
                    o = bank_a()
                    for q in range(4):
                        h, i = 2 * g + q // 2, q % 2
                        ins = turn(o[:, q * P:(q + 1) * P], TQ[:, 0, i, h * P:(h + 1) * P], ident)
                    ins.then_inc(a_full, 1)
                pe.wait_ge(a_free, c["a"])
                m["mix"] = []
                for i in range(2):
                    for b in range(2):
                        o = held[b] if i == 0 else bank_d()
                        for k in range(4, KT):
                            ins = mm(o, MIX2[:, k, i * P:(i + 1) * P], wout[b][:, k, :], start=i == 1 and k == 4, stop=k == KT - 1)
                        ins.then_inc(d_full, 1)
                    m["mix"].append(c["d"])
                was_read("d", 1)
                was_read("d")
                transposed(0, 4 * L + 3)
                m["ffn"] = []
                for b in range(FBLK + 1):
                    if b < FBLK:
                        w = weights(512)
                        if b == 0:
                            o2 = [bank_d(), bank_d()]
                            for i in range(2):
                                if i == 1:
                                    transposed(1, 4 * L + 4)
                                pe.wait_ge(a_free, m["turned"])
                                for g in range(2):
                                    for wh in range(2):
                                        for k in range(KT):
                                            ins = mm(o2[g][:, wh * SEQ + i * P:wh * SEQ + (i + 1) * P], w[:, k, wh * 256 + g * P:wh * 256 + (g + 1) * P],
                                                     XTP[:, k, i * P:(i + 1) * P], start=k == 0, stop=k == KT - 1)
                                    if i == 1:
                                        ins.then_inc(d_full, 1)
                            m["ffn"] += [c["d"] - 1, c["d"]]
                            acc = [bank_a() for _ in range(4)]
                        for g in range(2) if b else ():
                            o = bank_d()
                            for wh in range(2):
                                for k in range(KT):
                                    ins = mm(o[:, wh * SEQ:(wh + 1) * SEQ], w[:, k, wh * 256 + g * P:wh * 256 + (g + 1) * P], XTP[:, k, :], start=k == 0, stop=k == KT - 1)
                            ins.then_inc(d_full, 1)
                            m["ffn"].append(c["d"])
                        was_read("d")
                    if b >= 1:
                        n = FBLK * L + b - 1
                        pe.wait_ge(sem("gu_ready"), 2 * n + 2)
                        pe.wait_ge(sem(f"wo2_in{n % 2}"), 16 * (n // 2 + 1))
                        for i in range(2):
                            for h in range(2):
                                for g in range(2):
                                    ins = mm(acc[2 * i + h], GU[:, (b - 1) % 2, g, i * P:(i + 1) * P], WO2[:, n % 2, g, h * 512:(h + 1) * 512],
                                             start=b == 1 and g == 0, stop=b == FBLK and g == 1)
                                if b == FBLK:
                                    ins.then_inc(a_full, 1)
                        if b < FBLK:
                            ins.then_inc(sem("wo2_read"), 1)
                m["end"] = c["a"]


        @block.sync
        def _(sp):
            def load(n):
                if n >= WSLOTS:
                    ring, value = last_read[n - WSLOTS]
                    sp.wait_ge(d_full if ring == "d" else a_full, value)
                for dst, src in loads[n](n):
                    sp.dma_start(dst, src).then_inc(sem(f"w_in{n % WSLOTS}"), 16)

            sp.dma_start(CCOL[:, :, :], a["cc"].rearrange("p (k w) -> p k w", w=2)).then_inc(sem("cc_in"), 16)
            load(0)
            ba = a["b_ada"]
            for dst, piece in ((MODA[:, 0, :], 0), (MODA[:, 2, :], 0), (MODA[:, 1, :], 1), (MODA[:, 3, :], 1)):
                sp.dma_start(dst, ba[:, piece * D:(piece + 1) * D].to_broadcast([P, D])).then_inc(sem("moda_in"), 16)
            load(1)
            sp.dma_start(X[:, :, :], a["x"][0].rearrange("(t p) d -> p t d", p=P)).then_inc(sem("x_in"), 16)
            sp.dma_start(XC[:, :, :], a["ctx"][0].rearrange("(t p) d -> p t d", p=P)).then_inc(sem("xc_in"), 16)
            load(2)
            for dst, piece in ((MODB[:, 0, :], 2), (MODB[:, 1, :], 3), (MODB[:, 2, :], 4), (MODB[:, 3, :], 5)):
                sp.dma_start(dst, ba[:, piece * D:(piece + 1) * D].to_broadcast([P, D])).then_inc(sem("modb_in"), 16)
            sp.dma_start(GN[:, :], a["g_norm1"].to_broadcast([P, D])).then_inc(sem("gn_in"), 16)
            sp.dma_start(CONVW[:, :, :], a["conv1"].rearrange("p (f j) -> p f j", j=3)).then_inc(sem("small_in"), 16)
            sp.dma_start(GB[:, :], a["gate_bias"].to_broadcast([P, 16])).then_inc(sem("small_in"), 16)
            sp.dma_start(CW2[:, :, :, :], a["conv2"].rearrange("p (l f j) -> p l f j", l=DEPTH, j=4)).then_inc(sem("small_in"), 16)
            sp.dma_start(FW2[:, :, :, :], a["ffn_conv"].rearrange("p (l f j) -> p l f j", l=DEPTH, j=3)).then_inc(sem("small_in"), 16)
            sp.dma_start(FB2[:, :, :], a["ffn_bias"].rearrange("p (l f) -> p l f", l=DEPTH)).then_inc(sem("small_in"), 16)
            sp.dma_start(AB2[:, :, :], a["decay"].to_broadcast([P, 16]).rearrange("p (l n) -> p l n", l=DEPTH)).then_inc(sem("small_in"), 16)
            sp.dma_start(v(0, NCONST), a["consts"]).then_inc(sem("consts"), 16)
            for n in range(3, len(loads)):
                load(n)
            for i in range(2):
                sp.wait_ge(sem("x_ready"), 4 * DEPTH + 2 + i)
                sp.dma_start(out[0, i * P:(i + 1) * P, :], X[:, i, :]).then_inc(sem("stored"), 16)
            sp.wait_ge(sem("stored"), 2 * 16)

        @block.gpsimd
        def _(pool):
            nc.gpsimd.memset(HALF[:, :], -0.5).then_inc(sem("half"), 1)
            pool.wait_ge(sem("half"), 1)

            norm = iter(range(1, 100))

            def rsqrt(n, lo=0):
                pool.wait_ge(sem("ms_ready"), next(norm))
                nc.gpsimd.tensor_tensor(RS[:, lo:n], MS[:, lo:n], HALF[:, lo:n], ALU.pow).then_inc(sem("rs_ready"), 1)

            rsqrt(4)
            pool.wait_ge(sem("hn_ready"), 4)
            for lo, hi, name in ((0, QR, "g_cq"), (QR, QR + KVR, "g_ckv"), (384, 576, "g_qn"), (576, 768, "g_kn")):
                pool.dma_start(GAIN[:, lo:hi], a[name].to_broadcast([P, hi - lo])).then_inc(sem("gain_in"), 16)
            pool.dma_start(GOUT[:, :], a["g_mlstm"].to_broadcast([P, 512])).then_inc(sem("gout_in"), 16)
            rsqrt(6)
            rsqrt(24)
            pool.wait_ge(d_full, at["km_read_d"])
            pool.wait_ge(a_full, at["km_read_a"])
            pool.dma_start(MMASK[:, :, :], a["mmask"].rearrange("p (a t) -> p a t", a=4)).then_inc(sem("mmask_in"), 16)
            pool.wait_ge(d_full, at["ml_qk_read"])
            pool.dma_start(G2[:, :], a["g_norm2"].to_broadcast([P, D])).then_inc(sem("g2_in"), 16)
            pool.wait_ge(a_full, at["ml_v_read"])
            pool.dma_start(KEYS[:, :, :], a["sub_keys_T"].rearrange("p (c k) -> p c k", c=16)).then_inc(sem("keys_in"), 16)
            rsqrt(8)
            rsqrt(2)
            pool.wait_ge(a_full, at["sc"][7])
            for g in range(4 * PICKS):
                i, which, m = g // (2 * PICKS), g // PICKS % 2, g % PICKS
                if m % (PICKS // 2) == 0 and which == 0:
                    pool.wait_ge(sem("eidx"), 2 * i + m // (PICKS // 2) + 1)
                if g >= NG:
                    pool.wait_ge(*used(g - NG))
                nc.gpsimd.indirect_dma_start(
                    GROWS[g % NG], None, a["expert_u" if which == 0 else "expert_v"],
                    bass.IndirectOffsetOnAxis(ap=EIDX[:, i, m:m + 1], axis=0)).then_inc(sem(f"row{g % NG}"), 16)
            for L in range(DEPTH):
                m = at["L"][L]

                def gains(slot, name, layer):
                    pool.dma_start(NW[:, slot, :], a[name][layer:layer + 1, :].to_broadcast([P, D])).then_inc(sem(f"nw_in{slot}"), 16)

                if L == 0:
                    pool.wait_ge(sem("u_used"), 2 * PICKS)
                    pool.dma_start(DNW[:, :, :], a["dn_norm"].to_broadcast([P, DEPTH * P]).rearrange("p (l n) -> p l n", l=DEPTH)).then_inc(sem("dnw_in"), 16)
                    gains(0, "norm_pre_mix_2", 0)
                    gains(1, "norm_post_mix_2", 0)
                    for i in range(2):
                        rsqrt(i + 1, i)
                pool.wait_ge(sem("hn2_ready"), 4 * L + 2)
                gains(0, "norm_pre_ffn_2", L)
                rsqrt(16)
                pool.wait_ge(a_free, m["at_aT"])
                for lv in range(7):
                    if lv >= 2:
                        pool.wait_ge(d_full, m["level"][lv - 2])
                    nc.gpsimd.tensor_tensor(AM[:, lv % 2, :, :], AT[:, 0:2, :, :].rearrange("p s h j -> p (s h) j"),
                                            level[:, lv, :].unsqueeze(1).to_broadcast([P, 8, P]), ALU.mult).then_inc(sem("am_ready"), 1)
                rsqrt(8)
                for i in range(2):
                    rsqrt(i + 1, i)
                    rsqrt(i + 1, i)
                pool.wait_ge(sem("x_ready"), 4 * L + 5)
                gains(1, "norm_post_ffn_2", L)
                for b in range(FBLK):
                    n = FBLK * L + b
                    if b == 0:
                        pool.wait_ge(d_full, m["mix"][1])
                    if b >= 2:
                        pool.wait_ge(sem("wo2_read"), (FBLK - 1) * L + b - 1)
                    pool.dma_start(WO2[:, n % 2, :, :], a["ffn_w_out_2"][L].rearrange("(b g p) n -> b p g n", g=2, p=P)[b]).then_inc(sem(f"wo2_in{n % 2}"), 16)
                pool.wait_ge(sem("hn2_ready"), 4 * L + 4)
                if L + 1 < DEPTH:
                    gains(0, "norm_pre_mix_2", L + 1)
                for i in range(2):
                    rsqrt(i + 1, i)
                    if L + 1 < DEPTH:
                        rsqrt(i + 1, i)
                if L + 1 < DEPTH:
                    pool.wait_ge(sem("x_ready"), 4 * L + 7)
                    gains(1, "norm_post_mix_2", L + 1)

        @block.scalar
        def _(act):
            af = nc.scalar.activation
            c = {"a": 0}

            def full():
                c["a"] += 1
                act.wait_ge(a_full, c["a"])
                return PS[:, 4 + (c["a"] - 1) % 4, :]

            def squares(jobs):
                for k, (junk, src, n) in enumerate(jobs):
                    if k:
                        act.drain()
                    ins = af(junk, src, ACT.Square, accum_out=SS[:, n:n + 1])
                ins.then_inc(sem("ss_ready"), 1)

            act.wait_ge(sem("cc_in"), 16)
            af(SILC[:, :, :], CCOL[:, :, :], ACT.Silu).then_inc(sem("silu_c"), 1)
            act.wait_ge(sem("x_in"), 16)
            act.wait_ge(sem("xc_in"), 16)
            squares([(HN[:, 0, :], X[:, n, :] if n < 2 else XC[:, n - 2, :], n) for n in range(4)])
            for n, j in enumerate((2, 3, 0, 1)):
                for h in range(2):
                    o = full()
                    act.copy(XTv[:, 4 * h:4 * h + 4, j * P:(j + 1) * P], o.rearrange("p (k t) -> p k t", k=4)).then_inc(a_free, 1)
            for j in (2, 3, 0, 1):
                lo = 0 if j >= 2 else QR
                o = full()
                act.copy(CQKV[:, j, lo:448], o[:, lo:448])
                act.copy(GATE[:, j, :], o[:, 448:464]).then_inc(a_free, 1)
            act.drain()
            squares([(JUNK[:, 0:QR], CQKV[:, 2 + n, 0:QR], n) for n in range(2)]
                    + [(JUNK[:, 0:KVR], CQKV[:, j, QR:QR + KVR], 2 + j) for j in range(4)])
            act.wait_ge(sem("small_in"), 6 * 16)
            qkf = [QF[:, 0, :], QF[:, 1, :], KF[:, 0, :], KF[:, 1, :]]
            for f in range(4):
                n = at["ml_qk"][f]
                act.wait_ge(d_full, n)
                act.mul(qkf[f], PS[:, (n - 1) % 4, 0:SEQ if f < 2 else ALL], CONVW[:, f, 1:2]).then_inc(sem("centre_tap"), 1)
            for j in range(4):
                o = full()
                act.copy(VML[:, j, :], o).then_inc(a_free, 1)
            for i in range(2):
                o = full()
                af(OML[:, i, :], o, ACT.Sigmoid).then_inc(a_free, 1)
            for f in range(4):
                act.wait_ge(d_free, at["ml_qk"][f])
                af(qkf[f], qkf[f], ACT.Silu).then_inc(sem("mconv"), 1)
            for n in range(2):
                o = full()
                act.copy(CNT[:, n * 512:(n + 1) * 512], o).then_inc(a_free, 1)
            for i in range(2):
                for h in range(2):
                    o = full()
                    act.copy(QM[:, i, 2 * h:2 * h + 2, :], o[:, 0:384].rearrange("p (h d) -> p h d", h=2)).then_inc(a_free, 1)
            act.drain()
            act.wait_ge(sem("km_ready"), 1)
            squares([(JUNK[:, 0:QK], (QM[:, n, h, :] if n < 2 else KM[:, n - 2, h, :]), 4 * n + h) for n in range(6) for h in range(HEADS)])
            act.wait_ge(sem("fx_ready"), 1)
            af(LT1[:, :, :], LT2[:, :, :], ACT.Abs)
            act.drain()
            af(LT1[:, :, :], LT1[:, :, :], ACT.Exp, scale=-1.0).then_inc(sem("lf_exp"), 1)
            act.wait_ge(sem("lf_plus1"), 1)
            af(LT1[:, :, :], LT1[:, :, :], ACT.Ln).then_inc(sem("lf_ln"), 1)
            for hp in range(2):
                o = full()
                act.copy(QTR[:, 2 * hp:2 * hp + 2, :], o[0:ROPE, :].rearrange("p (h t) -> p h t", h=2)).then_inc(a_free, 1)
            for h in range(HEADS):
                o = full()
                act.copy(KTR[:, h, :], o[0:ROPE, :]).then_inc(a_free, 1)
            mla_step = iter(range(10))

            def mla():
                u = next(mla_step)
                if 1 <= u <= 8:
                    o = full()
                    act.copy(PT[:, (u - 1) % 2, :, :], o.rearrange("p (s q) -> p s q", s=4)).then_inc(a_free, 1)
                if u < 8:
                    o = full()
                    act.wait_ge(sem("mla_max"), u + 1)
                    af(EXPS[:, u % 2, :], o, ACT.Exp, bias=MX[:, u:u + 1], scale=float(QK) ** -0.5, accum_out=SM[:, u:u + 1]).then_inc(a_free, 1)

            mla()
            mla()
            for h in range(HEADS):
                act.wait_ge(sem("ml_max"), h + 1)
                for n in range(4):
                    af(TMP[n], TMP[n], ACT.Exp, bias=MX[:, 8 + n:9 + n])
                af(FLO[:, :], FLO[:, :], ACT.Exp).then_inc(sem("ml_exp"), 1)
                mla()
                mla()
                for i in range(2):
                    o = full()
                    act.copy(MLPT[:, i, :, :], o.rearrange("p (s q) -> p s q", s=4)).then_inc(a_free, 1)
                o = full()
                act.copy(HML[:, :, h * VD:(h + 1) * VD], o[:, 0:2 * VD].rearrange("p (i e) -> p i e", i=2)).then_inc(a_free, 1)
            act.drain()
            squares([(JUNK[:, 0:VD], HML[:, i, h * VD:(h + 1) * VD], 4 * i + h) for i in range(2) for h in range(HEADS)])
            for h in range(2):
                o = full()
                act.copy(MIXT[:, 4 + 2 * h:6 + 2 * h, :], o.rearrange("p (k t) -> p k t", k=2)).then_inc(a_free, 1)
            act.wait_ge(sem("x_ready"), 1)
            squares([(v(R7 + 1024, D), X[:, i, :], i) for i in range(2)])
            for i in range(2):
                for h in range(2):
                    o = full()
                    act.copy(XTP[:, 4 * h:4 * h + 4, i * P:(i + 1) * P], o.rearrange("p (k t) -> p k t", k=4)).then_inc(a_free, 1)
            for b in range(5):
                if b < 4:
                    for g in (2 * b, 2 * b + 1):
                        o = full()
                        act.copy(PQT[:, 2 * g:2 * g + 2, :], o.rearrange("p (f t) -> p f t", f=2)).then_inc(a_free, 1)
                if b >= 1:
                    for i in range(2):
                        o = full()
                        act.copy(SC[:, i, 4 * b - 4:4 * b, :], o.rearrange("p (c k) -> p c k", c=4)).then_inc(a_free, 1)
            n = 0
            for i in range(2):
                act.wait_ge(sem("best_ready"), i + 1)
                af(GW[:, i, :], GW[:, i, :], ACT.Exp).then_inc(sem("best_exp"), 1)
                act.wait_ge(sem("u_used"), (i + 1) * PICKS)
                af(DOT[:, i, :], DOT[:, i, :], ACT.Gelu).then_inc(sem("gelu_done"), 1)
                if i == 1:
                    act.wait_ge(sem("x_ready"), 2)
                    squares([(YSQ, X[:, 0, :], 0)])
                act.wait_ge(sem("gw_ready"), i + 1)
                for m in range(PICKS):
                    if on_dve(m):
                        continue
                    if n >= 4:
                        act.wait_ge(sem("v_used"), n - 3)
                    act.mul(DIAG[:, n % 4, :], ident, GW[:, i, m:m + 1]).then_inc(sem("diag"), 1)
                    n += 1
            for L in range(DEPTH):
                m = at["L"][L]

                def x_squares(i, count):
                    act.wait_ge(sem("x_ready"), count)
                    squares([(YSQ, X[:, i, :], i)])

                def turned(i):
                    for h in range(2):
                        o = full()
                        act.copy(XTP[:, 4 * h:4 * h + 4, i * P:(i + 1) * P], o.rearrange("p (k t) -> p k t", k=4)).then_inc(a_free, 1)

                if L == 0:
                    turned(0)
                    x_squares(1, 3)
                turned(1)
                for i in range(2):
                    o = full()
                    act.copy(V2[:, i, :], o).then_inc(a_free, 1)
                for wh in range(2):
                    for g in range(2):
                        o = full()
                        act.copy(QKT2[:, wh, 2 * g:2 * g + 2, :], o.rearrange("p (f t) -> p f t", f=2)).then_inc(a_free, 1)
                step = iter(range(ATT_STEPS))

                def attend():
                    h = next(step)
                    if 1 <= h <= AH:
                        o = full()
                        act.copy(EPT[:, (h - 1) % 2, :, :], o[:, 0:3 * P].rearrange("p (s q) -> p s q", s=3)).then_inc(a_free, 1)
                    if h < AH:
                        act.wait_ge(sem("at_max"), AH * L + h + 1)
                        for i in range(2):
                            e = ETMP[:, h % 2, i:1 + 2 * i, :]
                            ins = af(e, e, ACT.Exp, bias=MX[:, 2 * h + i:2 * h + i + 1], accum_out=SM[:, 2 * h + i:2 * h + i + 1])
                        ins.then_inc(sem("at_exp"), 1)

                attend()
                for g in range(6):
                    n = m["conv"][g]
                    act.wait_ge(d_full, n)
                    for f in range(2):
                        ins = act.mul(CV[:, 2 * g + f, :], PS[:, (n - 1) % 4, f * SEQ:(f + 1) * SEQ], CW2[:, L, 2 * g + f, 3:4])
                    ins.then_inc(sem("cv_tap"), 1)
                    attend()
                for g in range(6):
                    act.wait_ge(d_free, m["conv"][g])
                    af(CV[:, 2 * g:2 * g + 2, :], CV[:, 2 * g:2 * g + 2, :], ACT.Silu).then_inc(sem("cv_silu"), 1)
                o = full()
                ob = o[:, 0:16].rearrange("p (i n) -> p i n", i=2)
                act.copy(BT[:, :, :], ob[:, :, 0:4])
                act.copy(ST1[:, :, :], ob[:, :, 4:8]).then_inc(a_free, 1)
                attend()
                for i in range(2):
                    o = full()
                    act.copy(Z2[:, i, :], o).then_inc(a_free, 1)
                    attend()
                act.drain()
                af(BT[:, :, :], BT[:, :, :], ACT.Sigmoid)
                for wh in range(3):
                    for i in range(2):
                        o = full()
                        act.copy(TQ[:, wh, i, :], o).then_inc(a_free, 1)
                act.drain()
                squares([(v(C0 + 3072, P), TQ[:, wh, i, h * P:(h + 1) * P], wh * 8 + i * 4 + h)
                         for wh in range(2) for i in range(2) for h in range(DH)])
                act.wait_ge(sem("sp_in"), L + 1)
                af(ST2[:, :, :], ST1[:, :, :], ACT.Abs)
                act.drain()
                af(AE[:, :], AB2[:, L, 0:4], ACT.Exp)
                af(ST2[:, :, :], ST2[:, :, :], ACT.Exp, scale=-1.0).then_inc(sem("sp_exp"), 1)
                act.wait_ge(sem("sp_plus1"), L + 1)
                af(ST2[:, :, :], ST2[:, :, :], ACT.Ln).then_inc(sem("sp_ln"), 1)
                for F in (DQF, DKF):
                    for g in range(2):
                        o = full()
                        act.copy(F[:, 2 * g:2 * g + 2, :], o.rearrange("p (h t) -> p h t", h=2)).then_inc(a_free, 1)
                act.wait_ge(sem("dec_in"), L + 1)
                af(DEC[:, :, :, :], DEC[:, :, :, :], ACT.Exp, scale=-1.0).then_inc(sem("dec_exp"), 1)
                for n in range(3):
                    o = full()
                    act.copy(AT[:, n, :, :], o.rearrange("p (h j) -> p h j", h=4)).then_inc(a_free, 1)
                af(Z2[:, :, :], Z2[:, :, :], ACT.Silu)
                for lv in range(7):
                    for half in range(2):
                        o = full()
                        act.copy(TW[:, 4 * half:4 * half + 4, :], o.rearrange("p (h j) -> p h j", h=4)).then_inc(a_free, 1)
                    if lv < 3:
                        o = full()
                        act.copy(QKDT[:, :, lv, :], o.rearrange("p (h j) -> p h j", h=4)).then_inc(a_free, 1)
                for i in range(2):
                    o = full()
                    act.copy(TQ[:, 1, i, :], o).then_inc(a_free, 1)
                act.drain()
                squares([(v(C0 + 3072, P), TQ[:, 1, i, h * P:(h + 1) * P], i * 4 + h) for i in range(2) for h in range(DH)])
                for g in range(2):
                    o = full()
                    act.copy(MIX2[:, 4 + 2 * g:6 + 2 * g, :], o.rearrange("p (k t) -> p k t", k=2)).then_inc(a_free, 1)
                for i in range(2):
                    act.wait_ge(d_free, m["mix"][i])
                    act.drain()
                    squares([(YSQ, MO[:, i, :], i)])
                    if i == 1:
                        turned(0)
                    act.drain()
                    x_squares(i, 4 * L + 4 + i)
                turned(1)
                for n in range(2 * FBLK + 1):
                    if n < 2 * FBLK:
                        bank = m["ffn"][n]
                        act.wait_ge(d_full, bank)
                        N = 2 * FBLK * L + n
                        if N >= 4:
                            act.wait_ge(sem("gu_ready"), N - 3)
                        for wh in range(2):
                            f = wh * DFF // P + n
                            ins = af(YG[:, n % 4, wh, :], PS[:, (bank - 1) % 4, wh * SEQ:(wh + 1) * SEQ], ACT.Identity,
                                     scale=FW2[:, L, f, 2:3], bias=FB2[:, L, f:f + 1])
                        ins.then_inc(sem("ffn_tap"), 1)
                    if n >= 1:
                        act.wait_ge(d_free, m["ffn"][n - 1])
                        af(YG[:, (n - 1) % 4, 0, :], YG[:, (n - 1) % 4, 0, :], ACT.Gelu_apprx_tanh).then_inc(sem("ffn_gelu"), 1)
                for i in range(2):
                    for h in range(2):
                        o = full()
                        act.copy(MO[:, i, h * 512:(h + 1) * 512], o).then_inc(a_free, 1)
                    act.drain()
                    squares([(YSQ, MO[:, i, :], i)])
                    if L + 1 < DEPTH:
                        if i == 1:
                            turned(0)
                        act.drain()
                        x_squares(i, 4 * L + 6 + i)

        @block.vector
        def _(dve):
            tt, ts, stt, ttr = nc.vector.tensor_tensor, nc.vector.tensor_scalar, nc.vector.scalar_tensor_tensor, nc.vector.tensor_tensor_reduce
            copy = nc.vector.tensor_copy
            c = {"d": 0, "norm": 0}

            def full():
                c["d"] += 1
                dve.wait_ge(d_full, c["d"])
                return PS[:, (c["d"] - 1) % 4, :]

            def rsqrt_of_mean(parts, eps_only=False):
                c["norm"] += 1
                dve.wait_ge(sem("ss_ready"), c["norm"])
                for lo, hi, width in parts:
                    ins = ts(MS[:, lo:hi], SS[:, lo:hi], 1.0 / width, EPS, ALU.mult, ALU.add)
                ins.then_inc(sem("ms_ready"), 1)
                dve.wait_ge(sem("rs_ready"), c["norm"])

            def bcast(ap, at_, shape):
                return ap.unsqueeze(at_).to_broadcast(shape)

            dve.wait_ge(sem("moda_in"), 4 * 16)

            def normed(n):
                src = X[:, n, :] if n < 2 else XC[:, n - 2, :]
                if n >= 2:
                    dve.wait_ge(a_full, 2 * (n - 1))
                which = 0 if n < 2 else 2
                stt(HN[:, n % 2, :], src, RS[:, n:n + 1], MODA[:, which + 1, :], ALU.mult, ALU.mult)
                dve.drain()
                tt(HN[:, n % 2, :], HN[:, n % 2, :], MODA[:, which, :], ALU.add).then_inc(sem("hn_ready"), 1)

            def modulation(lo, hi):
                for b in range(lo, hi):
                    half = slice(b % 2 * 512, b % 2 * 512 + 512)
                    for dst in ([MODA[:, b // 2, half], MODA[:, 2 + b // 2, half]] if b < 4 else [MODB[:, b // 2 - 2, half]]):
                        o = full()
                        tt(dst, o, dst, ALU.add).then_inc(d_free, 1)

            modulation(0, 4)
            dve.wait_ge(sem("gn_in"), 16)
            dve.drain()
            rsqrt_of_mean([(0, 4, D)])
            for n in range(4):
                if n % 2 == 0:
                    stt(MODA[:, n + 1, :], MODA[:, n + 1, :], 1.0, GN[:, :], ALU.add, ALU.mult)
                    dve.drain()
                normed(n)
            dve.wait_ge(sem("modb_in"), 4 * 16)
            modulation(4, 6)
            dve.wait_ge(sem("gain_in"), 4 * 16)
            rsqrt_of_mean([(0, 2, QR), (2, 6, KVR)])
            for i in range(2):
                stt(CN[:, i * QR:(i + 1) * QR], CQKV[:, 2 + i, 0:QR], RS[:, i:i + 1], GAIN[:, 0:QR], ALU.mult, ALU.mult)
            for j in range(4):
                ins = stt(CN[:, 512 + j * P:512 + (j + 1) * P], CQKV[:, j, QR:QR + KVR], RS[:, 2 + j:3 + j], GAIN[:, QR:QR + KVR], ALU.mult, ALU.mult)
            ins.then_inc(sem("cn_ready"), 1)
            for f in range(4):
                o = full()
                dve.wait_ge(sem("centre_tap"), f + 1)
                n = 1 if f < 2 else 2
                y = (QF[:, f, :] if f < 2 else KF[:, f - 2, :]).rearrange("p (s t) -> p s t", s=n)
                x = o[:, 0:n * SEQ].rearrange("p (s t) -> p s t", s=n)
                stt(y[:, :, 1:SEQ], x[:, :, 0:SEQ - 1], CONVW[:, f, 0:1], y[:, :, 1:SEQ], ALU.mult, ALU.add)
                dve.drain()
                stt(y[:, :, 0:SEQ - 1], x[:, :, 1:SEQ], CONVW[:, f, 2:3], y[:, :, 0:SEQ - 1], ALU.mult, ALU.add).then_inc(d_free, 1)
            dve.wait_ge(sem("small_in"), 6 * 16)
            dve.wait_ge(a_free, at["cqkv"])
            tt(IG[:, :, :], GATE[:, :, 0:8], bcast(GB[:, 0:8], 1, [P, 4, 8]), ALU.add)
            tt(LT2[:, :, :], GATE[:, :, 8:16], bcast(GB[:, 8:16], 1, [P, 4, 8]), ALU.add).then_inc(sem("fx_ready"), 1)
            modulation(6, 8)
            for j in range(4):
                for h in range(2):
                    o = full().rearrange("p (h e) -> p h e", h=2)
                    copy(KM[:, j, 2 * h:2 * h + 2, 0:NOPE], o[:, :, 0:NOPE])
                    copy(VM[:, j, 2 * h:2 * h + 2, :], o[:, :, NOPE:NOPE + VD]).then_inc(d_free, 1)
            for j in range(4):
                ins = copy(KM[:, j, :, NOPE:QK], bcast(CQKV[:, j, QR + KVR:448], 1, [P, HEADS, ROPE]))
            ins.then_inc(sem("km_ready"), 1)
            rsqrt_of_mean([(0, 24, QK)])
            for n in range(6):
                for h in range(HEADS):
                    t = QM[:, n, h, :] if n < 2 else KM[:, n - 2, h, :]
                    stt(t, t, RS[:, 4 * n + h:4 * n + h + 1], GAIN[:, 384:576] if n < 2 else GAIN[:, 576:768], ALU.mult, ALU.mult)
            dve.drain()
            for n in range(4):
                t = QM[:, n, :, NOPE:QK] if n < 2 else KM[:, n, :, NOPE:QK]
                i = n % 2
                t5 = t.rearrange("p h (a f e) -> p h a f e", a=2, f=2)
                s5 = SWAP[:, n % 2, :, :].rearrange("p h (a f e) -> p h a f e", a=2, f=2)
                sin = rope1[:, 1, i, :].rearrange("p (a f e) -> p a f e", a=2, f=2)
                for f in range(2):
                    tt(s5[:, :, :, f, :], t5[:, :, :, 1 - f, :], bcast(sin[:, :, f, :], 1, [P, HEADS, 2, 16]), ALU.mult)
                dve.drain()
                tt(t, t, bcast(rope1[:, 0, i, :], 1, [P, HEADS, ROPE]), ALU.mult)
                dve.drain()
                ins = tt(t, t, SWAP[:, n % 2, :, :], ALU.add)
            ins.then_inc(sem("qk_roped"), 1)
            modulation(8, 12)
            dve.wait_ge(sem("lf_exp"), 1)
            ts(LT1[:, :, :], LT1[:, :, :], 1.0, None, ALU.add).then_inc(sem("lf_plus1"), 1)
            ts(LT2[:, :, :], LT2[:, :, :], 0.0, None, ALU.min)
            dve.wait_ge(sem("lf_ln"), 1)
            dve.drain()
            tt(LF[:, :, :], LT2[:, :, :], LT1[:, :, :], ALU.subtract).then_inc(sem("lf_ready"), 1)
            for hp in range(2):
                o = full()
                copy(QTN[:, 2 * hp:2 * hp + 2, :], o.rearrange("p (h t) -> p h t", h=2)).then_inc(d_free, 1)
            for h in range(HEADS):
                o = full()
                copy(KTN[:, h, :], o).then_inc(d_free, 1)
            mla_step, mla_early = iter(range(10)), iter(range(1, 9))

            def mla_probabilities():
                u = next(mla_early, None)
                if u is not None:
                    dve.wait_ge(a_free, at["mla_s"][u - 1])
                    nc.vector.reciprocal(RC[:, u - 1:u], SM[:, u - 1:u])
                    dve.drain()
                    ts(EXPS[:, (u - 1) % 2, :], EXPS[:, (u - 1) % 2, :], RC[:, u - 1:u], None, ALU.mult).then_inc(sem("mla_p"), 1)

            def mla():
                u = next(mla_step)
                if u < 8:
                    n = at["mla_s"][u]
                    dve.wait_ge(a_full, n)
                    nc.vector.reduce_max(MN[:, u:u + 1], PS[:, 4 + (n - 1) % 4, :], AX.X)
                    dve.drain()
                    ts(MX[:, u:u + 1], MN[:, u:u + 1], -float(QK) ** -0.5, None, ALU.mult).then_inc(sem("mla_max"), 1)
                if u >= 2:
                    h, i = (u - 2) // 2, u % 2
                    o = full()
                    copy(MIXT[:, h, i * P:(i + 1) * P], o[:, 0:P]).then_inc(d_free, 1)

            o = full()
            copy(FCOL[:, :, :], o[:, 0:32].rearrange("p (j n) -> p j n", j=4)).then_inc(d_free, 1)
            dve.drain()
            tt(BCOL[:, :, :], IG[:, :, :], FCOL[:, :, :], ALU.subtract).then_inc(sem("bcol_ready"), 1)
            mla()
            mla_probabilities()
            mla()
            dve.wait_ge(sem("mmask_in"), 16)
            for h in range(HEADS):
                mla_probabilities()
                for d in range(2):
                    o = full()
                    for i in range(2):
                        n = 2 * i + d
                        ins = ttr(out=TMP[n], in0=o, in1=MMASK[:, n, :], scale=1.0, scalar=-3e38, op0=ALU.add, op1=ALU.max, accum_out=MN[:, 8 + n:9 + n])
                    ins.then_inc(d_free, 1)
                dve.drain()
                ts(MX[:, 8:12], MN[:, 8:12], -1.0, None, ALU.mult)
                stt(FLO[:, :].rearrange("p (i d) -> p i d", i=2), MN[:, 8:12].rearrange("p (i d) -> p i d", i=2), -1.0,
                    FCOL[:, 2:4, h::4], ALU.mult, ALU.subtract)
                dve.drain()
                ts(FLO[:, :], FLO[:, :], 88.0, None, ALU.min).then_inc(sem("ml_max"), 1)
                mla()
                mla_probabilities()
                dve.wait_ge(sem("ml_exp"), h + 1)
                for i in range(2):
                    o = full()
                    for d in range(2):
                        n = 2 * i + d
                        ins = ttr(out=TMP[n], in0=TMP[n], in1=o, scale=float(MLQK) ** -0.5, scalar=0.0, op0=ALU.mult, op1=ALU.add, accum_out=DEN[:, n:n + 1])
                    ins.then_inc(d_free, 1)
                dve.drain()
                stt(FLO[:, :], DEN[:, :], -1.0, FLO[:, :], ALU.mult, ALU.max)
                dve.drain()
                tt(DEN[:, :], DEN[:, :], FLO[:, :], ALU.max)
                dve.drain()
                nc.vector.reciprocal(RC[:, 8:12], DEN[:, :])
                dve.drain()
                for i in range(2):
                    ts(COMB[:, i, :], TMP[2 * i], RC[:, 8 + 2 * i:9 + 2 * i], None, ALU.mult)
                dve.drain()
                for i in range(2):
                    stt(COMB[:, i, :], TMP[2 * i + 1], RC[:, 9 + 2 * i:10 + 2 * i], COMB[:, i, :], ALU.mult, ALU.add).then_inc(sem("ml_p"), 1)
                mla()
            dve.wait_ge(sem("gout_in"), 16)
            rsqrt_of_mean([(0, 8, VD)])
            for i in range(2):
                for h in range(HEADS):
                    e = slice(h * VD, (h + 1) * VD)
                    stt(HMT[:, i, e], HML[:, i, e], RS[:, 4 * i + h:4 * i + h + 1], GOUT[:, e], ALU.mult, ALU.mult)
            dve.drain()
            tt(HMT[:, :, :], HMT[:, :, :], OML[:, :, :], ALU.mult).then_inc(sem("hml_gated"), 1)
            for b in range(2):
                e = slice(b * 512, (b + 1) * 512)
                for i in range(2):
                    o = full()
                    tt(MTMP[:, i, :], o, MODB[:, 0, e], ALU.mult).then_inc(d_free, 1)
                    dve.drain()
                    ins = tt(X[:, i, e], X[:, i, e], MTMP[:, i, :], ALU.add)
            ins.then_inc(sem("x_ready"), 1)
            dve.wait_ge(sem("g2_in"), 16)
            stt(MODB[:, 2, :], MODB[:, 2, :], 1.0, G2[:, :], ALU.add, ALU.mult)
            rsqrt_of_mean([(0, 2, D)])
            dve.drain()
            for i in range(2):
                stt(H2[:, i, :], X[:, i, :], RS[:, i:i + 1], MODB[:, 2, :], ALU.mult, ALU.mult)
                dve.drain()
                tt(H2[:, i, :], H2[:, i, :], MODB[:, 1, :], ALU.add).then_inc(sem("h2_ready"), 1)

            def top16(values, best, index, rest, n):
                for k in range(n):
                    nc.vector.max(best[:, k, 0:8], values[:, k, :])
                dve.drain()
                yield
                for k in range(n):
                    nc.vector.max_index(index[:, k, 0:8], best[:, k, 0:8], values[:, k, :])
                    nc.vector.match_replace(out=rest[:, k, :], in_to_replace=best[:, k, 0:8], in_values=values[:, k, :], imm_value=-3e38)
                dve.drain()
                yield
                for k in range(n):
                    nc.vector.max(best[:, k, 8:16], rest[:, k, :])
                dve.drain()
                for k in range(n):
                    nc.vector.max_index(index[:, k, 8:16], best[:, k, 8:16], rest[:, k, :])
                dve.drain()
                yield

            def search(i):
                for b in range(4):
                    dve.wait_ge(a_free, at["sc"][2 * b + i])
                    c4 = slice(4 * b, 4 * b + 4)
                    yield from top16(SC[:, i, c4, :], SV[:, c4, :], SIU[:, c4, :], SCR[:, c4, :], 4)
                copy(SIF[:, :, :], SIU[:, :, :])
                sv = SV.rearrange("p (h w) k -> p h w k", w=2)
                sf = SIF.rearrange("p (h w) k -> p h w k", w=2)
                full4 = [P, PH, TOPK, TOPK]
                tt(CAND.rearrange("p h (x y) -> p h x y", x=TOPK), bcast(sv[:, :, 0, :], 3, full4), bcast(sv[:, :, 1, :], 2, full4), ALU.add)
                dve.drain()
                yield
                half4 = [P, 4, TOPK, TOPK]
                for h in (0, 4):
                    h4 = slice(h, h + 4)
                    yield from top16(CAND[:, h4, :], BEST[:, h4, :], POSU[:, h4, :], CANDR[:, h4, :], 4)
                    pa, eq = PA[:, h4, :], EQ[:, h4, :, :]
                    ts(pa, POSU[:, h4, :], 4, None, ALU.logical_shift_right)
                    dve.drain()
                    copy(POSF[:, 0, h4, :], pa)
                    dve.drain()
                    ts(pa, POSU[:, h4, :], TOPK - 1, None, ALU.bitwise_and)
                    dve.drain()
                    copy(POSF[:, 1, h4, :], pa)
                    dve.drain()
                    yield
                    for w in range(2):
                        tt(eq, bcast(POSF[:, w, h4, :], 3, half4), iota.unsqueeze(1).unsqueeze(1).to_broadcast(half4), ALU.is_equal)
                        dve.drain()
                        tt(eq, eq, bcast(sf[:, h4, w, :], 2, half4), ALU.mult)
                        dve.drain()
                        nc.vector.tensor_reduce(SEL[:, w, h4, :], eq, AX.X, ALU.add)
                        dve.drain()
                        yield
                    stt(EIDX[:, i, h * TOPK:(h + 4) * TOPK].rearrange("p (h k) -> p h k", h=4), SEL[:, 0, h4, :], float(NKEYS), SEL[:, 1, h4, :],
                        ALU.mult, ALU.add).then_inc(sem("eidx"), 1)
                gw = GW[:, i, :].rearrange("p (h k) -> p h k", h=PH)
                tt(gw, BEST[:, :, :], BEST[:, :, 0:1].to_broadcast([P, PH, TOPK]), ALU.subtract).then_inc(sem("best_ready"), 1)

            def pick_softmax(i):
                gw = GW[:, i, :].rearrange("p (h k) -> p h k", h=PH)
                dve.wait_ge(sem("best_exp"), i + 1)
                nc.vector.tensor_reduce(SUM8[:, :], gw, AX.X, ALU.add)
                dve.drain()
                nc.vector.reciprocal(SUM8[:, :], SUM8[:, :])
                dve.drain()
                tt(gw, gw, bcast(SUM8[:, :], 2, [P, PH, TOPK]), ALU.mult)

            def pre_norm(i, loads):
                rsqrt_of_mean([(i, i + 1, D)])
                dve.wait_ge(sem("nw_in0"), 16 * loads)
                stt(HN2[:, i, :], X[:, i, :], RS[:, i:i + 1], NW[:, 0, :], ALU.mult, ALU.mult).then_inc(sem("hn2_ready"), 1)

            def post_norm(i, loads):
                rsqrt_of_mean([(i, i + 1, D)])
                dve.wait_ge(sem("nw_in1"), 16 * loads)
                stt(MO[:, i, :], MO[:, i, :], RS[:, i:i + 1], NW[:, 1, :], ALU.mult, ALU.mult)
                dve.drain()
                tt(X[:, i, :], X[:, i, :], MO[:, i, :], ALU.add).then_inc(sem("x_ready"), 1)
                dve.drain()

            for _ in search(0):
                pass
            second = search(1)
            for i in range(2):
                pick_softmax(i)
                for m in range(PICKS):
                    g = 2 * i * PICKS + m
                    dve.wait_ge(sem(f"row{g % NG}"), 16 * (g // NG + 1))
                    dve.drain()
                    ttr(out=PROD, in0=GROWS[g % NG], in1=H2[:, i, :], scale=1.0, scalar=0.0, op0=ALU.mult, op1=ALU.add,
                        accum_out=DOT[:, i, m:m + 1]).then_inc(sem("u_used"), 1)
                    if i == 0 and m % 16 == 15:
                        next(second, None)
                dve.wait_ge(sem("gelu_done"), i + 1)
                tt(GW[:, i, :], GW[:, i, :], DOT[:, i, :], ALU.mult)
                dve.drain().then_inc(sem("gw_ready"), 1)
                for m in range(3, PICKS, 4):
                    g = (2 * i + 1) * PICKS + m
                    dve.wait_ge(sem(f"row{g % NG}"), 16 * (g // NG + 1))
                    if m == 3:
                        ins = ts(ACC, GROWS[g % NG], GW[:, i, m:m + 1], None, ALU.mult)
                    else:
                        dve.drain()
                        ins = stt(ACC, GROWS[g % NG], GW[:, i, m:m + 1], ACC, ALU.mult, ALU.add)
                    ins.then_inc(sem("v_added"), 1)
                    if i == 0:
                        next(second, None)
                if i == 0:
                    for _ in second:
                        pass
                if i == 1:
                    pre_norm(0, 1)
                dve.drain()
                for h in range(2):
                    e = slice(h * 512, (h + 1) * 512)
                    o = full()
                    tt(ACC[:, e], o, ACC[:, e], ALU.add).then_inc(d_free, 1)
                    dve.drain()
                    tt(ACC[:, e], ACC[:, e], MODB[:, 3, e], ALU.mult)
                    dve.drain()
                    ins = tt(X[:, i, e], X[:, i, e], ACC[:, e], ALU.add)
                ins.then_inc(sem("x_ready"), 1)
            for L in range(DEPTH):
                m = at["L"][L]

                if L == 0:
                    dve.drain()
                    pre_norm(1, 1)
                for wh in range(2):
                    for i in range(2):
                        o = full().rearrange("p (h f e) -> p h f e", h=AH, f=2)
                        r = RTMP[:, i, :].rearrange("p (h f e) -> p h f e", h=AH, f=2)
                        q = QKR[:, wh, i, :]
                        sin = rope2[:, 1, i, :].rearrange("p (f e) -> p f e", f=2)
                        for f in range(2):
                            tt(r[:, :, f, :], o[:, :, 1 - f, :], bcast(sin[:, f, :], 1, [P, AH, AD // 2]), ALU.mult)
                        tt(q.rearrange("p (h e) -> p h e", h=AH), o.rearrange("p h f e -> p h (f e)"), bcast(rope2[:, 0, i, :], 1, [P, AH, AD]), ALU.mult).then_inc(d_free, 1)
                        dve.drain()
                        ins = tt(q, q, RTMP[:, i, :], ALU.add)
                ins.then_inc(sem("rot2"), 1)
                step, early = iter(range(ATT_STEPS)), iter(range(AH))

                def probabilities():
                    h = next(early, None)
                    if h is not None:
                        h += 1
                        n = 2 * h - 2
                        dve.wait_ge(sem("at_exp"), AH * L + h)
                        nc.vector.reciprocal(RC[:, n:n + 2], SM[:, n:n + 2])
                        dve.drain()
                        for i in range(2):
                            e = ETMP[:, (h - 1) % 2, i:1 + 2 * i, :]
                            ins = ts(e, e, RC[:, n + i:n + i + 1], None, ALU.mult)
                        ins.then_inc(sem("at_p"), 1)

                def attend():
                    h = next(step)
                    if h < AH:
                        n = 2 * h
                        o = full()
                        for i in range(2):
                            seg = slice(i * P, (1 + 2 * i) * P)
                            ins = ttr(out=ETMP[:, h % 2, i:1 + 2 * i, :].rearrange("p s q -> p (s q)"), in0=o[:, seg], in1=v(DILM + i * P, (i + 1) * P),
                                      scale=float(AD) ** -0.5, scalar=-3e38, op0=ALU.add, op1=ALU.max, accum_out=MN[:, n + i:n + i + 1])
                        ins.then_inc(d_free, 1)
                        dve.drain()
                        ts(MX[:, n:n + 2], MN[:, n:n + 2], -1.0, None, ALU.mult).then_inc(sem("at_max"), 1)
                    if h >= 2:
                        h -= 2
                        p0 = (h % 2) * AD
                        o = full()
                        copy(MIX2[p0:p0 + AD, h // 2, :], o[p0:p0 + AD, 0:SEQ]).then_inc(d_free, 1)

                attend()
                for g in range(6):
                    probabilities()
                    o = full()
                    dve.wait_ge(sem("cv_tap"), 6 * L + g + 1)
                    for s in range(1, 4):
                        for f in range(2):
                            y = CV[:, 2 * g + f, s:SEQ]
                            ins = stt(y, o[:, f * SEQ:(f + 1) * SEQ - s], CW2[:, L, 2 * g + f, 3 - s:4 - s], y, ALU.mult, ALU.add)
                        if s < 3:
                            dve.drain()
                    ins.then_inc(d_free, 1)
                    attend()
                for _ in range(3):
                    probabilities()
                    attend()
                share = iter([(b, 1) for b in range(2)])

                def projected():
                    b, i = next(share)
                    o = full()
                    copy(MO1[:, i, b * 512:(b + 1) * 512], o).then_inc(d_free, 1)

                dve.wait_ge(a_free, m["ba"])
                tt(ST1[:, :, :], ST1[:, :, :], bcast(AB2[:, L, 4:8], 1, [P, 2, 4]), ALU.add).then_inc(sem("sp_in"), 1)
                c["norm"] += 1
                dve.wait_ge(sem("ss_ready"), c["norm"])
                ts(MS[:, 0:16], SS[:, 0:16], EPS, None, ALU.add).then_inc(sem("ms_ready"), 1)
                for i in range(2):
                    for h in range(DH):
                        e = TQ[:, 2, i, h * P:(h + 1) * P]
                        ins = ts(e, e, BT[:, i, h:h + 1], None, ALU.mult)
                ins.then_inc(sem("vb_ready"), 1)
                projected()
                projected()
                dve.wait_ge(sem("rs_ready"), c["norm"])
                for wh in range(2):
                    for i in range(2):
                        for h in range(DH):
                            e = TQ[:, wh, i, h * P:(h + 1) * P]
                            n = wh * 8 + i * 4 + h
                            ins = ts(e, e, RS[:, n:n + 1], float(P) ** -0.5 if wh == 0 else 1.0, ALU.mult, ALU.mult)
                    ins.then_inc(sem("dn_normed"), 1)
                for T in (TI, TU):
                    ins = copy(T[:, :, :], bcast(ident, 1, [P, 8, P]))
                ins.then_inc(sem("t_init"), 1)
                dve.wait_ge(sem("sp_exp"), L + 1)
                ts(ST2[:, :, :], ST2[:, :, :], 1.0, None, ALU.add).then_inc(sem("sp_plus1"), 1)
                ts(ST1[:, :, :], ST1[:, :, :], 0.0, None, ALU.max)
                dve.wait_ge(sem("sp_ln"), L + 1)
                dve.drain()
                tt(ST1[:, :, :], ST1[:, :, :], ST2[:, :, :], ALU.add)
                dve.drain()
                stt(GT[:, :, :], ST1[:, :, :], -1.0, bcast(AE[:, :], 1, [P, 2, 4]), ALU.mult, ALU.mult).then_inc(sem("g_ready"), 1)
                o = full()
                copy(GC[:, :, :], o[:, 0:8].rearrange("p (i h) -> p i h", i=2)).then_inc(d_free, 1)
                dve.drain()
                for g in range(2):
                    o = full().rearrange("p (h i j) -> p h i j", h=2, i=2)
                    for hh in range(2):
                        h = 2 * g + hh
                        stt(DEC[:, h, 0, :], o[:, hh, 0, :], GC[:, 0, h:h + 1], v(DECM, P), ALU.subtract, ALU.add)
                        ts(DEC[:, h, 1, :], o[:, hh, 0, :], GC[:, 1, h:h + 1], None, ALU.subtract)
                        ins = stt(DEC[:, h, 2, :], o[:, hh, 1, :], GC[:, 1, h:h + 1], v(DECM, P), ALU.subtract, ALU.add)
                    ins.then_inc(d_free, 1)
                dve.drain().then_inc(sem("dec_in"), 1)
                dve.wait_ge(sem("dec_exp"), L + 1)
                for seg in range(3):
                    o = full()
                    tt(QKD[:, :, seg, :], o.rearrange("p (h j) -> p h j", h=4), DEC[:, :, seg, :], ALU.mult).then_inc(d_free, 1)
                for seg in range(3):
                    o = full()
                    for h in range(DH):
                        ins = stt(AA[:, h, seg, :], o[:, h * P:(h + 1) * P], BT[:, (seg + 1) // 2, h:h + 1], DEC[:, h, seg, :], ALU.mult, ALU.mult)
                    ins.then_inc(d_free, 1)
                dve.drain().then_inc(sem("aa_ready"), 1)
                for lv in range(7):
                    for half in range(2):
                        s = slice(4 * half, 4 * half + 4)
                        for T in ((TI, TU) if lv < 6 else (TU,)):
                            o = full()
                            tt(T[:, s, :], T[:, s, :], o.rearrange("p (h j) -> p h j", h=4), ALU.subtract).then_inc(d_free, 1)
                    if lv < 6:
                        dve.drain()
                o = full()
                copy(UU[:, 0, :], o).then_inc(d_free, 1)
                o = full()
                tt(TQ[:, 2, 1, :], TQ[:, 2, 1, :], o, ALU.subtract).then_inc(d_free, 1)
                o = full()
                copy(UU[:, 1, :], o).then_inc(d_free, 1)
                dve.wait_ge(sem("dnw_in"), 16)
                rsqrt_of_mean([(0, 8, P)])
                for i in range(2):
                    for h in range(DH):
                        e = slice(h * P, (h + 1) * P)
                        stt(TQ[:, 0, i, e], TQ[:, 1, i, e], RS[:, 4 * i + h:4 * i + h + 1], DNW[:, L, :], ALU.mult, ALU.mult)
                dve.drain()
                tt(TQ[:, 0, :, :], TQ[:, 0, :, :], Z2[:, :, :], ALU.mult).then_inc(sem("do_gated"), 1)
                for i in range(2):
                    for b in range(2):
                        o = full()
                        e = slice(b * 512, (b + 1) * 512)
                        if i == 0:
                            copy(MO[:, i, e], o).then_inc(d_free, 1)
                        else:
                            tt(MO[:, i, e], o, MO1[:, i, e], ALU.add).then_inc(d_free, 1)
                    post_norm(i, 2 * L + 1)
                    pre_norm(i, 2 * L + 2)
                for n in range(2 * FBLK + 1):
                    N = 2 * FBLK * L + n
                    if n < 2 * FBLK:
                        o = full()
                        dve.wait_ge(sem("ffn_tap"), N + 1)
                        for s in range(1, 3):
                            for wh in range(2):
                                f = wh * DFF // P + n
                                y = YG[:, n % 4, wh, s:SEQ]
                                ins = stt(y, o[:, wh * SEQ:(wh + 1) * SEQ - s], FW2[:, L, f, 2 - s:3 - s], y, ALU.mult, ALU.add)
                            if s == 1:
                                dve.drain()
                        ins.then_inc(d_free, 1)
                    if n >= 1:
                        dve.wait_ge(sem("ffn_gelu"), N)
                        q = n - 1
                        tt(GU[:, q // 2 % 2, q % 2, :], YG[:, q % 4, 0, :], YG[:, q % 4, 1, :], ALU.mult).then_inc(sem("gu_ready"), 1)
                for i in range(2):
                    post_norm(i, 2 * L + 2)
                    if L + 1 < DEPTH:
                        pre_norm(i, 2 * L + 3)



def kernel(**inputs):
    import concourse.bacc as _bacc
    from concourse.bass_utils import run_bass_kernel_spmd as _run

    def col(x):
        x = np.asarray(x)
        x = x.reshape(x.shape[:-1] + (x.shape[-1] // P, P))
        return np.ascontiguousarray(np.moveaxis(x, -1, 0))

    i = {k: np.ascontiguousarray(x) for k, x in inputs.items()}
    arrays = {k: i[k] for k in ("x", "ctx", "w_ada", "b_ada", "g_norm1", "g_norm2", "w_in", "g_cq", "g_ckv", "g_qn", "g_kn",
                                "w_uq", "w_ukv", "w_out", "w_pq", "g_mlstm", "w_in_2", "w_out_2", "ffn_w_in_2", "ffn_w_out_2")}
    for k in ("pre_mix", "post_mix", "pre_ffn", "post_ffn"):
        arrays[f"norm_{k}_2"] = i[f"norm_{k}_2"]
    arrays["expert_u"] = i["expert_u"][0]
    arrays["expert_v"] = i["expert_v"][0]
    arrays["cc"] = np.ascontiguousarray(np.stack([col(i["c"][0]), col(i["c_ctx"])], -1).reshape(P, 2 * KT))
    arrays["sub_keys_T"] = np.ascontiguousarray(i["sub_keys"][0].transpose(3, 0, 1, 2).reshape(P, 2 * PH * NKEYS))
    arrays["conv1"] = np.ascontiguousarray(col(i["conv_qk"][0]).transpose(0, 2, 1).reshape(P, 12))
    arrays["gate_bias"] = np.concatenate([i["b_igate"].reshape(1, 8), i["b_fgate"].reshape(1, 8)], 1)
    arrays["conv2"] = np.ascontiguousarray(col(i["dn_conv_w_2"]).transpose(0, 1, 3, 2).reshape(P, DEPTH * 48))
    arrays["ffn_conv"] = np.ascontiguousarray(col(i["ffn_conv_w_2"]).transpose(0, 1, 3, 2).reshape(P, DEPTH * 132))
    arrays["ffn_bias"] = np.ascontiguousarray(col(i["ffn_conv_b_2"]).reshape(P, DEPTH * 44))
    arrays["decay"] = np.stack([i["dn_a_log_2"], i["dn_dt_bias_2"]], 1).reshape(1, DEPTH * 8)
    arrays["dn_norm"] = i["dn_norm_w_2"].reshape(1, DEPTH * P)
    arrays["consts"] = constants()
    arrays["mmask"] = mlstm_masks()

    nc = _bacc.Bacc("TRN2", target_bir_lowering=False, num_devices=1)
    aps = {k: nc.dram_tensor(f"in_{k}", x.shape, mybir.dt.from_np(x.dtype), kind="ExternalInput").ap() for k, x in arrays.items()}
    out = nc.dram_tensor("out_0", (1, SEQ, D), F32, kind="ExternalOutput").ap()
    program(nc, aps, out)
    r = _run(nc, [{f"in_{k}": x for k, x in arrays.items()}], core_ids=[0])
    return r.results[0]["out_0"]
```
